# Optimizing a Trainium2 kernel written in Bass

```python
import math
import jax, jax.numpy as jnp
from jax import lax
import numpy as np

D_MODEL = 1024
BATCH = 1
SEQ = 256
DEPTH = 1

D_FF = 2816
RMS_EPS = 1e-6
N_DIR = 2
D_HYENA = 512
HYENA_ORDER = 2
HYENA_BANDS = 16
HYENA_EMB = 2 * HYENA_BANDS + 1
HYENA_FFN = 64
HYENA_MIN_DECAY = abs(math.log(1e-2)) / 1.5
HYENA_MAX_DECAY = abs(math.log(1e-2)) / 0.3
FILTER_EPS = 1e-6
D_RWKV = 512
RWKV_HEAD = 64
RWKV_HEADS = D_RWKV // RWKV_HEAD
DECAY_LORA = 64
AAA_LORA = 64
GATE_LORA = 160
GN_EPS = 64e-5
N_HY_IN = 3 * D_HYENA
N_RW_IN = 3 * D_RWKV + N_DIR * (DECAY_LORA + AAA_LORA) + GATE_LORA
N_GATE = 2 * D_MODEL
N_IN = N_HY_IN + N_RW_IN + N_GATE


def _rmsnorm(x, g):
    xf = x.astype(jnp.float32)
    y = xf * lax.rsqrt(jnp.mean(xf * xf, axis=-1, keepdims=True) + RMS_EPS)
    return (y * g.astype(jnp.float32)).astype(x.dtype)

def _swiglu(h, w_gu, w_down):
    gate, up = jnp.split(h @ w_gu, 2, axis=-1)
    return (jax.nn.silu(gate) * up) @ w_down

def _centred_conv3(u, w, b):
    up = jnp.pad(u, ((0, 0), (1, 1), (0, 0)))
    return w[0] * up[:, :-2] + w[1] * up[:, 1:-1] + w[2] * up[:, 2:] + b

def _centred_token_shift(u, mu):
    prev = jnp.pad(u, ((0, 0), (1, 0), (0, 0)))[:, :-1]
    nxt = jnp.pad(u, ((0, 0), (0, 1), (0, 0)))[:, 1:]
    return u + mu[0] * (prev - u) + mu[1] * (nxt - u)

def _hyena_filters(L, w1, b1, w2, b2, w3, b3, freq, decay):
    f32 = jnp.float32
    pos = jnp.arange(L, dtype=f32)
    t = (pos / max(L - 1, 1))[:, None]
    ang = (2.0 * math.pi / L) * pos[:, None]
    bands = jnp.linspace(1e-4, HYENA_BANDS - 1, HYENA_BANDS, dtype=f32)[None, :]
    feats = jnp.concatenate([t, jnp.cos(bands * ang), -jnp.sin(bands * ang)], axis=-1)
    fr = freq.astype(f32)
    h = jnp.sin(fr * (feats @ w1.astype(f32) + b1.astype(f32)))
    h = jnp.sin(fr * (h @ w2.astype(f32) + b2.astype(f32)))
    h = h @ w3.astype(f32) + b3.astype(f32)
    h = h.reshape(L, N_DIR, HYENA_ORDER, D_HYENA)
    h = h * jnp.exp(-t[:, :, None, None] * jnp.abs(decay.astype(f32))[None])
    fwd, bwd = h[:, 0], h[:, 1]
    zero = jnp.zeros((1, HYENA_ORDER, D_HYENA), f32)
    k = jnp.concatenate([fwd, zero, jnp.flip(bwd[1:], axis=0)], axis=0)
    k = k * lax.rsqrt(jnp.sum(k * k, axis=0, keepdims=True) + FILTER_EPS)
    return k

def _long_conv(z, k_f, d, L):
    zf = jnp.fft.rfft(z, n=2 * L, axis=1)
    y = jnp.fft.irfft(zf * k_f[None], n=2 * L, axis=1)[:, :L]
    return y + d * z

def _hyena_branch(u, conv_w, conv_b, w1, b1, w2, b2, w3, b3, freq, decay, bias_d, w_o):
    out_dtype = u.dtype
    L = u.shape[1]
    uc = _centred_conv3(u, conv_w, conv_b).astype(jnp.float32)
    x1, x2, v = jnp.split(uc, 3, axis=-1)
    k = _hyena_filters(L, w1, b1, w2, b2, w3, b3, freq, decay)
    k_f = jnp.fft.rfft(k, axis=0)
    d = bias_d.astype(jnp.float32)
    z = x1 * _long_conv(v, k_f[:, 0], d[0], L)
    z = x2 * _long_conv(z, k_f[:, 1], d[1], L)
    return z.astype(out_dtype) @ w_o

def _time_major_pair(fwd, bwd):
    return jnp.moveaxis(jnp.stack([fwd, jnp.flip(bwd, axis=1)], axis=0), 2, 0)

def _rwkv7_step(S, inp):
    r, w, k, v, kk, a = inp
    sa = jnp.einsum('dbhij,dbhj->dbhi', S, -kk)
    S = S * w[..., None, :] + sa[..., None] * (kk * a)[..., None, :] + v[..., None] * k[..., None, :]
    y = jnp.einsum('dbhij,dbhj->dbhi', S, r)
    return S, y

def _rwkv7_branch(u, mu, w0, w2, a0, a2, g2, k_k, k_a, r_k, ln_w, ln_b, w_o):
    out_dtype = u.dtype
    B, L, _ = u.shape
    H, N = RWKV_HEADS, RWKV_HEAD
    f32 = jnp.float32
    u = _centred_token_shift(u, mu).astype(f32)
    splits = [D_RWKV, 2 * D_RWKV, 3 * D_RWKV, 3 * D_RWKV + N_DIR * DECAY_LORA,
              3 * D_RWKV + N_DIR * (DECAY_LORA + AAA_LORA)]
    r, k, v, wd, ad, gd = jnp.split(u, splits, axis=-1)
    wd = wd.reshape(B, L, N_DIR, DECAY_LORA)
    ad = ad.reshape(B, L, N_DIR, AAA_LORA)
    w = -jax.nn.softplus(-(w0 + jnp.einsum('bldr,drc->bldc', jnp.tanh(wd), w2))) - 0.5
    decay = jnp.exp(-jnp.exp(w))
    a = jax.nn.sigmoid(a0 + jnp.einsum('bldr,drc->bldc', ad, a2))
    g = jax.nn.sigmoid(gd) @ g2
    kk = (k * k_k).reshape(B, L, H, N)
    kk = kk / jnp.maximum(jnp.sqrt(jnp.sum(kk * kk, axis=-1, keepdims=True)), 1e-12)
    k_dir = k[:, :, None, :] * (1.0 + (a - 1.0) * k_a)

    def heads(t):
        return t.reshape(t.shape[:-1] + (H, N))

    r_h, v_h = heads(r), heads(v)
    decay_h, a_h, k_h = heads(decay), heads(a), heads(k_dir)
    seq = (_time_major_pair(r_h, r_h),
           _time_major_pair(decay_h[:, :, 0], decay_h[:, :, 1]),
           _time_major_pair(k_h[:, :, 0], k_h[:, :, 1]),
           _time_major_pair(v_h, v_h),
           _time_major_pair(kk, kk),
           _time_major_pair(a_h[:, :, 0], a_h[:, :, 1]))
    S0 = jnp.zeros((N_DIR, B, H, N, N), f32)
    _, ys = lax.scan(_rwkv7_step, S0, seq)
    y = jnp.moveaxis(ys[:, 0] + jnp.flip(ys[:, 1], axis=0), 0, 1)
    mean = jnp.mean(y, axis=-1, keepdims=True)
    var = jnp.mean(jnp.square(y - mean), axis=-1, keepdims=True)
    y = ((y - mean) * lax.rsqrt(var + GN_EPS)).reshape(B, L, D_RWKV) * ln_w + ln_b
    bonus = jnp.sum(r_h[:, :, None] * k_h * r_k, axis=-1, keepdims=True)
    y = y + (jnp.sum(bonus, axis=2) * v_h).reshape(B, L, D_RWKV)
    y = y * g
    return y.astype(out_dtype) @ w_o

def first_inputs(seed: int = 0) -> dict:
    key = jax.random.key(seed)
    ks = jax.random.split(key, 35)
    f32 = jnp.float32

    def nrm(i, shape, scale):
        return scale * jax.random.normal(ks[i], shape, f32)

    hy_decay_base = jnp.linspace(HYENA_MIN_DECAY, HYENA_MAX_DECAY, D_HYENA, dtype=f32)
    rw_w0_base = jnp.linspace(-6.0, -1.0, D_RWKV, dtype=f32)
    return {
        "x": nrm(0, (BATCH, SEQ, D_MODEL), 1.0),
        "ffn1_norm": 1.0 + nrm(1, (D_MODEL,), 0.05),
        "ffn1_w_gu": nrm(2, (D_MODEL, 2 * D_FF), D_MODEL ** -0.5),
        "ffn1_w_down": nrm(3, (D_FF, D_MODEL), D_FF ** -0.5),
        "mix_norm": 1.0 + nrm(4, (D_MODEL,), 0.05),
        "w_in": nrm(5, (D_MODEL, N_IN), D_MODEL ** -0.5),
        "hy_conv_w": nrm(6, (3, N_HY_IN), 3 ** -0.5),
        "hy_conv_b": nrm(7, (N_HY_IN,), 0.02),
        "hy_ffn_w1": nrm(8, (HYENA_EMB, HYENA_FFN), HYENA_EMB ** -0.5),
        "hy_ffn_b1": nrm(9, (HYENA_FFN,), 0.1),
        "hy_ffn_w2": nrm(10, (HYENA_FFN, HYENA_FFN), HYENA_FFN ** -0.5),
        "hy_ffn_b2": nrm(11, (HYENA_FFN,), 0.1),
        "hy_ffn_w3": nrm(12, (HYENA_FFN, N_DIR * HYENA_ORDER * D_HYENA), HYENA_FFN ** -0.5),
        "hy_ffn_b3": nrm(13, (N_DIR * HYENA_ORDER * D_HYENA,), 0.1),
        "hy_sin_freq": 1.0 + nrm(14, (HYENA_FFN,), 0.1),
        "hy_decay": hy_decay_base + nrm(15, (N_DIR, HYENA_ORDER, D_HYENA), 0.1),
        "hy_bias_d": nrm(16, (HYENA_ORDER, D_HYENA), 0.5),
        "hy_out": nrm(17, (D_HYENA, D_MODEL), D_HYENA ** -0.5),
        "rw_mu": jax.random.uniform(ks[18], (2, N_RW_IN), f32, 0.0, 0.5),
        "rw_w0": rw_w0_base + nrm(19, (N_DIR, D_RWKV), 0.1),
        "rw_w2": nrm(20, (N_DIR, DECAY_LORA, D_RWKV), 0.1),
        "rw_a0": nrm(21, (N_DIR, D_RWKV), 0.3),
        "rw_a2": nrm(22, (N_DIR, AAA_LORA, D_RWKV), 0.1),
        "rw_g2": nrm(23, (GATE_LORA, D_RWKV), GATE_LORA ** -0.5),
        "rw_k_k": 0.85 + nrm(24, (D_RWKV,), 0.05),
        "rw_k_a": 1.0 + nrm(25, (D_RWKV,), 0.05),
        "rw_r_k": nrm(26, (RWKV_HEADS, RWKV_HEAD), 0.1),
        "rw_ln_w": 1.0 + nrm(27, (D_RWKV,), 0.05),
        "rw_ln_b": nrm(28, (D_RWKV,), 0.02),
        "rw_out": nrm(29, (D_RWKV, D_MODEL), D_RWKV ** -0.5),
        "w_out": nrm(30, (D_MODEL, D_MODEL), D_MODEL ** -0.5),
        "ffn2_norm": 1.0 + nrm(31, (D_MODEL,), 0.05),
        "ffn2_w_gu": nrm(32, (D_MODEL, 2 * D_FF), D_MODEL ** -0.5),
        "ffn2_w_down": nrm(33, (D_FF, D_MODEL), D_FF ** -0.5),
        "final_norm": 1.0 + nrm(34, (D_MODEL,), 0.05),
    }

def first_block(x, ffn1_norm, ffn1_w_gu, ffn1_w_down, mix_norm, w_in, hy_conv_w, hy_conv_b,
              hy_ffn_w1, hy_ffn_b1, hy_ffn_w2, hy_ffn_b2, hy_ffn_w3, hy_ffn_b3, hy_sin_freq,
              hy_decay, hy_bias_d, hy_out, rw_mu, rw_w0, rw_w2, rw_a0, rw_a2, rw_g2, rw_k_k,
              rw_k_a, rw_r_k, rw_ln_w, rw_ln_b, rw_out, w_out, ffn2_norm, ffn2_w_gu,
              ffn2_w_down, final_norm):
    split_at = [N_HY_IN, N_HY_IN + N_RW_IN, N_HY_IN + N_RW_IN + D_MODEL]
    for _ in range(DEPTH):
        x = x + 0.5 * _swiglu(_rmsnorm(x, ffn1_norm), ffn1_w_gu, ffn1_w_down)
        h = _rmsnorm(x, mix_norm)
        u_hy, u_rw, g_hy, g_rw = jnp.split(h @ w_in, split_at, axis=-1)
        y_hy = _hyena_branch(u_hy, hy_conv_w, hy_conv_b, hy_ffn_w1, hy_ffn_b1, hy_ffn_w2,
                             hy_ffn_b2, hy_ffn_w3, hy_ffn_b3, hy_sin_freq, hy_decay,
                             hy_bias_d, hy_out)
        y_rw = _rwkv7_branch(u_rw, rw_mu, rw_w0, rw_w2, rw_a0, rw_a2, rw_g2, rw_k_k, rw_k_a,
                             rw_r_k, rw_ln_w, rw_ln_b, rw_out)
        merged = jax.nn.sigmoid(g_hy) * y_hy + jax.nn.sigmoid(g_rw) * y_rw
        x = x + merged @ w_out
        x = x + 0.5 * _swiglu(_rmsnorm(x, ffn2_norm), ffn2_w_gu, ffn2_w_down)
    return _rmsnorm(x, final_norm)


MEM_LEN = 256
SB_HEADS = 16
SB_HEAD_DIM = 64
SB_WIDTH = SB_HEADS * SB_HEAD_DIM
SB_BLOCK = 128
SSM_EXPAND = 2
SSM_INNER = SSM_EXPAND * D_MODEL
SSM_HEAD_DIM = 64
SSM_HEADS = SSM_INNER // SSM_HEAD_DIM
SSM_GROUPS = 4
SSM_STATE = 128
SSM_CONV = 4
SSM_CHUNK = 128
SSM_CONV_DIM = SSM_INNER + 2 * SSM_GROUPS * SSM_STATE
XA_HEADS = 4
XA_HEAD_DIM = D_MODEL // XA_HEADS
FFN_HIDDEN = ((8 * D_MODEL + 767) // 768) * 256
IN_SIZES = (SB_WIDTH, SB_WIDTH, SB_WIDTH, SSM_INNER, SSM_CONV_DIM, SSM_HEADS, D_MODEL, D_MODEL)
IN_WIDTH = 3 * SB_WIDTH + SSM_INNER + SSM_CONV_DIM + SSM_HEADS + 2 * D_MODEL


def _split(a, sizes):
    idx = tuple(int(i) for i in np.cumsum(sizes)[:-1])
    return jnp.split(a, idx, axis=-1)

def rms_norm(x, g):
    xf = x.astype(jnp.float32)
    y = xf * lax.rsqrt(jnp.mean(xf * xf, axis=-1, keepdims=True) + RMS_EPS)
    return (y * g.astype(jnp.float32)).astype(x.dtype)

def stick_breaking_attention(q, k, v):
    bsz, seq = q.shape[0], q.shape[1]
    qf = jnp.swapaxes(q.astype(jnp.float32), 1, 2) * (SB_HEAD_DIM ** -0.5)
    kf = jnp.swapaxes(k.astype(jnp.float32), 1, 2)
    vf = jnp.swapaxes(v.astype(jnp.float32), 1, 2)
    outs = []
    for blk in range(seq // SB_BLOCK):
        t0 = blk * SB_BLOCK
        t1 = t0 + SB_BLOCK
        z = jnp.einsum('bhtd,bhsd->bhts', qf[:, :, t0:t1], kf[:, :, :t1])
        causal = jnp.arange(t1)[None, :] < (t0 + jnp.arange(SB_BLOCK))[:, None]
        log_1mb = jnp.where(causal, jax.nn.log_sigmoid(-z), 0.0)
        tail = lax.cumsum(log_1mb, axis=3, reverse=True)
        w = jnp.where(causal, jnp.exp(z + tail), 0.0)
        outs.append(jnp.einsum('bhts,bhsd->bhtd', w, vf[:, :, :t1]))
    o = jnp.concatenate(outs, axis=2)
    return jnp.swapaxes(o, 1, 2).reshape(bsz, seq, SB_WIDTH)

def ssd_chunked(x, dt, a, bm, cm):
    b, l, h, p = x.shape
    g, n = bm.shape[2], bm.shape[3]
    e = h // g
    c = l // SSM_CHUNK
    xc = (x * dt[..., None]).reshape(b, c, SSM_CHUNK, g, e, p)
    a_dt = (dt * a).reshape(b, c, SSM_CHUNK, g, e).transpose(0, 1, 3, 4, 2)
    a_cs = jnp.cumsum(a_dt, axis=-1)
    bc = bm.reshape(b, c, SSM_CHUNK, g, n)
    cc = cm.reshape(b, c, SSM_CHUNK, g, n)
    tril = jnp.tril(jnp.ones((SSM_CHUNK, SSM_CHUNK), dtype=bool))
    decay = jnp.exp(jnp.where(tril, a_cs[..., :, None] - a_cs[..., None, :], -jnp.inf))
    cb = jnp.einsum('bclgn,bcsgn->bcgls', cc, bc)
    y_diag = jnp.einsum('bcgls,bcgels,bcsgep->bclgep', cb, decay, xc)
    decay_to_end = jnp.exp(a_cs[..., -1:] - a_cs)
    states = jnp.einsum('bclgn,bcgel,bclgep->bcgepn', bc, decay_to_end, xc)
    chunk_decay = jnp.exp(a_cs[..., -1])

    def step(prev, inp):
        st, dec = inp
        return prev * dec[..., None, None] + st, prev

    init = jnp.zeros((b, g, e, p, n), dtype=states.dtype)
    _, prev_states = lax.scan(step, init, (jnp.moveaxis(states, 1, 0), jnp.moveaxis(chunk_decay, 1, 0)))
    prev_states = jnp.moveaxis(prev_states, 0, 1)
    y_off = jnp.einsum('bclgn,bcgepn,bcgel->bclgep', cc, prev_states, jnp.exp(a_cs))
    return (y_diag + y_off).reshape(b, l, h, p)

def ssd_branch(z, xbc, dt_raw, conv_w, conv_b, dt_bias, a_log, d_skip, g_norm):
    bsz, seq = xbc.shape[0], xbc.shape[1]
    xbc = lax.conv_general_dilated(
        xbc, conv_w[:, None, :].astype(xbc.dtype), window_strides=(1,),
        padding=[(SSM_CONV - 1, 0)], dimension_numbers=('NWC', 'WIO', 'NWC'),
        feature_group_count=SSM_CONV_DIM)
    xbc = jax.nn.silu(xbc.astype(jnp.float32) + conv_b.astype(jnp.float32))
    xs, bm, cm = _split(xbc, (SSM_INNER, SSM_GROUPS * SSM_STATE, SSM_GROUPS * SSM_STATE))
    dt = jax.nn.softplus(dt_raw.astype(jnp.float32) + dt_bias.astype(jnp.float32))
    a = -jnp.exp(a_log.astype(jnp.float32))
    xh = xs.reshape(bsz, seq, SSM_HEADS, SSM_HEAD_DIM)
    y = ssd_chunked(xh, dt, a,
                    bm.reshape(bsz, seq, SSM_GROUPS, SSM_STATE),
                    cm.reshape(bsz, seq, SSM_GROUPS, SSM_STATE))
    y = y + d_skip.astype(jnp.float32)[:, None] * xh
    y = y.reshape(bsz, seq, SSM_INNER) * jax.nn.silu(z.astype(jnp.float32))
    yg = y.reshape(bsz, seq, SSM_GROUPS, SSM_INNER // SSM_GROUPS)
    yg = yg * lax.rsqrt(jnp.mean(yg * yg, axis=-1, keepdims=True) + RMS_EPS)
    return yg.reshape(bsz, seq, SSM_INNER) * g_norm.astype(jnp.float32)

def memory_cross_attention(h, mem_n, w_xq, w_xkv, w_xo):
    bsz, seq = h.shape[0], h.shape[1]
    q = (h @ w_xq).reshape(bsz, seq, XA_HEADS, XA_HEAD_DIM)
    k, v = _split(mem_n @ w_xkv, (D_MODEL, D_MODEL))
    k = k.reshape(bsz, MEM_LEN, XA_HEADS, XA_HEAD_DIM)
    v = v.reshape(bsz, MEM_LEN, XA_HEADS, XA_HEAD_DIM)
    s = jnp.einsum('bshd,bmhd->bhsm', q.astype(jnp.float32), k.astype(jnp.float32)) * (XA_HEAD_DIM ** -0.5)
    p = jax.nn.softmax(s, axis=-1)
    o = jnp.einsum('bhsm,bmhd->bshd', p, v.astype(jnp.float32)).reshape(bsz, seq, D_MODEL)
    return o.astype(h.dtype) @ w_xo

def swiglu(h, w_gu, w_down):
    gate, up = _split(h @ w_gu, (FFN_HIDDEN, FFN_HIDDEN))
    return (jax.nn.silu(gate) * up) @ w_down

def second_inputs(seed: int = 0) -> dict:
    key = jax.random.key(seed)
    ks = jax.random.split(key, 32)
    f32 = jnp.float32

    def dense(k, shape, fan_in):
        return jax.random.normal(k, shape, f32) * (fan_in ** -0.5)

    def gain(k, shape):
        return 1.0 + 0.02 * jax.random.normal(k, shape, f32)

    dt0 = jnp.exp(jax.random.uniform(ks[5], (DEPTH, SSM_HEADS), f32,
                                     minval=math.log(1e-3), maxval=math.log(1e-1)))
    dt_bias = dt0 + jnp.log(-jnp.expm1(-dt0))
    a_log = jnp.log(jax.random.uniform(ks[6], (DEPTH, SSM_HEADS), f32, minval=1.0, maxval=16.0))
    return {
        "x": jax.random.normal(ks[0], (BATCH, SEQ, D_MODEL), f32),
        "mem": jax.random.normal(ks[1], (BATCH, MEM_LEN, D_MODEL), f32),
        "g_pre_mix": gain(ks[2], (DEPTH, D_MODEL)),
        "w_in": dense(ks[3], (DEPTH, D_MODEL, IN_WIDTH), D_MODEL),
        "conv_w": dense(ks[4], (DEPTH, SSM_CONV, SSM_CONV_DIM), SSM_CONV),
        "conv_b": 0.01 * jax.random.normal(ks[7], (DEPTH, SSM_CONV_DIM), f32),
        "dt_bias": dt_bias,
        "a_log": a_log,
        "d_skip": 1.0 + 0.1 * jax.random.normal(ks[8], (DEPTH, SSM_HEADS), f32),
        "g_ssm_norm": gain(ks[9], (DEPTH, SSM_INNER)),
        "w_br_att": dense(ks[10], (DEPTH, SB_WIDTH, D_MODEL), SB_WIDTH),
        "w_br_ssm": dense(ks[11], (DEPTH, SSM_INNER, D_MODEL), SSM_INNER),
        "w_mix_out": dense(ks[12], (DEPTH, D_MODEL, D_MODEL), D_MODEL),
        "g_post_mix": gain(ks[13], (DEPTH, D_MODEL)),
        "g_pre_xa": gain(ks[14], (DEPTH, D_MODEL)),
        "g_mem": gain(ks[15], (DEPTH, D_MODEL)),
        "w_xq": dense(ks[16], (DEPTH, D_MODEL, D_MODEL), D_MODEL),
        "w_xkv": dense(ks[17], (DEPTH, D_MODEL, 2 * D_MODEL), D_MODEL),
        "w_xo": dense(ks[18], (DEPTH, D_MODEL, D_MODEL), D_MODEL),
        "g_post_xa": gain(ks[19], (DEPTH, D_MODEL)),
        "g_pre_ffn": gain(ks[20], (DEPTH, D_MODEL)),
        "w_gu": dense(ks[21], (DEPTH, D_MODEL, 2 * FFN_HIDDEN), D_MODEL),
        "w_down": dense(ks[22], (DEPTH, FFN_HIDDEN, D_MODEL), FFN_HIDDEN),
        "g_post_ffn": gain(ks[23], (DEPTH, D_MODEL)),
    }

def second_block(x, mem, g_pre_mix, w_in, conv_w, conv_b, dt_bias, a_log, d_skip, g_ssm_norm,
              w_br_att, w_br_ssm, w_mix_out, g_post_mix, g_pre_xa, g_mem, w_xq, w_xkv, w_xo,
              g_post_xa, g_pre_ffn, w_gu, w_down, g_post_ffn):
    bsz, seq = x.shape[0], x.shape[1]
    for l in range(DEPTH):
        h = rms_norm(x, g_pre_mix[l])
        q, k, v, z, xbc, dt_raw, ga, gs = _split(h @ w_in[l], IN_SIZES)
        o_att = stick_breaking_attention(
            q.reshape(bsz, seq, SB_HEADS, SB_HEAD_DIM),
            k.reshape(bsz, seq, SB_HEADS, SB_HEAD_DIM),
            v.reshape(bsz, seq, SB_HEADS, SB_HEAD_DIM)).astype(x.dtype)
        o_ssm = ssd_branch(z, xbc, dt_raw, conv_w[l], conv_b[l], dt_bias[l], a_log[l],
                           d_skip[l], g_ssm_norm[l]).astype(x.dtype)
        merged = jax.nn.sigmoid(ga) * (o_att @ w_br_att[l]) + jax.nn.sigmoid(gs) * (o_ssm @ w_br_ssm[l])
        x = x + rms_norm(merged @ w_mix_out[l], g_post_mix[l])
        h = rms_norm(x, g_pre_xa[l])
        mem_n = rms_norm(mem, g_mem[l])
        x = x + rms_norm(memory_cross_attention(h, mem_n, w_xq[l], w_xkv[l], w_xo[l]), g_post_xa[l])
        h = rms_norm(x, g_pre_ffn[l])
        x = x + rms_norm(swiglu(h, w_gu[l], w_down[l]), g_post_ffn[l])
    return x


def setup_inputs(seed=0):
    out = dict(first_inputs(seed))
    for name, value in second_inputs(seed + 1).items():
        if name != "x":
            out[name + "_2"] = value
    return out


def reference(
    x, ffn1_norm, ffn1_w_gu, ffn1_w_down, mix_norm, w_in, hy_conv_w, hy_conv_b, hy_ffn_w1,
    hy_ffn_b1, hy_ffn_w2, hy_ffn_b2, hy_ffn_w3, hy_ffn_b3, hy_sin_freq, hy_decay, hy_bias_d,
    hy_out, rw_mu, rw_w0, rw_w2, rw_a0, rw_a2, rw_g2, rw_k_k, rw_k_a, rw_r_k, rw_ln_w, rw_ln_b,
    rw_out, w_out, ffn2_norm, ffn2_w_gu, ffn2_w_down, final_norm, mem_2, g_pre_mix_2, w_in_2,
    conv_w_2, conv_b_2, dt_bias_2, a_log_2, d_skip_2, g_ssm_norm_2, w_br_att_2, w_br_ssm_2,
    w_mix_out_2, g_post_mix_2, g_pre_xa_2, g_mem_2, w_xq_2, w_xkv_2, w_xo_2, g_post_xa_2,
    g_pre_ffn_2, w_gu_2, w_down_2, g_post_ffn_2,
):
    x = first_block(
        x, ffn1_norm, ffn1_w_gu, ffn1_w_down, mix_norm, w_in, hy_conv_w, hy_conv_b, hy_ffn_w1,
        hy_ffn_b1, hy_ffn_w2, hy_ffn_b2, hy_ffn_w3, hy_ffn_b3, hy_sin_freq, hy_decay, hy_bias_d,
        hy_out, rw_mu, rw_w0, rw_w2, rw_a0, rw_a2, rw_g2, rw_k_k, rw_k_a, rw_r_k, rw_ln_w,
        rw_ln_b, rw_out, w_out, ffn2_norm, ffn2_w_gu, ffn2_w_down, final_norm,
    )
    return second_block(
        x, mem_2, g_pre_mix_2, w_in_2, conv_w_2, conv_b_2, dt_bias_2, a_log_2, d_skip_2,
        g_ssm_norm_2, w_br_att_2, w_br_ssm_2, w_mix_out_2, g_post_mix_2, g_pre_xa_2, g_mem_2,
        w_xq_2, w_xkv_2, w_xo_2, g_post_xa_2, g_pre_ffn_2, w_gu_2, w_down_2, g_post_ffn_2,
    )


_drawn_inputs = setup_inputs


def setup_inputs(seed=0):
    import zlib

    import numpy as np

    out = dict(_drawn_inputs(seed))
    spreads = {}
    factors = {'rw_w2': 2.896,
     'rw_k_k': 4.417,
     'rw_k_a': 2.758,
     'rw_ln_w': 3.828,
     'rw_ln_b': 8.0,
     'conv_b_2': 6.218,
     'g_ssm_norm_2': 4.191,
     'g_post_mix_2': 3.531,
     'g_pre_xa_2': 4.541,
     'g_mem_2': 3.031,
     'g_post_xa_2': 11.116,
     'g_pre_ffn_2': 10.798,
     'g_post_ffn_2': 22.275}
    for name, (base, spread) in spreads.items():
        noise = np.random.default_rng([zlib.crc32(name.encode()), seed]).standard_normal(out[name].shape)
        drawn = base * np.exp(spread * noise) if base else spread * noise
        out[name] = __import__('jax').numpy.asarray(drawn.astype(out[name].dtype))
    for name, factor in factors.items():
        out[name] = (out[name] * factor).astype(out[name].dtype)
    return out
```

```python
import math
from contextlib import ExitStack

import numpy as np

import concourse.bass as bass
from concourse import mybir

F32 = mybir.dt.float32
F32R = mybir.dt.float32r
ALU = mybir.AluOpType
ACT = mybir.ActivationFunctionType
AX = mybir.AxisListType

P = 128
T = 256
TB = T // P
D = 1024
KD = D // P
FF = 2816
KF = FF // P
EPS = 1e-6
GN_EPS = 64e-5
LOG_DECAY = -math.exp(-0.5)
HY = 512
KH = HY // P
CH = 32
NCH = T // CH
ORDERS = 2
NFREQ = 2 * T // P
RING = 4
BANKS = 5

SEGMENTS = [
    ("ffn1_up", 2 * KF, "m"), ("ffn1_down", KF, "k"),
    ("conv_in", 28, "m"), ("gates", 16, "m"), ("hy_out", KH, "k"), ("rw_out", KH, "k"), ("w_out", KD, "k"),
    ("ffn2_up", 2 * KF, "m"), ("ffn2_down", KF, "k"),
    ("xbc", 24, "m"), ("dt", 1, "m"), ("qk", 16, "m"), ("v", KD, "k"), ("z", 16, "m"), ("gates2", 16, "m"),
    ("br_att", KD, "k"), ("br_ssm", 16, "k"), ("mix_out", KD, "k"),
    ("mem_k", KD, "m"), ("mem_v", KD, "k"), ("xq", KD, "m"), ("xo", KD, "k"), ("ffn3_up", 2 * KF, "m"), ("ffn3_down", KF, "k"),
]
SPLIT = {"ffn1_up", "ffn1_down", "conv_in", "ffn2_up", "ffn2_down", "xbc", "dt", "qk", "v", "z", "ffn3_up", "ffn3_down"}
LAST_READER = {"gates": "act", "qk": "act", "z": "act", "gates2": "act", "mem_k": "act", "xq": "act"}

START, COUNT, FIRST_PAIR, PAIRS = {}, {}, {}, {}
PAIR_OWNER = []
_n = 0
_freed = {"dve": 0, "act": 0}
for _name, _tiles, _form in SEGMENTS:
    START[_name], COUNT[_name] = _n, _tiles
    _n += _tiles
    if _form == "m":
        FIRST_PAIR[_name], PAIRS[_name] = len(PAIR_OWNER), (_tiles + 1) // 2
        for _ in range(PAIRS[_name]):
            _e = LAST_READER.get(_name, "dve")
            PAIR_OWNER.append((_e, _freed[_e]))
            _freed[_e] += 1
TILES = _n
RUNS, SPLIT_RANK = [], []
for _name, _tiles, _form in SEGMENTS:
    _split = _name in SPLIT
    for _ in range(_tiles):
        SPLIT_RANK.append(SPLIT_RANK[-1] + _was_split if SPLIT_RANK else 0)
        _was_split = int(_split)
    if RUNS and RUNS[-1][2] == _split:
        RUNS[-1] = (RUNS[-1][0], START[_name] + _tiles, _split)
    else:
        RUNS.append((START[_name], START[_name] + _tiles, _split))
RUN_STARTS = {_first for _first, _, _split in RUNS if _split}

PARAMS = {}
_n = 0
for _name, _cols in [
    ("ffn1_norm", KD), ("mix_norm", KD), ("ffn2_norm", KD), ("final_norm", KD), ("g_pre_mix", KD),
    ("g_post_mix", KD), ("g_pre_xa", KD), ("g_mem", KD), ("g_post_xa", KD), ("g_pre_ffn", KD), ("g_post_ffn", KD),
    ("tap_prev", 28), ("tap_mid", 28), ("tap_next", 28), ("tap_bias", 28),
    ("hy_d", 8), ("w0", 8), ("a0", 8), ("k_k", 4), ("k_a", 4), ("r_k", 4), ("ln_w", 4), ("ln_b", 4),
    ("conv_w", 96), ("conv_b", 24), ("g_ssm", 16), ("d_skip", 16),
    ("sin_b", 2), ("sin_f", 1), ("dt_bias", 1), ("a_log", 1),
]:
    PARAMS[_name] = (_n, _cols)
    _n += _cols
NPARAMS = _n

TABLES = {}
_n = 0
for _name, _cols in [
    ("ident", P), ("ones", P), ("head_ones", P), ("upper", 2 * P), ("level_n", P), ("level_t", 5 * P),
    ("causal", 3 * P), ("neg_causal", 3 * P), ("tri", P), ("until", P), ("keep32", 2 * HY),
    ("minus_t", TB), ("dft", TB * 2 * T), ("idft", NFREQ * T), ("feats", T),
]:
    TABLES[_name] = (_n, _cols)
    _n += _cols
NTABLES = _n
EMB = 33


def tables():
    t = {}
    i = np.arange(P)
    t["ident"] = np.eye(P)
    t["ones"] = np.ones((P, P))
    t["head_ones"] = (i[:, None] // 64 == i[None] // 64).astype(float)
    same = i[:, None] // CH == i[None] // CH
    strict = same & (i[:, None] < i[None])
    t["upper"] = np.concatenate([strict, same & (i[:, None] <= i[None])], 1)
    levels = []
    for l in range(1, 6):
        n = 1 << l
        levels.append((i[:, None] // n == i[None] // n) & (i[:, None] // (n // 2) < i[None] // (n // 2)))
    t["level_t"] = np.concatenate([-levels[0].astype(float)] + [x.astype(float) for x in levels[1:]], 1)
    t["level_n"] = -levels[0].T.astype(float)
    before = (i[:, None] < i[None]).astype(float)
    t["causal"] = np.concatenate([before, np.ones((P, P)), before], 1)
    t["neg_causal"] = -t["causal"]
    t["tri"] = (i[:, None] >= i[None]).astype(float)
    t["until"] = (i[:, None] <= i[None]).astype(float)
    t["keep32"] = np.tile((np.arange(2 * HY) % CH != 0).astype(float), (P, 1))
    n = np.arange(T)[:, None].astype(float)
    f = np.arange(T)[None].astype(float)
    angle = 2 * np.pi * ((n * f) % (2 * T)) / (2 * T)
    re, im = np.cos(angle), -np.sin(angle)
    im[:, 0] = (-1.0) ** np.arange(T)
    dft = np.concatenate([re, im], 1)
    t["dft"] = dft.reshape(TB, P, 2 * T).transpose(1, 0, 2).reshape(P, -1)
    scale = np.full((2 * T, 1), 2.0)
    scale[0] = scale[T] = 1.0
    idft = dft.T * scale / (2 * T)
    t["idft"] = idft.reshape(NFREQ, P, T).transpose(1, 0, 2).reshape(P, -1)
    pos = np.arange(T, dtype=np.float32)
    tt = pos / np.float32(T - 1)
    t["minus_t"] = -tt.reshape(TB, P).T
    ang = (np.float32(2.0 * math.pi / T) * pos)[:, None].astype(np.float64)
    bands = np.linspace(1e-4, 15, 16, dtype=np.float32)[None].astype(np.float64)
    feats = np.concatenate([tt[:, None], np.cos(bands * ang), -np.sin(bands * ang)], 1)
    fp = np.zeros((P, T))
    fp[:EMB] = feats.T
    t["feats"] = fp
    out = np.zeros((P, NTABLES), np.float32)
    for name, (at, cols) in TABLES.items():
        out[:, at:at + cols] = t[name]
    return out


class Jobs:

    def __init__(self):
        self.index, self.engine, self.order = {}, [], []
        self.emptied = {"dve": 0, "act": 0}

    def add(self, name, engine):
        self.index[name] = len(self.order)
        self.order.append((name, engine, self.emptied[engine]))
        self.emptied[engine] += 1


def plan_jobs():
    jobs = Jobs()
    add = jobs.add
    for half in range(2):
        add(("gate_lora", half), "act")
    for half in range(2):
        add(("key_norm", half), "dve")
    for d in range(2):
        for half in range(2):
            add(("decay_lora", d, half), "act")
        for half in range(2):
            add(("rate_lora", d, half), "act")
        for what in ("v", "alpha", "beta", "kappa"):
            for b in range(TB):
                add((what, d, b), "act")
        for u in range(4):
            for e in range(2):
                add(("beta_pairs", d, u, e), "dve")
                add(("kappa_pairs", d, u, e), "dve")
            for e in range(2):
                add(("alpha_beta", d, u, e), "dve")
        for level in range(2, 6):
            add(("product", d, level, 0), "act")
            add(("product", d, level, 1), "act")
            for u in range(4):
                if level < 5:
                    add(("inverse", d, level, u), "dve")
                add(("inverse_t", d, level, u), "dve")
                if u + 2 < 4:
                    add(("product", d, level, u + 2), "act")
        for b in range(TB):
            add(("alpha_v", d, b), "act")
            add(("w_t", d, b), "act")
        for b in range(TB):
            for e in range(2):
                add(("chain", d, b, e), "dve")
        for pair in range(2):
            add(("y", d, pair), "dve")
    for half in range(2):
        add(("mean", half), "dve")
    for half in range(2):
        add(("var", half), "dve")
    for half in range(2):
        add(("bonus", half), "dve")
    add(("sin", 0), "dve")
    add(("sin", 1), "dve")
    for b in range(TB):
        for c in range(4):
            add(("filter", b, c), "dve")
    for o in range(ORDERS):
        add(("filter_norm", o), "dve")
        for m in range(NFREQ):
            add(("filter_dft", o, m), "dve")
        add(("nyquist", o), "dve")
    for o in range(ORDERS):
        for b in range(TB):
            add(("turn", o, b), "act")
        for m in (0, 2, 1, 3):
            add(("dft", o, m), "dve")
        for half in range(2):
            add(("idft", o, half), "dve")
    for i in range(16 + 3):
        if i < 16:
            add(("scores", i), "dve")
        if 2 <= i < 18:
            add(("stick", i - 2), "act")
        if i >= 3 and (i - 3) % 2 == 1:
            add(("attend", (i - 3) // 2), "dve")
    add(("small_turns",), "act")
    add(("b_turn",), "act")
    for g in range(0, 4, 2):
        add(("cb", g), "dve")
    for b in range(TB):
        for c in range(4):
            add(("x_turn", b, c), "dve")
    for g in range(4):
        add(("state", g), "act")
    for g in range(4):
        for b in range(TB):
            for half in range(2):
                add(("decay_rows", g, b, half), "dve")
                add(("ssm_y", g, b, half), "dve")
    for g in range(0, 4, 2):
        add(("group_norm", g), "dve")
    for h in range(4):
        add(("xa_scores", h), "act")
    for h in range(4):
        add(("xa_turn", h), "act")
        add(("xa_out", h), "act")
    return jobs


def build_program(nc, w, params_in, tables_in, x_in, mem_in, lora_in, filt_in, decay_in, out):
    jobs = plan_jobs()
    counts = {}
    with ExitStack() as ctx:
        sems = {}

        def S(name):
            if name not in sems:
                sems[name] = ctx.enter_context(nc.semaphore(name))
                counts[name] = 0
            return sems[name]

        for name in ("tile_used", "job_done", "dve_emptied", "act_emptied", "dve_freed_pair", "act_freed_pair",
                     "acc_read", "x_ready", "sq_ready", "ssq_done", "root_ready", "h_ready", "silu_ready",
                     "high_ready", "low_ready", "h_high", "h_low", "act_high", "act_low",
                     "dve_step", "act_step", "pool_step"):
            S(name)
        landed = [ctx.enter_context(nc.semaphore(f"landed{s}")) for s in range(RING)]

        words = 53208
        base_words = NPARAMS + TABLES["dft"][0] + 2 * KD * T + RING * KD * P + 2 * T + 4 * HY + 2 * T + 28 + 2 + 4 + 3
        base_words += base_words % 2
        base = ctx.enter_context(nc.sbuf_tensor("base", [P, base_words], F32))
        with nc.sbuf_tensor("stages", [P, words - base_words], F32) as stages:
            pass
        split_words = 2 * (KF * T + KD * T + RING * KD * P)
        ctx.enter_context(nc.sbuf_tensor("below_split", [P, words - base_words - split_words], F32))
        act_parts = ctx.enter_context(nc.sbuf_tensor("act_parts", [P, 2 * KF * T], F32R))
        h_parts = ctx.enter_context(nc.sbuf_tensor("h_parts", [P, 2 * KD * T], F32R))
        ring_parts = ctx.enter_context(nc.sbuf_tensor("ring_parts", [P, 2 * RING * KD * P], F32R))
        ACT_HI, ACT_LO = (act_parts[:, i * KF * T:(i + 1) * KF * T].rearrange("p (a b) -> p a b", a=KF) for i in range(2))
        H_HI, H_LO = (h_parts[:, i * KD * T:(i + 1) * KD * T].rearrange("p (a b) -> p a b", a=KD) for i in range(2))
        W_HI, W_LO = (ring_parts[:, i * RING * KD * P:(i + 1) * RING * KD * P]
                      .rearrange("p (a b c) -> p a b c", a=RING, b=KD) for i in range(2))
        top = [0]

        def cut(cols, *shape):
            if top[0] < base_words:
                assert top[0] + cols <= base_words
                a = base[:, top[0]:top[0] + cols]
            else:
                a = stages[:, top[0] - base_words:top[0] - base_words + cols]
            top[0] += cols
            assert top[0] <= words, top[0]
            if len(shape) == 2:
                a = a.rearrange("p (a b) -> p a b", a=shape[0], b=shape[1])
            if len(shape) == 3:
                a = a.rearrange("p (a b c) -> p a b c", a=shape[0], b=shape[1], c=shape[2])
            if len(shape) == 4:
                a = a.rearrange("p (a b c d) -> p a b c d", a=shape[0], b=shape[1], c=shape[2], d=shape[3])
            return a

        par = cut(NPARAMS)
        tab_split = TABLES["dft"][0]
        tab = cut(tab_split)
        x = cut(KD * T, KD, T)
        h = cut(KD * T, KD, T)
        ring = cut(RING * KD * P, RING, KD, P)
        root = cut(T)
        rs = cut(T)
        lora = cut(4 * HY, 4, HY)
        gate_tmp = cut(2 * T, 2, T)
        c_mid = cut(28)
        c_fb = cut(2)
        c_ka = cut(4)
        c_a = cut(1)
        eps = cut(1)
        one_col = cut(1)
        assert base_words - top[0] in (0, 1)
        top[0] = free_from = base_words
        act_raw = cut(KF * T, KF, T)[:, 0:2]
        sq = cut(KD * T, KD, T)
        sq2 = sq.rearrange("p (a b) c -> p a (b c)", a=4)
        x2 = x.rearrange("p (a b) c -> p a (b c)", a=4)

        def param(name, i=0, rows=P):
            at, cols = PARAMS[name]
            assert i < cols
            return par[0:rows, at + i:at + i + 1]

        def table(name, rows=P):
            at, cols = TABLES[name]
            return tab[0:rows, at:at + cols]

        ident, ones, head_ones = table("ident"), table("ones"), table("head_ones")
        upper = table("upper").rearrange("p (a b) -> p a b", a=2)
        level_t = table("level_t").rearrange("p (a b) -> p a b", a=5)

        psum = ctx.enter_context(nc.psum_tensor("psum", [P, 8, 512], F32))
        LP = [psum[:, i, :] for i in range(2)]
        MB = [psum[:, 2 + i, :] for i in range(BANKS)]
        ACC = [psum[:, 2 + i, :] for i in range(4)]
        SS = psum[:, 7, 0:T]

        top[0] = free_from
        U = cut(28 * T, 28, T)
        G = cut(KH * T, KH, T)
        KK = cut(KH * T, KH, T)
        BON = cut(KH * T, KH, T)
        Y = cut(KH * T, KH, T)
        rwkv_from = top[0]
        L = cut(KH * T, KH, T)
        A = cut(KH * T, KH, T)
        AR = cut(2 * KH * T, KH, TB, 2, P)
        BE = cut(KH * T, KH, T)
        KA = cut(KH * T, KH, T)
        hat_from = top[0]
        BH = cut(KH * T, KH, T)
        KHAT = cut(KH * T, KH, T)
        hat_to = top[0]
        TM = {n: cut(TB * HY, TB, HY) for n in ("v", "alpha", "beta", "kappa")}
        BX = cut(4 * 4 * 2 * P, 4, 4, 2, P)
        KX = cut(4 * 4 * 2 * P, 4, 4, 2, P)
        WT = cut(KH * T, KH, T)
        AV = cut(TB * HY, TB, HY)
        EEND = cut(KH * NCH)
        tr_from = top[0]
        C = cut(KH * T, KH, T)
        RV = C
        EX = cut(KH * T, KH, T)
        EP = cut(KH * T, KH, T)
        EN = BH
        rwkv_top = top[0]
        top[0] = tr_from
        TN = cut(4 * HY, 4, 4, P)
        TT = cut(4 * HY, 4, 4, P)
        rwkv_top = top[0]
        top[0] = hat_from
        BT = cut(2 * HY, 2, 4, P)
        PR = cut(2 * HY, 2, 4, P)
        assert top[0] <= hat_to
        top[0] = tr_from
        HS = cut((NCH + 1) * KH * 64, NCH + 1, KH * 64)
        SA = cut(TB * HY, TB, 2, HY // 2)
        assert top[0] <= rwkv_top
        top[0] = rwkv_from
        late_tab = cut(TB * 2 * T + NFREQ * T + T)
        dft = late_tab[:, 0:TB * 2 * T].rearrange("p (a b) -> p a b", a=TB)
        idft = late_tab[:, TB * 2 * T:TB * 2 * T + NFREQ * T].rearrange("p (a b) -> p a b", a=NFREQ)
        feats = late_tab[:, TB * 2 * T + NFREQ * T:]
        filt_w = cut(2 * 64 + 4 * HY)
        sin_in = cut(T)
        sin_k = cut(T)
        sin_out = cut(2 * T, 2, T)
        spectra_from = top[0]
        fsum = cut(2 * 2 * HY, ORDERS, TB, HY)
        fdiff = cut(2 * 2 * HY, ORDERS, TB, HY)
        fnorm = cut(2 * HY, ORDERS, HY)
        FK = cut(2 * NFREQ * HY, ORDERS, NFREQ, HY)
        FKP = cut(2 * HY, ORDERS, HY)
        env_from = top[0]
        env = cut(4 * 2 * HY, TB, 4, HY)
        decay_row = cut(4 * HY, 4, HY)
        top[0] = env_from
        ZF = cut(4 * HY, 4, HY)
        Z2 = cut(KH * T, KH, T)
        top[0] = spectra_from
        ZT = cut(TB * HY, TB, HY)
        YF = cut(NFREQ * HY, NFREQ, HY)
        Z1 = cut(KH * T, KH, T)
        top[0] = env_from + 2 * 4 * HY
        GATE = cut(16 * T, 16, T)
        ZSQ = GATE.rearrange("p (a b) c -> p a (b c)", a=8).rearrange("p (o i) c -> p o i c", o=2)
        GATE2 = GATE.rearrange("p (a b) c -> p a (b c)", b=2)
        top[0] = env_from
        top[0] = rwkv_from
        M1 = cut(KD * T, KD, T)

        top[0] = free_from
        XBC = cut(24 * T, 24, T)
        Z = cut(16 * T, 16, T)
        V2 = cut(TB * D, TB, D)
        OT = cut(KD * T, KD, T)
        QK = cut(16 * T, 16, T)
        Q, K2 = QK[:, 0:KD], QK[:, KD:]
        G2 = QK.rearrange("p (a b) c -> p a (b c)", b=2)
        dtf = cut(6 * T, 6, T)
        mix2_from = top[0]
        NEG = cut(3 * 3 * P, 3, 3 * P)
        SP = cut(3 * 3 * P, 3, 3 * P)
        LM = cut(3 * 3 * P, 3, 3 * P)
        WA = cut(3 * 3 * P, 3, 3 * P)
        top[0] = mix2_from
        SMALL = cut(5 * 32, 5, 32)
        CBT = cut(4 * TB * P, 4, TB, P)
        BTM = cut(4 * P, 4, P)
        XTM = cut(TB * 2 * D, TB, 2 * D)
        XD = cut(2 * D)
        S0 = cut(4 * HY, 4, HY)
        DD = cut(2 * HY, 2, 4, P)
        DM = cut(2 * HY, 2, 4, P)
        CE = cut(2 * HY, 2, 4, P)
        assert top[0] <= words, top[0]
        SQ4 = XTM.rearrange("p a (b c) -> p (a b) c", c=T)
        M2 = XBC[:, 0:KD]
        top[0] = mix2_from
        MX = cut(KD * T, KD, T)
        MX2 = MX.rearrange("p (a b) c -> p a (b c)", b=2)
        HM = cut(KD * T, KD, T)
        KM = cut(KD * T, KD, T)
        VM = cut(TB * D, TB, D)
        XP = cut(4 * 2 * T, 4, TB, T)
        top[0] = free_from
        top[0] += KF * T + KD * T
        XQ = cut(KD * T, KD, T)
        XO = cut(KD * T, KD, T)
        XT = cut(2 * 2 * T, 2, TB, T)
        stat = cut(3 * 8, 3, 8)
        assert top[0] <= mix2_from

        def tell(ins, name, n=1):
            ins.then_inc(S(name), n)
            counts[name] += n
            return counts[name]

        def link(eng, ins, name):
            eng.wait_ge(S(name), tell(ins, name))

        def wait_emptied(eng, name):
            _, engine, before = jobs.order[jobs.index[name]]
            eng.wait_ge(S(engine + "_emptied"), before + 1)

        def wait_filled(eng, name):
            i = jobs.index[name]
            eng.wait_ge(S("job_done"), i + 1)
            return MB[i % BANKS]

        def emptied(ins, name):
            _, engine, before = jobs.order[jobs.index[name]]
            assert tell(ins, engine + "_emptied") == before + 1, name

        def tiles_done(name, n=None):
            return START[name] + (COUNT[name] if n is None else n)

        def pair_freed(eng, name, j):
            engine, before = PAIR_OWNER[FIRST_PAIR[name] + j]
            eng.wait_ge(S(engine + "_freed_pair"), before + 1)

        def flat(a):
            return a.rearrange("p a b -> p (a b)")

        def four(a):
            return a.rearrange("p (a b) -> p a b", a=4)

        def over(a, n):
            return a.unsqueeze(1).broadcast_to([a.shape[0], n, a.shape[1]])

        def along(a, n):
            return a.unsqueeze(2).broadcast_to([a.shape[0], a.shape[1], n])

        NORMS = ["ffn1_norm", "mix_norm", "ffn2_norm", "final_norm", "g_pre_mix", "g_post_mix", "g_mem",
                 "g_pre_xa", "g_post_xa", "g_pre_ffn", "g_post_ffn"]
        X_VERSION = {"mix_norm": 1, "ffn2_norm": 2, "final_norm": 3, "g_pre_mix": 4, "g_pre_xa": 5, "g_pre_ffn": 6}
        H_VERSION = {"ffn1_norm": 1, "mix_norm": 2, "ffn2_norm": 3, "g_pre_mix": 4, "g_mem": 5, "g_pre_xa": 6,
                     "g_pre_ffn": 7}

        SPLIT_VERSION = {1: 0, 2: 1, 3: 2, 4: 3, 7: 4}

        def make_high(act_eng, n, it=None):
            value = 16 * (n // RING + 1)
            act_eng.wait_ge(landed[n % RING], value if it is None else 16 * it + value)
            if n - RING >= max(r for r in RUN_STARTS if r <= n):
                act_eng.wait_ge(S("tile_used"), n - RING + 1 if it is None else RING * it + (n - RING + 1))
            act_eng.activation(flat(W_HI[:, n % RING]), flat(ring[:, n % RING]), ACT.Copy).then_inc(S("high_ready"), 1)

        def make_low(vec, n, it=None):
            value = SPLIT_RANK[n] + 1
            vec.wait_ge(S("high_ready"), value if it is None else RING * it + value)
            vec.tensor_tensor(flat(W_LO[:, n % RING]), flat(ring[:, n % RING]), flat(W_HI[:, n % RING]).bitcast(F32),
                              ALU.subtract).then_inc(S("low_ready"), 1)

        def split_tiles(eng, make, first, end):
            loops = (end - first) // RING
            if loops > 1:
                with eng.Fori(0, loops) as it:
                    for i in range(RING):
                        make(eng, first + i, it)
            else:
                loops = 0
            for n in range(first + RING * loops, end):
                make(eng, n)

        block = ctx.enter_context(nc.Block())

        @block.sync
        def _(sp):
            w_tile = [w[n] for n in range(RING)]
            for s in range(RING):
                sp.dma_start(ring[:, s].rearrange("p a b -> p (a b)"), w_tile[s]).then_inc(landed[s], 16)

            def refill(m, split, it=None):
                slot = m % RING
                if split:
                    value = SPLIT_RANK[m] + 1
                    sp.wait_ge(S("low_ready"), value if it is None else RING * it + value)
                else:
                    sp.wait_ge(S("tile_used"), m + 1 if it is None else RING * it + (m + 1))
                n = m + RING
                sp.dma_start(flat(ring[:, slot]), w[n] if it is None else w[RING * it + n]).then_inc(landed[slot], 16)

            for first, end, split in RUNS:
                end = min(end, TILES - RING)
                loops = (end - first) // RING
                if loops > 1:
                    with sp.Fori(0, loops) as it:
                        for i in range(RING):
                            refill(first + i, split, it)
                else:
                    loops = 0
                for m in range(first + RING * loops, end):
                    refill(m, split)

        @block.tensor
        def _(pe):
            begun = [0]
            accs = [0]

            def mm(o, l, r, start=True, stop=True, loose=False):
                return pe.matmul(o, l, r, start=start, stop=stop, skip_group_check=loose)

            def begin(name):
                i = jobs.index[name]
                assert i == begun[0], (name, i, begun)
                begun[0] += 1
                if i >= BANKS:
                    wait_emptied(pe, jobs.order[i - BANKS][0])
                return MB[i % BANKS]

            def banks_idle():
                for name, engine, _ in reversed(jobs.order[:begun[0]][-BANKS:]):
                    wait_emptied(pe, name)
                if accs[0]:
                    pe.wait_ge(S("acc_read"), accs[0])

            def done(ins):
                tell(ins, "job_done")

            def wait_tile(n, it=None):
                value = 16 * (n // RING + 1)
                pe.wait_ge(landed[n % RING], value if it is None else 16 * it + value)
                return ring[:, n % RING]

            def norm_sum(i):
                for c in range(4):
                    pe.wait_ge(S("sq_ready"), 4 * i + c + 1)
                    for k in (2 * c, 2 * c + 1):
                        m = mm(SS, ones, sq[:, k], start=k == 0, stop=k == KD - 1)
                tell(m, "ssq_done")

            def mm3(o, l_hi, l_lo, r_hi, r_lo, start, stop, loose=False):
                mm(o, l_hi, r_hi, start=start, stop=False, loose=loose)
                mm(o, l_hi, r_lo, start=False, stop=False, loose=loose)
                return mm(o, l_lo, r_hi, start=False, stop=stop, loose=loose)

            def wait_parts(n, it=None):
                value = SPLIT_RANK[n] + 1
                pe.wait_ge(S("low_ready"), value if it is None else RING * it + value)
                return W_HI[:, n % RING], W_LO[:, n % RING]

            def pair(name, j, rhs, it=None, parts_of=None):
                g = FIRST_PAIR[name] + j
                if g >= 2:
                    engine, before = PAIR_OWNER[g - 2]
                    pe.wait_ge(S(engine + "_freed_pair"), before + 1 if it is None else before + 1 + 2 * it)
                for half in range(2):
                    if 2 * j + half >= COUNT[name]:
                        break
                    n = START[name] + 2 * j + half
                    dst = LP[g % 2][:, half * T:half * T + T]
                    if name in SPLIT:
                        hi, lo = wait_parts(n, it)
                        for k in range(KD):
                            if parts_of is not None and half == 0:
                                pe.wait_ge(S("h_low"), KD * parts_of + k + 1)
                            m = mm3(dst, hi[:, k], lo[:, k], H_HI[:, k], H_LO[:, k], k == 0, k == KD - 1)
                    else:
                        tile = wait_tile(n, it)
                        for k in range(KD):
                            m = mm(dst, tile[:, k], rhs[:, k], start=k == 0, stop=k == KD - 1)
                    m.then_inc(S("tile_used"), 1)

            def ups(name, rhs, version):
                if name not in SPLIT:
                    pe.wait_ge(S("h_ready"), KD * version)
                pairs = PAIRS[name]
                for j in range(min(2, pairs)):
                    pair(name, j, rhs, None, SPLIT_VERSION[version] if name in SPLIT and j == 0 else None)
                loops = (pairs - 2) // 2
                if COUNT[name] % 2:
                    loops = 0
                if loops > 1:
                    with pe.Fori(0, loops) as it:
                        pair(name, 2, rhs, it)
                        pair(name, 3, rhs, it)
                else:
                    loops = 0
                for j in range(2 + 2 * loops, pairs):
                    pair(name, j, rhs)

            def acc_tile(n, rhs, first, last, it=None):
                tile = wait_tile(n, it)
                for m_ in range(KD):
                    m = mm(ACC[m_ // 2][:, (m_ % 2) * T:(m_ % 2) * T + T], tile[:, m_], rhs,
                           start=first and m_ % 2 == 0, stop=last, loose=True)
                m.then_inc(S("tile_used"), 1)

            def downs(name, rhs):
                banks_idle()
                for k in range(COUNT[name]):
                    acc_tile(START[name] + k, rhs[:, k], k == 0, k == COUNT[name] - 1)
                accs[0] += 1

            def ffn_down(name, index):
                banks_idle()
                n0 = START[name]

                def one(k, it=None):
                    hi, lo = wait_parts(n0 + k, it)
                    value = KF * index + k + 1
                    pe.wait_ge(S("act_low"), value if it is None else RING * it + value)
                    at = k if it is None else RING * it + k
                    for m_ in range(KD):
                        m = mm3(ACC[m_ // 2][:, (m_ % 2) * T:(m_ % 2) * T + T], hi[:, m_], lo[:, m_],
                                ACT_HI[:, at], ACT_LO[:, at], it is None and k == 0 and m_ % 2 == 0,
                                it is None and k == KF - 1, loose=True)
                    m.then_inc(S("tile_used"), 1)

                one(0)
                one(1)
                with pe.Fori(0, 4) as it:
                    for i in range(4):
                        one(2 + i, it)
                for k in range(KF - 4, KF):
                    one(k)
                accs[0] += 1

            def by_token(name, src):
                banks_idle()
                for k in range(COUNT[name]):
                    if name in SPLIT:
                        hi, lo = (flat(part) for part in wait_parts(START[name] + k))
                    else:
                        tile = flat(wait_tile(START[name] + k))
                    for b in range(TB):
                        at = slice(b * P, b * P + P)
                        for half in range(2):
                            cols = slice(half * HY, half * HY + HY)
                            if name in SPLIT:
                                m = mm3(ACC[2 * b + half], H_HI[:, k, at], H_LO[:, k, at], hi[:, cols], lo[:, cols],
                                        k == 0, k == COUNT[name] - 1, loose=True)
                            else:
                                m = mm(ACC[2 * b + half], src[:, k, at], tile[:, cols],
                                       start=k == 0, stop=k == COUNT[name] - 1, loose=True)
                    m.then_inc(S("tile_used"), 1)
                accs[0] += 1

            pe.wait_ge(S("in_x"), 16 * 3)
            norm_sum(0)
            ups("ffn1_up", h, 1)
            ffn_down("ffn1_down", 0)
            norm_sum(1)
            ups("conv_in", h, 2)

            banks_idle()
            pe.wait_ge(S("in_small"), 16)
            pe.wait_ge(S("lora_in"), 2)
            for half in range(2):
                o = begin(("gate_lora", half))
                for qq in range(2):
                    q = 2 * half + qq
                    mm(o[:, qq * T:qq * T + T], lora[:, 2, q * P:q * P + P], U[:, 14], stop=False)
                    m = mm(o[:, qq * T:qq * T + T], lora[0:32, 3, q * P:q * P + P], U[0:32, 15], start=False)
                done(m)
            for half in range(2):
                pe.wait_ge(S("kk_sq"), 1)
                o = begin(("key_norm", half))
                done(mm(o, head_ones, flat(Y[:, 2 * half:2 * half + 2])))
            for d in range(2):
                rows = slice(64 * d, 64 * d + 64)
                for name, wi, ui in (("decay_lora", 0, 12), ("rate_lora", 1, 13)):
                    for half in range(2):
                        o = begin((name, d, half))
                        for qq in range(2):
                            q = 2 * half + qq
                            m = mm(o[:, qq * T:qq * T + T], lora[rows, wi, q * P:q * P + P], U[rows, ui])
                        done(m)
                pe.wait_ge(S("dir_ready"), d + 1)
                for what, src in (("v", RV), ("alpha", None), ("beta", BH), ("kappa", KHAT)):
                    for b in range(TB):
                        o = begin((what, d, b))
                        for q in range(KH):
                            s_ = AR[:, q, b, 0] if src is None else src[:, q, b * P:b * P + P]
                            m = pe.transpose(o[:, q * P:q * P + P], s_, ident)
                        done(m)
                for u in range(4):
                    b = u // 2
                    for e in range(2):
                        r = slice(64 * e, 64 * e + 64)
                        for name, src in (("beta_pairs", BE), ("kappa_pairs", KA)):
                            o = begin((name, d, u, e))
                            for qq in range(2):
                                q = 2 * (u % 2) + qq
                                m = mm(o[:, qq * T:qq * T + T], src[r, q, b * P:b * P + P],
                                       AR[r, q, b].rearrange("p a b -> p (a b)"))
                            done(m)
                    for e in range(2):
                        r = slice(64 * e, 64 * e + 64)
                        o = begin(("alpha_beta", d, u, e))
                        for qq in range(2):
                            q = 2 * (u % 2) + qq
                            m = mm(o[:, qq * P:qq * P + P], AR[r, q, b, 0], BE[r, q, b * P:b * P + P])
                        done(m)

                def product(level, u):
                    o = begin(("product", d, level, u))
                    if level > 2:
                        wait_emptied(pe, ("inverse", d, level - 1, u))
                    else:
                        pe.wait_ge(S("first_level"), 4 * d + u + 1)
                    pe.wait_ge(S("off_diagonal"), 16 * d + 4 * (level - 2) + u + 1)
                    for hh in range(4):
                        m = mm(o[:, hh * P:hh * P + P], BT[:, u % 2, hh], TN[:, u, hh])
                    done(m)

                for level in range(2, 6):
                    product(level, 0)
                    product(level, 1)
                    for u in range(4):
                        if level > 2:
                            wait_emptied(pe, ("inverse_t", d, level - 1, u))
                        wait_emptied(pe, ("product", d, level, u))
                        if level < 5:
                            o = begin(("inverse", d, level, u))
                            for hh in range(4):
                                m = mm(o[:, hh * P:hh * P + P], TT[:, u, hh], PR[:, u % 2, hh])
                            done(m)
                        o = begin(("inverse_t", d, level, u))
                        for hh in range(4):
                            m = mm(o[:, hh * P:hh * P + P], PR[:, u % 2, hh], TT[:, u, hh])
                        done(m)
                        if u + 2 < 4:
                            product(level, u + 2)
                for b in range(TB):
                    wait_emptied(pe, ("v", d, b))
                    wait_emptied(pe, ("alpha", d, b))
                    wait_emptied(pe, ("kappa_pairs", d, 3, 1))
                    wait_emptied(pe, ("inverse_t", d, 5, 3))
                    o = begin(("alpha_v", d, b))
                    for hd in range(8):
                        u, hh = 2 * b + hd // 4, hd % 4
                        m = mm(o[:, hd * 64:hd * 64 + 64], KX[:, u, hh, 0], TM["v"][:, b, hd * 64:hd * 64 + 64])
                    done(m)
                    o = begin(("w_t", d, b))
                    for hd in range(8):
                        u, hh = 2 * b + hd // 4, hd % 4
                        m = mm(o[64 * (hd % 2):64 * (hd % 2) + 64, (hd // 2) * P:(hd // 2) * P + P],
                               TM["alpha"][:, b, hd * 64:hd * 64 + 64], TT[:, u, hh])
                    done(m)
                wait_emptied(pe, ("beta", d, 1))
                wait_emptied(pe, ("kappa", d, 1))
                for c in range(NCH):
                    b, r = c // 4, slice(CH * (c % 4), CH * (c % 4) + CH)
                    if c % 4 == 0:
                        wait_emptied(pe, ("alpha_v", d, b))
                        wait_emptied(pe, ("w_t", d, b))
                        o2 = [begin(("chain", d, b, e)) for e in range(2)]
                        for e in range(2):
                            for q in range(KH):
                                hd = 2 * q + e
                                u, hh = 2 * b + hd // 4, hd % 4
                                m = mm(o2[e][:, q * 64:q * 64 + 64], TT[:, u, hh], AV[:, b, hd * 64:hd * 64 + 64],
                                       start=q == 0, stop=c == 0, loose=True)
                    if c:
                        pe.wait_ge(S("state_ready"), 7 * d + c)
                        for e in range(2):
                            er = slice(64 * e, 64 * e + 64)
                            for q in range(KH):
                                m = mm(o2[e][r, q * 64:q * 64 + 64], WT[er, q, c * CH:c * CH + CH],
                                       HS[er, c, q * 64:q * 64 + 64], start=False, stop=True, loose=True)
                            if c % 4 == 3:
                                done(m)
                    if c % 4 < 3:
                        tell(m, "sa_psum")
                    if c == NCH - 1:
                        break
                    for hd in range(8):
                        q, e = hd // 2, slice(64 * (hd % 2), 64 * (hd % 2) + 64)
                        mm(LP[c % 2][e, q * 64:q * 64 + 64], TM["kappa"][r, b, hd * 64:hd * 64 + 64],
                           TM["v"][r, b, hd * 64:hd * 64 + 64], start=hd < 2, stop=False, loose=True)
                    pe.wait_ge(S("sa_ready"), 8 * d + c + 1)
                    for hd in range(8):
                        q, e = hd // 2, slice(64 * (hd % 2), 64 * (hd % 2) + 64)
                        m = mm(LP[c % 2][e, q * 64:q * 64 + 64], TM["beta"][r, b, hd * 64:hd * 64 + 64],
                               SA[r, b, hd % 2, q * 64:q * 64 + 64], start=False, stop=True, loose=True)
                    tell(m, "state_psum")
                pe.wait_ge(S("sa_ready"), 8 * d + NCH)
                for pr in range(2):
                    o = begin(("y", d, pr))
                    for qq in range(2):
                        q = 2 * pr + qq
                        for e in range(2):
                            er = slice(64 * e, 64 * e + 64)
                            hd = 2 * q + e
                            for b in range(TB):
                                u, hh = 2 * b + hd // 4, hd % 4
                                cols = slice(qq * T + b * P, qq * T + b * P + P)
                                mm(o[er, cols], SA[:, b, e, q * 64:q * 64 + 64], BX[:, u, hh, 1],
                                   start=qq == 0 and b == 0, stop=False, loose=True)
                                m = mm(o[er, cols], TM["v"][:, b, hd * 64:hd * 64 + 64], KX[:, u, hh, 1],
                                       start=False, stop=True, loose=True)
                                for cc in range(4):
                                    if 4 * b + cc == 0:
                                        continue
                                    at = qq * T + b * P + cc * CH
                                    m = mm(o[er, at:at + CH], HS[er, 4 * b + cc, q * 64:q * 64 + 64],
                                           AR[er, q, b, 1, cc * CH:cc * CH + CH], start=False, stop=True, loose=True)
                    done(m)
            wait_emptied(pe, ("y", 1, 1))
            for half in range(2):
                o = begin(("mean", half))
                done(mm(o, head_ones, flat(Y[:, 2 * half:2 * half + 2])))
            for half in range(2):
                pe.wait_ge(S("y_sq"), half + 1)
                o = begin(("var", half))
                done(mm(o, head_ones, flat(KA[:, 2 * half:2 * half + 2])))
            for half in range(2):
                o = begin(("bonus", half))
                done(mm(o, head_ones, flat(BON[:, 2 * half:2 * half + 2])))

            pe.wait_ge(S("in_hyena"), 16 * 3)
            o = begin(("sin", 0))
            done(mm(o[0:64, 0:T], filt_w[0:EMB, 0:64], feats[0:EMB, :]))
            pe.wait_ge(S("sin_ready"), 1)
            o = begin(("sin", 1))
            done(mm(o[0:64, 0:T], filt_w[0:64, 64:128], sin_out[0:64, 0]))
            pe.wait_ge(S("sin_ready"), 2)
            for b in range(TB):
                for c in range(4):
                    o = begin(("filter", b, c))
                    done(mm(o, sin_out[0:65, 1, b * P:b * P + P], filt_w[0:65, 128 + c * HY:128 + c * HY + HY]))
            for o_ in range(ORDERS):
                pe.wait_ge(S("filt_sq"), 4 * (o_ + 1))
                o = begin(("filter_norm", o_))
                for i in range(4):
                    m = mm(o, ones, ZSQ[:, o_, i], start=i == 0, stop=i == 3)
                done(m)
                pe.wait_ge(S("filt_sum"), 4 * (o_ + 1))
                for m_ in range(NFREQ):
                    o = begin(("filter_dft", o_, m_))
                    src = fsum if m_ < 2 else fdiff
                    for b in range(TB):
                        m = mm(o, dft[:, b, m_ * P:m_ * P + P], src[:, o_, b], start=b == 0, stop=b == 1)
                    done(m)
                o = begin(("nyquist", o_))
                for b in range(TB):
                    m = mm(o[0:1], dft[:, b, T:T + 1], fsum[:, o_, b], start=b == 0, stop=b == 1)
                done(m)
            for o_ in range(ORDERS):
                src = U[:, 24:28] if o_ == 0 else Z1
                if o_:
                    wait_emptied(pe, ("idft", 0, 1))
                else:
                    wait_emptied(pe, ("nyquist", 1))
                for b in range(TB):
                    o = begin(("turn", o_, b))
                    for q in range(KH):
                        m = pe.transpose(o[:, q * P:q * P + P], src[:, q, b * P:b * P + P], ident)
                    done(m)
                wait_emptied(pe, ("turn", o_, 1))
                for m_ in (0, 2, 1, 3):
                    o = begin(("dft", o_, m_))
                    for b in range(TB):
                        m = mm(o, dft[:, b, m_ * P:m_ * P + P], ZT[:, b], start=b == 0, stop=b == 1)
                    done(m)
                pe.wait_ge(S("spectrum_ready"), 2 * (o_ + 1))
                for half in range(2):
                    o = begin(("idft", o_, half))
                    for qq in range(2):
                        q = 2 * half + qq
                        for m_ in range(NFREQ):
                            m = mm(o[:, qq * T:qq * T + T], YF[:, m_, q * P:q * P + P], idft[:, m_],
                                   start=m_ == 0, stop=m_ == NFREQ - 1)
                    done(m)
            ups("gates", h, 2)
            wait_emptied(pe, ("idft", 1, 1))
            downs("hy_out", Z2)
            pe.wait_ge(S("rwkv_done"), 1)
            downs("rw_out", Y)
            pe.wait_ge(S("merged"), 1)
            downs("w_out", M1)
            norm_sum(2)
            ups("ffn2_up", h, 3)
            ffn_down("ffn2_down", 1)
            norm_sum(3)
            norm_sum(4)

            ups("xbc", h, 4)
            ups("dt", h, 4)
            ups("qk", h, 4)
            by_token("v", h)
            ups("z", h, 4)
            banks_idle()
            for j in range(PAIRS["qk"]):
                pass
            pair_freed(pe, "qk", PAIRS["qk"] - 1)

            def scores_into(o, i, start, stop):
                q, r = i // 2, slice(64 * (i % 2), 64 * (i % 2) + 64)
                mm(o[:, 0:T], K2[r, q, 0:P], Q[r, q, :], start=start, stop=stop, loose=True)
                return mm(o[:, T:T + P], K2[r, q, P:T], Q[r, q, P:T], start=False, stop=stop, loose=True)

            for i in range(16 + 3):
                if i < 16:
                    o = begin(("scores", i))
                    done(scores_into(o, i, True, True))
                if 2 <= i < 18:
                    hd = i - 2
                    o = begin(("stick", hd))
                    scores_into(o, hd, True, False)
                    pe.wait_ge(S("log_ready"), hd + 1)
                    lm = LM[:, hd % 3]
                    mm(o[:, 0:T], table("tri"), lm[:, 0:T], start=False, stop=False, loose=True)
                    mm(o[:, P:T], ones, lm[:, T:T + P], start=False, stop=True, loose=True)
                    done(mm(o[:, T:T + P], table("tri"), lm[:, T:T + P], start=False, stop=True, loose=True))
                if i >= 3 and (i - 3) % 2 == 1:
                    q = (i - 3) // 2
                    o = begin(("attend", q))
                    for e in range(2):
                        hd = 2 * q + e
                        pe.wait_ge(S("stick_weights"), hd + 1)
                        wa = WA[:, hd % 3]
                        r = slice(64 * e, 64 * e + 64)
                        mm(o[r, 0:T], V2[:, 0, hd * 64:hd * 64 + 64], wa[:, 0:T], start=True, stop=False, loose=True)
                        m = mm(o[r, P:T], V2[:, 1, hd * 64:hd * 64 + 64], wa[:, T:T + P], start=False, stop=True, loose=True)
                    done(m)
            pe.wait_ge(S("dt_ready"), 1)
            o = begin(("small_turns",))
            for j, src in enumerate((dtf[0:32, 2, 0:P], dtf[0:32, 2, P:T], dtf[0:32, 0, 0:P], dtf[0:32, 0, P:T],
                                     dtf[0:32, 4, 0:P])):
                m = pe.transpose(o[:, 32 * j:32 * j + 32], src, ident[0:32, 0:32])
            done(m)
            pe.wait_ge(S("xbc_ready"), 3)
            o = begin(("b_turn",))
            for g in range(4):
                m = pe.transpose(o[:, g * P:g * P + P], XBC[:, 16 + g, 0:P], ident)
            done(m)
            for g0 in range(0, 4, 2):
                o = begin(("cb", g0))
                for gg in range(2):
                    for b in range(TB):
                        at = (gg * TB + b) * P
                        m = mm(o[:, at:at + P], XBC[:, 16 + g0 + gg, b * P:b * P + P], XBC[:, 20 + g0 + gg, b * P:b * P + P])
                done(m)
            for b in range(TB):
                for c in range(4):
                    o = begin(("x_turn", b, c))
                    for q in range(4):
                        m = pe.transpose(o[:, q * P:q * P + P], XBC[:, 4 * c + q, b * P:b * P + P], ident)
                    done(m)
            wait_emptied(pe, ("b_turn",))
            for g in range(4):
                pe.wait_ge(S("xd_ready"), 1)
                o = begin(("state", g))
                done(mm(o, BTM[:, g], XD[:, g * HY:g * HY + HY]))
            turn = 0
            for g in range(4):
                for b in range(TB):
                    for half in range(2):
                        o = begin(("decay_rows", g, b, half))
                        for i in range(4):
                            hd = 8 * g + 4 * half + i
                            m = mm(o[:, i * P:i * P + P], ident[0:32, hd:hd + 1].broadcast_to([32, P]),
                                   dtf[0:32, 2, b * P:b * P + P])
                        done(m)
                        turn += 1
                        pe.wait_ge(S("ssm_mix_ready"), turn)
                        o = begin(("ssm_y", g, b, half))
                        if b:
                            wait_emptied(pe, ("state", g))
                        for i in range(4):
                            hd = 8 * g + 4 * half + i
                            dst = o[64 * (i % 2):64 * (i % 2) + 64, (i // 2) * P:(i // 2) * P + P]
                            m = mm(dst, XTM[:, b, hd * 64:hd * 64 + 64], DM[:, turn % 2, i],
                                   start=i < 2, stop=b == 0, loose=True)
                            if b:
                                m = mm(dst, S0[:, g, (4 * half + i) * 64:(4 * half + i) * 64 + 64], CE[:, turn % 2, i],
                                       start=False, stop=True, loose=True)
                        done(m)
            for g0 in range(0, 4, 2):
                o = begin(("group_norm", g0))
                for gg in range(2):
                    pe.wait_ge(S("gy_sq"), g0 + gg + 1)
                    for q in range(4):
                        m = mm(o[:, gg * T:gg * T + T], ones, SQ4[:, 4 * (g0 + gg) + q], start=q == 0, stop=q == 3)
                done(m)
            ups("gates2", h, 4)
            wait_emptied(pe, ("attend", 7))
            downs("br_att", OT)
            pe.wait_ge(S("ssm_done"), 1)
            downs("br_ssm", XBC)
            pe.wait_ge(S("merged"), 2)
            downs("mix_out", M2)
            norm_sum(5)

            norm_sum(6)
            ups("mem_k", HM, 5)
            by_token("mem_v", HM)
            norm_sum(7)
            ups("xq", h, 6)
            banks_idle()
            pair_freed(pe, "mem_k", 3)
            pair_freed(pe, "xq", 3)
            for hd in range(4):
                o = begin(("xa_scores", hd))
                for b in range(TB):
                    for c in range(2):
                        m = mm(o[:, b * T:b * T + T], XQ[:, 2 * hd + c, b * P:b * P + P], KM[:, 2 * hd + c],
                               start=c == 0, stop=c == 1)
                done(m)
            for hd in range(4):
                pe.wait_ge(S("xa_probs"), hd + 1)
                o = begin(("xa_turn", hd))
                for mb in range(2):
                    for b in range(TB):
                        m = pe.transpose(o[:, mb * T + b * P:mb * T + b * P + P], XP[:, hd, b, mb * P:mb * P + P], ident)
                done(m)
                wait_emptied(pe, ("xa_turn", hd))
                o = begin(("xa_out", hd))
                for dd in range(2):
                    for mb in range(2):
                        m = mm(o[:, dd * T:dd * T + T], VM[:, mb, hd * T + dd * P:hd * T + dd * P + P], XT[:, hd % 2, mb],
                               start=mb == 0, stop=mb == 1)
                done(m)
            wait_emptied(pe, ("xa_out", 3))
            downs("xo", XO)
            norm_sum(8)
            norm_sum(9)
            ups("ffn3_up", h, 7)
            ffn_down("ffn3_down", 2)
            norm_sum(10)

        @block.scalar
        def _(a):
            def f(o, i, func, **kw):
                return a.activation(o, i, func, **kw)

            def squares(i, first_tile=None):
                name = NORMS[i]
                after = {"g_post_mix": "mix_out", "g_post_xa": "xo", "g_post_ffn": "ffn3_down"}
                if i:
                    a.wait_ge(S("ssq_done"), i)
                if name in after:
                    a.wait_ge(S("tile_used"), tiles_done(after[name]))
                if name == "ffn1_norm":
                    a.wait_ge(S("in_x"), 48)
                if name == "g_mem":
                    a.wait_ge(S("in_mem"), 16)
                src = [ACC[c] for c in range(4)] if name in after else [(MX2 if name == "g_mem" else x2)[:, c] for c in range(4)]
                for c in range(4):
                    if name in X_VERSION:
                        a.wait_ge(S("x_ready"), 4 * (X_VERSION[name] - 1) + c + 1)
                    tell(f(sq2[:, c], src[c], ACT.Square), "sq_ready")
                if first_tile is not None:
                    make_high(a, first_tile)
                    make_high(a, first_tile + 1)
                if i:
                    a.wait_ge(S("root_read"), i)
                a.wait_ge(S("ssq_done"), i + 1)
                tell(f(root, SS, ACT.Sqrt, scale=1.0 / D, bias=eps[:, 0:1]), "root_ready")

            def split_h(version):
                for k in range(KD):
                    a.wait_ge(S("h_ready"), KD * (version - 1) + k + 1)
                    tell(f(H_HI[:, k], h[:, k], ACT.Copy), "h_high")

            def ahead(name, j, it=None):
                for n in (START[name] + 2 * j + 2, START[name] + 2 * j + 3):
                    make_high(a, n, it)

            def silus(name, version):
                n0, fp = START[name], FIRST_PAIR[name]
                before = PAIR_OWNER[fp][1]

                def one(j, it=None):
                    ahead(name, j, it)
                    tw = n0 + 2 * j + 2
                    a.wait_ge(S("tile_used"), tw if it is None else 2 * 2 * it + tw)
                    if j >= 2:
                        fr = before + j - 1
                        a.wait_ge(S("dve_freed_pair"), fr if it is None else 2 * it + fr)
                    f(gate_tmp[:, j % 2], LP[(fp + j) % 2][:, 0:T], ACT.Silu).then_inc(S("silu_ready"), 1)

                one(0)
                one(1)
                with a.Fori(0, (KF - 2) // 2) as it:
                    one(2, it)
                    one(3, it)
                down = n0 + 2 * KF
                split_tiles(a, make_high, down + 2, down + KF + (0 if name == "ffn3_up" else 2))

            def pair_loop(name, body):
                loops, n0 = PAIRS[name] // 2, START[name]
                last = name in SPLIT and name != "xbc"
                with a.Fori(0, loops - last) as it:
                    for p in range(2):
                        if name in SPLIT:
                            ahead(name, p, it)
                        a.wait_ge(S("tile_used"), n0 + 2 * p + 2 + 4 * it)
                        body(p, it)
                if last:
                    for p in range(2):
                        if p == 0:
                            ahead(name, 2 * (loops - 1))
                        a.wait_ge(S("tile_used"), n0 + 4 * (loops - 1) + 2 * p + 2)
                        body(p, loops - 1)

            a.dma_start(par, params_in).then_inc(S("in_x"), 16)
            a.dma_start(flat(x), x_in).then_inc(S("in_x"), 16)
            a.dma_start(tab, tables_in[:, 0:tab_split]).then_inc(S("in_x"), 16)
            a.dma_start(flat(lora), lora_in).then_inc(S("in_small"), 16)
            a.wait_ge(S("consts"), 2)
            squares(0, START["ffn1_up"])
            split_h(1)
            tell(f(c_a[0:32], param("a_log", 0, 32), ACT.Exp), "c_a_exp")
            silus("ffn1_up", 0)
            squares(1)
            split_h(2)
            a.wait_ge(S("coefs"), 2)

            def taps_mid(p, it):
                bank = LP[(FIRST_PAIR["conv_in"] + p) % 2]
                at = PARAMS["tap_bias"][0]
                for half in range(2):
                    blk = 4 * it + (2 * p + half)
                    ins = f(U[:, blk], bank[:, half * T:half * T + T], ACT.Identity, scale=c_mid[:, bass.ds(blk, 1)],
                            bias=par[:, bass.ds(blk + at, 1)])
                ins.then_inc(S("mid_ready"), 1)

            pair_loop("conv_in", taps_mid)

            pair_freed(a, "conv_in", 7)
            tell(f(U[:, 12], U[:, 12], ACT.Tanh), "lora_in")
            tell(f(U[:, 14:16], U[:, 14:16], ACT.Sigmoid), "lora_in")
            for half in range(2):
                o = wait_filled(a, ("gate_lora", half))
                emptied(f(flat(G[:, 2 * half:2 * half + 2]), o, ACT.Copy), ("gate_lora", half))
            a.wait_ge(S("kk_raw"), 1)
            tell(f(Y, KK, ACT.Square), "kk_sq")
            wait_emptied(a, ("key_norm", 1))
            tell(f(BON, BON, ACT.Sqrt), "kk_root")
            for d in range(2):
                if d:
                    a.wait_ge(S("dir_ready"), d)
                for name, dst, bias in (("decay_lora", L, "w0"), ("rate_lora", A, "a0")):
                    for half in range(2):
                        o = wait_filled(a, (name, d, half))
                        for qq in range(2):
                            q = 2 * half + qq
                            to = dst[:, q, ::-1] if d else dst[:, q, :]
                            ins = f(to, o[:, qq * T:qq * T + T], ACT.Sigmoid, bias=param(bias, 4 * d + q))
                        emptied(ins, (name, d, half))
                a.wait_ge(S("cum_ready"), 2 * d + 1)
                tell(f(EP, C, ACT.Exp), "exps")
                tell(f(EN, C, ACT.Exp, scale=-1.0), "exps")
                a.wait_ge(S("cum_ready"), 2 * d + 2)
                tell(f(EX, EX, ACT.Exp), "exps")
                for what in ("v", "alpha", "beta", "kappa"):
                    for b in range(TB):
                        o = wait_filled(a, (what, d, b))
                        emptied(f(TM[what][:, b], o, ACT.Copy), (what, d, b))
                for level in range(2, 6):
                    for u in range(4):
                        o = wait_filled(a, ("product", d, level, u))
                        emptied(f(PR[:, u % 2], four(o), ACT.Copy), ("product", d, level, u))
                for b in range(TB):
                    o = wait_filled(a, ("alpha_v", d, b))
                    emptied(f(AV[:, b], o, ACT.Copy), ("alpha_v", d, b))
                    o = wait_filled(a, ("w_t", d, b))
                    emptied(f(WT[:, :, b * P:b * P + P], four(o), ACT.Copy), ("w_t", d, b))
            for half in range(2):
                wait_emptied(a, ("mean", half))
                tell(f(KA[:, 2 * half:2 * half + 2], Y[:, 2 * half:2 * half + 2], ACT.Square), "y_sq")
            wait_emptied(a, ("var", 1))
            tell(f(BE, BE, ACT.Sqrt), "y_root")

            a.wait_ge(S("rwkv_done"), 1)
            a.dma_start(late_tab, tables_in[:, tab_split:]).then_inc(S("in_hyena"), 16)
            a.dma_start(filt_w, filt_in).then_inc(S("in_hyena"), 16)
            a.dma_start(flat(decay_row), decay_in.partition_broadcast(P)).then_inc(S("in_hyena"), 16)
            a.wait_ge(S("in_hyena"), 48)
            link(a, f(decay_row, decay_row, ACT.Abs), "act_step")
            for b in range(TB):
                tell(f(env[:, b], decay_row, ACT.Exp, scale=table("minus_t")[:, b:b + 1]), "env_ready")
            for i in range(2):
                a.wait_ge(S("sin_args"), i + 1)
                tell(f(sin_out[0:64, i], sin_in[0:64], ACT.Sin), "sin_ready")
            for o_ in range(ORDERS):
                a.wait_ge(S("filt_made"), 1)
                for i in range(4):
                    tell(f(ZSQ[:, o_, i], env[:, i % 2, 2 * (i // 2) + o_], ACT.Square), "filt_sq")
            for o_ in range(ORDERS):
                o = wait_filled(a, ("filter_norm", o_))
                tell(f(fnorm[:, o_], o, ACT.Sqrt, bias=eps[:, 0:1]), "filt_root")
            for o_ in range(ORDERS):
                for b in range(TB):
                    o = wait_filled(a, ("turn", o_, b))
                    emptied(f(ZT[:, b], o, ACT.Copy), ("turn", o_, b))

            def gates(p, it):
                bank = LP[(FIRST_PAIR["gates"] + p) % 2]
                f(GATE2[:, 2 * it + p], bank, ACT.Sigmoid).then_inc(S("act_freed_pair"), 1)

            pair_loop("gates", gates)
            squares(2, START["ffn2_up"])
            split_h(3)
            silus("ffn2_up", 1)
            squares(3)
            squares(4)
            split_h(4)


            def conv_last(p, it):
                bank = LP[(FIRST_PAIR["xbc"] + p) % 2]
                at, bt = PARAMS["conv_w"][0] + 72, PARAMS["conv_b"][0]
                for half in range(2):
                    blk = 4 * it + (2 * p + half)
                    ins = f(XBC[:, blk], bank[:, half * T:half * T + T], ACT.Identity,
                            scale=par[:, bass.ds(blk + at, 1)], bias=par[:, bass.ds(blk + bt, 1)])
                ins.then_inc(S("mid2_ready"), 1)

            pair_loop("xbc", conv_last)
            make_high(a, START["dt"] + 2)
            for at, scale in ((0, 0.125), (4, 1.0)):
                with a.Fori(0, 2) as it:
                    for p in range(2):
                        ahead("qk", at + p, it)
                        a.wait_ge(S("tile_used"), START["qk"] + 2 * (at + p) + 2 + 4 * it)
                        f(G2[:, 2 * it + (at + p)], LP[(FIRST_PAIR["qk"] + p) % 2], ACT.Copy, scale=scale)\
                            .then_inc(S("act_freed_pair"), 1)

            split_tiles(a, make_high, START["v"] + 2, START["z"] + 2)

            def z_silu(p, it):
                bank = LP[(FIRST_PAIR["z"] + p) % 2]
                f(flat(Z).rearrange("p (a b) -> p a b", b=2 * T)[:, 2 * it + p], bank, ACT.Silu)\
                    .then_inc(S("act_freed_pair"), 1)

            pair_loop("z", z_silu)
            a.wait_ge(S("dt_neg"), 1)
            link(a, f(dtf[0:32, 1], dtf[0:32, 1], ACT.Exp), "act_step")
            tell(f(dtf[0:32, 1], dtf[0:32, 1], ACT.Ln, bias=one_col[0:32, 0:1]), "dt_log")
            pair_freed(a, "xbc", PAIRS["xbc"] - 1)
            for c in range(3):
                tell(f(XBC[:, 8 * c:8 * c + 8], XBC[:, 8 * c:8 * c + 8], ACT.Silu), "xbc_ready")
            for i in range(18):
                if i < 16:
                    a.wait_ge(S("neg_abs"), i + 1)
                    link(a, f(NEG[:, i % 3], NEG[:, i % 3], ACT.Exp), "act_step")
                    tell(f(NEG[:, i % 3], NEG[:, i % 3], ACT.Ln, bias=one_col[:, 0:1]), "neg_log")
                if i >= 2:
                    hd = i - 2
                    o = wait_filled(a, ("stick", hd))
                    if hd >= 3:
                        a.wait_ge(S("job_done"), jobs.index[("attend", (hd - 3) // 2)] + 1)
                    emptied(f(WA[:, hd % 3], o[:, 0:3 * P], ACT.Exp), ("stick", hd))
            a.wait_ge(S("dte_arg"), 1)
            tell(f(dtf[0:32, 4, 0:P], dtf[0:32, 4, 0:P], ACT.Exp), "dt_ready")
            o = wait_filled(a, ("small_turns",))
            emptied(f(SMALL.rearrange("p a b -> p (a b)"), o[:, 0:160], ACT.Copy), ("small_turns",))
            o = wait_filled(a, ("b_turn",))
            emptied(f(BTM, four(o), ACT.Copy), ("b_turn",))
            for g in range(4):
                o = wait_filled(a, ("state", g))
                emptied(f(S0[:, g], o, ACT.Copy), ("state", g))
            turn = 0
            prev_job = [0] + [jobs.index[("ssm_y", n // 4, n // 2 % 2, n % 2)] for n in range(16)]
            for g in range(4):
                for b in range(TB):
                    for half in range(2):
                        turn += 1
                        o = wait_filled(a, ("decay_rows", g, b, half))
                        a.wait_ge(S("decay_arg"), turn)
                        if b:
                            if turn > 2:
                                a.wait_ge(S("job_done"), prev_job[turn - 2] + 1)
                            tell(f(CE[:, turn % 2], four(o), ACT.Exp), "row_exp")
                        tell(f(DD[:, turn % 2], DD[:, turn % 2], ACT.Exp), "decay_exp")
            for g in range(4):
                a.wait_ge(S("gated"), g + 1)
                tell(f(SQ4[:, 4 * g:4 * g + 4], XBC[:, 4 * g:4 * g + 4], ACT.Square), "gy_sq")
            wait_emptied(a, ("group_norm", 2))
            tell(f(CBT.rearrange("p a b c -> p (a b c)"), CBT.rearrange("p a b c -> p (a b c)"), ACT.Sqrt), "gy_root")

            def gates2(p, it):
                bank = LP[(FIRST_PAIR["gates2"] + p) % 2]
                f(G2[:, 2 * it + p], bank, ACT.Sigmoid).then_inc(S("act_freed_pair"), 1)

            pair_loop("gates2", gates2)
            a.wait_ge(S("ssm_done"), 1)
            a.dma_start(flat(MX), mem_in).then_inc(S("in_mem"), 16)
            squares(5)
            squares(6)

            def mem_keys(p, it):
                bank = LP[(FIRST_PAIR["mem_k"] + p) % 2]
                f(KM.rearrange("p (a b) c -> p a (b c)", b=2)[:, 2 * it + p], bank, ACT.Copy)\
                    .then_inc(S("act_freed_pair"), 1)

            pair_loop("mem_k", mem_keys)
            squares(7)

            def xa_queries(p, it):
                bank = LP[(FIRST_PAIR["xq"] + p) % 2]
                f(XQ.rearrange("p (a b) c -> p a (b c)", b=2)[:, 2 * it + p], bank, ACT.Copy)\
                    .then_inc(S("act_freed_pair"), 1)

            pair_loop("xq", xa_queries)
            for hd in range(4):
                a.wait_ge(S("xa_max"), hd + 1)
                o = wait_filled(a, ("xa_scores", hd))
                for b in range(TB):
                    ins = f(XP[:, hd, b], o[:, b * T:b * T + T], ACT.Exp, scale=1.0 / 16,
                            bias=stat[:, 0, 2 * hd + b:2 * hd + b + 1])
                emptied(ins, ("xa_scores", hd))
            for hd in range(4):
                o = wait_filled(a, ("xa_turn", hd))
                emptied(f(flat(XT[:, hd % 2]), o, ACT.Copy), ("xa_turn", hd))
                o = wait_filled(a, ("xa_out", hd))
                emptied(f(flat(XO[:, 2 * hd:2 * hd + 2]), o, ACT.Copy), ("xa_out", hd))
            squares(8)
            squares(9, START["ffn3_up"])
            split_h(7)
            silus("ffn3_up", 2)
            squares(10)
            for c in range(4):
                a.wait_ge(S("x_ready"), 24 + c + 1)
                a.dma_start(out[:, c * 2 * T:(c + 1) * 2 * T], x2[:, c]).then_inc(S("stored"), 16)
            a.wait_ge(S("stored"), 64)

        @block.vector
        def _(v):
            def tt(o, i, j, op):
                return v.tensor_tensor(o, i, j, op)

            def ts(o, i, s1, op0, s2=None, op1=None):
                return v.tensor_scalar(o, i, s1, s2, op0) if op1 is None else v.tensor_scalar(o, i, s1, s2, op0, op1)

            def stt(o, i, s, j, op0, op1):
                return v.scalar_tensor_tensor(out=o, in0=i, scalar=s, in1=j, op0=op0, op1=op1)

            MUL, ADD, SUB, MAX, MIN = ALU.mult, ALU.add, ALU.subtract, ALU.max, ALU.min

            def step(ins):
                link(v, ins, "dve_step")

            def signal(name):
                v.sem_inc(S(name), 1)
                counts[name] += 1

            def signal_emptied(name):
                assert counts["dve_emptied"] == jobs.order[jobs.index[name]][2]
                signal("dve_emptied")

            def inverse_root(i):
                v.wait_ge(S("root_ready"), i + 1)
                link(v, v.reciprocal(rs, root), "root_read")

            def low_of_h(k):
                v.wait_ge(S("h_high"), counts["h_low"] + 1)
                tell(tt(H_LO[:, k], h[:, k], H_HI[:, k].bitcast(F32), SUB), "h_low")

            def norm(i, dst, src, sem, first_tile=None, split=False):
                if first_tile is not None:
                    make_low(v, first_tile)
                    make_low(v, first_tile + 1)
                inverse_root(i)
                for k in range(KD):
                    ins = stt(dst[:, k], src[:, k], param(NORMS[i], k), rs, MUL, MUL)
                    if sem == "h_ready" or k % 2:
                        tell(ins, sem)
                    if split and k >= 2:
                        low_of_h(k - 2)
                if split:
                    low_of_h(KD - 2)
                    low_of_h(KD - 1)

            def residual(name, scale):
                v.wait_ge(S("tile_used"), tiles_done(name))
                for c in range(4):
                    tell(stt(x2[:, c], ACC[c], scale, x2[:, c], MUL, ADD), "x_ready")
                v.wait_ge(S("x_ready"), counts["x_ready"])
                signal("acc_read")

            def post_norm(i):
                inverse_root(i)
                for c in range(4):
                    for k in (2 * c, 2 * c + 1):
                        ins = stt(h[:, k], ACC[c][:, (k % 2) * T:(k % 2) * T + T], param(NORMS[i], k), rs, MUL, MUL)
                        if k < KD - 1:
                            step(ins)
                    if c == 3:
                        tell(ins, "acc_read")
                        v.wait_ge(S("acc_read"), counts["acc_read"])
                    tell(tt(x2[:, c], x2[:, c], flat(h[:, 2 * c:2 * c + 2]), ADD), "x_ready")

            def ffn_mul(name, index):
                n0, fp = START[name], FIRST_PAIR[name]

                def low_of_act(j, it=None):
                    value = KF * index + j + 1
                    v.wait_ge(S("act_high"), value if it is None else value + 2 * it)
                    at = j if it is None else 2 * it + j
                    tt(ACT_LO[:, at], act_raw[:, j % 2], ACT_HI[:, at].bitcast(F32), SUB).then_inc(S("act_low"), 1)

                def one(j, it=None):
                    for n in (n0 + 2 * j + 2, n0 + 2 * j + 3):
                        make_low(v, n, it)
                    value = KF * index + j + 1
                    v.wait_ge(S("silu_ready"), value if it is None else value + 2 * it)
                    if j >= 2:
                        v.wait_ge(S("act_low"), value - 2 if it is None else value - 2 + 2 * it)
                    tt(act_raw[:, j % 2], gate_tmp[:, j % 2], LP[(fp + j) % 2][:, T:2 * T], MUL)\
                        .then_inc(S("dve_freed_pair"), 1)
                    if it is not None or j:
                        low_of_act(j - 1, it)

                one(0)
                one(1)
                with v.Fori(0, (KF - 2) // 2) as it:
                    one(2, it)
                    one(3, it)
                low_of_act(KF - 1)
                down = n0 + 2 * KF
                split_tiles(v, make_low, down + 2, down + KF + (0 if name == "ffn3_up" else 2))
                counts["dve_freed_pair"] += KF

            def ahead(name, j, it=None):
                for n in (START[name] + 2 * j + 2, START[name] + 2 * j + 3):
                    make_low(v, n, it)

            tell(v.memset(eps, EPS), "consts")
            tell(v.memset(one_col, 1.0), "consts")
            
            v.wait_ge(S("in_x"), 48)
            at_p, at_m, at_n = (PARAMS[n][0] for n in ("tap_prev", "tap_mid", "tap_next"))
            step(ts(c_mid[:, 0:16], par[:, at_p:at_p + 16], -1.0, MUL, 1.0, ADD))
            step(tt(c_mid[:, 0:16], c_mid[:, 0:16], par[:, at_n:at_n + 16], SUB))
            tell(v.tensor_copy(c_mid[:, 16:28], par[:, at_m + 16:at_m + 28]), "coefs")
            step(ts(c_ka, par[:, PARAMS["k_a"][0]:PARAMS["k_a"][0] + 4], -1.0, MUL, 1.0, ADD))
            step(ts(c_fb[0:64], par[0:64, PARAMS["sin_b"][0]:PARAMS["sin_b"][0] + 2], param("sin_f", 0, 64), MUL))
            v.wait_ge(S("coefs"), 1)
            signal("coefs")
            norm(0, h, x, "h_ready", START["ffn1_up"], True)
            v.wait_ge(S("c_a_exp"), 1)
            step(ts(c_a[0:32], c_a[0:32], -1.0, MUL))
            ffn_mul("ffn1_up", 0)
            residual("ffn1_down", 0.5)
            norm(1, h, x, "h_ready", None, True)

            def taps(p, it):
                bank = LP[(FIRST_PAIR["conv_in"] + p) % 2]
                v.wait_ge(S("mid_ready"), 2 * it + (p + 1))
                for half in range(2):
                    blk = 4 * it + (2 * p + half)
                    src = bank[:, half * T:half * T + T]
                    stt(U[:, blk, 1:T], src[:, 0:T - 1], par[:, bass.ds(blk + at_p, 1)], U[:, blk, 1:T], MUL, ADD)\
                        .then_inc(S("tap_step"), 1)
                v.wait_ge(S("tap_step"), 4 * it + (2 * p + 2))
                for half in range(2):
                    blk = 4 * it + (2 * p + half)
                    src = bank[:, half * T:half * T + T]
                    ins = stt(U[:, blk, 0:T - 1], src[:, 1:T], par[:, bass.ds(blk + at_n, 1)], U[:, blk, 0:T - 1], MUL, ADD)
                ins.then_inc(S("dve_freed_pair"), 1)

            with v.Fori(0, 6) as it:
                for p in range(2):
                    ahead("conv_in", p, it)
                    taps(p, it)
            ahead("conv_in", 12)
            taps(0, 6)
            taps(1, 6)
            counts["dve_freed_pair"] += 14
            v.wait_ge(S("dve_freed_pair"), counts["dve_freed_pair"])

            for q in range(KH):
                ins = ts(KK[:, q], U[:, 4 + q], param("k_k", q), MUL)
            tell(ins, "kk_raw")
            for half in range(2):
                o = wait_filled(v, ("key_norm", half))
                emptied(ts(flat(BON[:, 2 * half:2 * half + 2]), o, 1e-24, MAX), ("key_norm", half))
            v.wait_ge(S("kk_root"), 1)
            step(v.reciprocal(flat(BON), flat(BON)))
            step(tt(flat(KK), flat(KK), flat(BON), MUL))
            for d in range(2):
                def R(s):
                    return s[:, :, ::-1] if d else s

                def R4(s):
                    return R(s).rearrange("p q (b t) -> p q b t", b=TB)

                wait_emptied(v, ("rate_lora", d, 1))
                step(ts(flat(L), flat(L), LOG_DECAY, MUL))
                tell(v.tensor_tensor_scan(flat(C), table("keep32"), flat(L), 0.0, MUL, ADD), "cum_ready")
                v.wait_ge(S("cum_ready"), 2 * d + 1)
                tell(tt(flat(EX), flat(C), flat(L), SUB), "cum_ready")
                v.wait_ge(S("cum_ready"), 2 * d + 2)
                for q in range(KH):
                    ins = ts(L[:, q], A[:, q], param("k_a", q), MUL, c_ka[:, q:q + 1], ADD)
                step(ins)
                step(tt(L, L, R(U[:, 4:8]), MUL))
                if d:
                    step(tt(BON, BON, R(L), ADD))
                    for q in range(KH):
                        ins = stt(BON[:, q], U[:, q], param("r_k", q), BON[:, q], MUL, MUL)
                    step(ins)
                else:
                    step(v.tensor_copy(flat(BON), flat(L)))
                step(tt(A, A, R(KK), MUL))
                v.wait_ge(S("exps"), 3 * d + 3)
                for q in range(KH):
                    b2 = "p (b t) -> p b t"
                    kk_q, r_q = (KK[:, q, ::-1], U[:, q, ::-1]) if d else (KK[:, q, :], U[:, q, :])
                    tt(AR[:, q, :, 0, :], kk_q.rearrange(b2, b=TB), EX[:, q].rearrange(b2, b=TB), MUL)
                    tt(AR[:, q, :, 1, :], r_q.rearrange(b2, b=TB), EP[:, q].rearrange(b2, b=TB), MUL)
                v.tensor_copy(EEND.rearrange("p (a b) -> p a b", a=KH), EP[:, :, CH - 1:T:CH])
                tt(flat(KA), flat(L), flat(EN), MUL)
                step(tt(flat(BE), flat(A), flat(EN), MUL))
                ee = EEND.unsqueeze(2).broadcast_to([P, KH * NCH, CH])
                ch = "p (a b) -> p a b"
                tt(flat(BH).rearrange(ch, b=CH), flat(BE).rearrange(ch, b=CH), ee, MUL)
                tt(flat(KHAT).rearrange(ch, b=CH), flat(KA).rearrange(ch, b=CH), ee, MUL)
                tell(v.tensor_copy(RV, R(U[:, 8:12])), "dir_ready")
                v.wait_ge(S("dir_ready"), d + 1)
                for u in range(4):
                    for e in range(2):
                        for name, dst in (("beta_pairs", BX), ("kappa_pairs", KX)):
                            o = wait_filled(v, (name, d, u, e))
                            emptied(tt(dst[:, u, e::2].rearrange("p e a b -> p e (a b)"),
                                       o.rearrange("p (e a) -> p e a", e=2), over(table("upper"), 2), MUL),
                                    (name, d, u, e))
                    wait_emptied(v, ("kappa_pairs", d, u, 1))
                    tt(TT[:, u], BX[:, u, :, 0, :], over(level_t[:, 0], 4), MUL)
                    for e in range(2):
                        o = wait_filled(v, ("alpha_beta", d, u, e))
                        emptied(tt(TN[:, u, e::2], o[:, 0:T].rearrange("p (a b) -> p a b", a=2),
                                   over(table("level_n"), 2), MUL), ("alpha_beta", d, u, e))
                    wait_emptied(v, ("alpha_beta", d, u, 1))
                    tt(TT[:, u], TT[:, u], over(ident, 4), ADD)
                    tell(tt(TN[:, u], TN[:, u], over(ident, 4), ADD), "first_level")
                for level in range(2, 6):
                    for u in range(4):
                        if level < 5:
                            o = wait_filled(v, ("inverse", d, level, u))
                            emptied(tt(flat(TN[:, u]), flat(TN[:, u]), o, SUB), ("inverse", d, level, u))
                        o = wait_filled(v, ("inverse_t", d, level, u))
                        if level < 5:
                            emptied(tt(flat(TT[:, u]), flat(TT[:, u]), o, SUB), ("inverse_t", d, level, u))
                        else:
                            emptied(tt(flat(TT[:, u]), o, flat(TT[:, u]), SUB), ("inverse_t", d, level, u))
                ends = EEND.rearrange("p (a b) -> p a b", a=KH)
                for c in range(NCH):
                    b, r = c // 4, slice(CH * (c % 4), CH * (c % 4) + CH)
                    if c % 4 == 3:
                        wait_filled(v, ("chain", d, b, 1))
                    else:
                        v.wait_ge(S("sa_psum"), 6 * d + 3 * b + c % 4 + 1)
                    for e in range(2):
                        bank = MB[jobs.index[("chain", d, b, e)] % BANKS]
                        ins = v.tensor_copy(SA[r, b, e], bank[r, 0:T])
                    tell(ins, "sa_ready")
                    if c % 4 == 3:
                        v.wait_ge(S("sa_ready"), counts["sa_ready"])
                        for e in range(2):
                            signal_emptied(("chain", d, b, e))
                    if c == NCH - 1:
                        break
                    to = HS[:, c + 1].rearrange("p (a b) -> p a b", a=KH)
                    st = LP[c % 2][:, 0:KH * 64].rearrange("p (a b) -> p a b", a=KH)
                    if c:
                        fr = HS[:, c].rearrange("p (a b) -> p a b", a=KH)
                        step(tt(to, fr, ends[:, :, c:c + 1].broadcast_to([P, KH, 64]), MUL))
                        v.wait_ge(S("state_psum"), 7 * d + c + 1)
                        tell(tt(to, to, st, ADD), "state_ready")
                    else:
                        v.wait_ge(S("state_psum"), 7 * d + c + 1)
                        tell(v.tensor_copy(to, st), "state_ready")
                    v.wait_ge(S("state_ready"), counts["state_ready"])
                for pr in range(2):
                    o = wait_filled(v, ("y", d, pr)).rearrange("p (a b) -> p a b", a=2)
                    to = Y[:, 2 * pr:2 * pr + 2]
                    if d:
                        emptied(tt(to, to, o[:, :, ::-1], ADD), ("y", d, pr))
                    else:
                        emptied(v.tensor_copy(to, o), ("y", d, pr))
            for half in range(2):
                o = wait_filled(v, ("mean", half))
                yy = flat(Y[:, 2 * half:2 * half + 2])
                emptied(stt(yy, o, -1.0 / 64, yy, MUL, ADD), ("mean", half))
            for half in range(2):
                o = wait_filled(v, ("var", half))
                emptied(ts(flat(BE[:, 2 * half:2 * half + 2]), o, 1.0 / 64, MUL, GN_EPS, ADD), ("var", half))
            v.wait_ge(S("y_root"), 1)
            step(v.reciprocal(flat(BE), flat(BE)))
            step(tt(flat(Y), flat(Y), flat(BE), MUL))
            for q in range(KH):
                ins = ts(Y[:, q], Y[:, q], param("ln_w", q), MUL, param("ln_b", q), ADD)
            step(ins)
            for half in range(2):
                o = wait_filled(v, ("bonus", half))
                s2 = slice(2 * half, 2 * half + 2)
                emptied(tt(flat(L[:, s2]), o, flat(U[:, 8 + 2 * half:10 + 2 * half]), MUL), ("bonus", half))
            wait_emptied(v, ("bonus", 1))
            step(tt(flat(Y), flat(Y), flat(L), ADD))
            tell(tt(flat(Y), flat(Y), flat(G), MUL), "rwkv_done")
            v.wait_ge(S("rwkv_done"), 1)

            two_pi_hi = 6.28125
            two_pi_lo = 2 * math.pi - two_pi_hi
            for i in range(2):
                o = wait_filled(v, ("sin", i))
                if i:
                    v.wait_ge(S("sin_ready"), 1)
                emptied(ts(sin_in[0:64], o[0:64, 0:T], param("sin_f", 0, 64), MUL, c_fb[0:64, i:i + 1], ADD), ("sin", i))
                wait_emptied(v, ("sin", i))
                step(ts(sin_k[0:64], sin_in[0:64], 1 / (2 * math.pi), MUL, 12582912.0, ADD))
                step(ts(sin_k[0:64], sin_k[0:64], -12582912.0, ADD))
                step(stt(sin_in[0:64], sin_k[0:64], -two_pi_hi, sin_in[0:64], MUL, ADD))
                step(stt(sin_in[0:64], sin_k[0:64], -two_pi_lo, sin_in[0:64], MUL, ADD))
                if i == 0:
                    step(v.memset(sin_out[64:65, 1], 1.0))
                tell(ts(sin_in[0:64], sin_in[0:64], 3.1415925, MIN, -3.1415925, MAX), "sin_args")
            for b in range(TB):
                v.wait_ge(S("env_ready"), b + 1)
                for c in range(4):
                    o = wait_filled(v, ("filter", b, c))
                    emptied(tt(env[:, b, c], o, env[:, b, c], MUL), ("filter", b, c))
            wait_emptied(v, ("filter", 1, 3))
            for o_ in range(ORDERS):
                step(v.memset(env[0:1, 0, 2 + o_], 0.0))
            signal("filt_made")
            for o_ in range(ORDERS):
                for b in range(TB):
                    tell(tt(fsum[:, o_, b], env[:, b, o_], env[:, b, 2 + o_], ADD), "filt_sum")
                    tell(tt(fdiff[:, o_, b], env[:, b, o_], env[:, b, 2 + o_], SUB), "filt_sum")
            for o_ in range(ORDERS):
                v.wait_ge(S("filt_root"), o_ + 1)
                step(v.reciprocal(fnorm[:, o_], fnorm[:, o_]))
                signal_emptied(("filter_norm", o_))
                for m_ in range(NFREQ):
                    o = wait_filled(v, ("filter_dft", o_, m_))
                    emptied(tt(FK[:, o_, m_], o, fnorm[:, o_], MUL), ("filter_dft", o_, m_))
                wait_emptied(v, ("filter_dft", o_, 3))
                step(v.tensor_copy(FKP[:, o_], FK[:, o_, 0]))
                step(v.memset(FK[0:1, o_, 2], 0.0))
                o = wait_filled(v, ("nyquist", o_))
                emptied(tt(FKP[0:1, o_], o[0:1], fnorm[0:1, o_], MUL), ("nyquist", o_))
            wait_emptied(v, ("nyquist", 1))
            for o_ in range(ORDERS):
                for pr in range(2):
                    re, im = FK[:, o_, pr], FK[:, o_, 2 + pr]
                    re_im = FKP[:, o_] if pr == 0 else re
                    o = wait_filled(v, ("dft", o_, pr))
                    tt(ZF[:, 0], o, re, MUL)
                    emptied(tt(ZF[:, 1], o, im, MUL), ("dft", o_, pr))
                    o = wait_filled(v, ("dft", o_, 2 + pr))
                    tt(ZF[:, 2], o, im, MUL)
                    emptied(tt(ZF[:, 3], o, re_im, MUL), ("dft", o_, 2 + pr))
                    wait_emptied(v, ("dft", o_, 2 + pr))
                    tt(YF[:, pr], ZF[:, 0], ZF[:, 2], SUB)
                    tell(tt(YF[:, 2 + pr], ZF[:, 1], ZF[:, 3], ADD), "spectrum_ready")
                    v.wait_ge(S("spectrum_ready"), counts["spectrum_ready"])
                zin, dst, xg = (U[:, 24:28], Z1, U[:, 16:20]) if o_ == 0 else (Z1, Z2, U[:, 20:24])
                for half in range(2):
                    o = wait_filled(v, ("idft", o_, half))
                    for qq in range(2):
                        q = 2 * half + qq
                        step(stt(dst[:, q], zin[:, q], param("hy_d", 4 * o_ + q), o[:, qq * T:qq * T + T], MUL, ADD))
                    s2 = slice(2 * half, 2 * half + 2)
                    emptied(tt(flat(dst[:, s2]), flat(dst[:, s2]), flat(xg[:, s2]), MUL), ("idft", o_, half))
                    wait_emptied(v, ("idft", o_, half))
            m12 = M1.rearrange("p (a b) c -> p a (b c)", a=4)

            def gated(name, gate, prev, sem, free=True):
                v.wait_ge(S("tile_used"), tiles_done(name))
                for c in range(4):
                    ins = tt(gate[:, c], ACC[c], gate[:, c], MUL)
                tell(ins, "acc_read")
                v.wait_ge(S("acc_read"), counts["acc_read"])
                if prev is not None:
                    dst, other = prev
                    for c in range(4):
                        ins = tt(dst[:, c], gate[:, c], other[:, c], ADD)
                    tell(ins, sem)

            pair_freed(v, "gates", 7)
            gated("hy_out", GATE2[:, 0:4], None, None)
            gated("rw_out", GATE2[:, 4:8], (m12, GATE2[:, 0:4]), "merged")
            residual("w_out", 1.0)
            norm(2, h, x, "h_ready", START["ffn2_up"], True)
            ffn_mul("ffn2_up", 1)
            residual("ffn2_down", 0.5)
            norm(3, x, x, "x_ready")
            norm(4, h, x, "h_ready", None, True)

            at_w = PARAMS["conv_w"][0]

            def taps4(p, it):
                bank = LP[(FIRST_PAIR["xbc"] + p) % 2]
                v.wait_ge(S("mid2_ready"), 2 * it + (p + 1))
                for s in (1, 2, 3):
                    if s > 1:
                        v.wait_ge(S("tap4_step"), 4 * it + (2 * p + s - 1))
                    for half in range(2):
                        blk = 4 * it + (2 * p + half)
                        src = bank[:, half * T:half * T + T]
                        ins = stt(XBC[:, blk, s:T], src[:, 0:T - s], par[:, bass.ds(blk + (at_w + 24 * (3 - s)), 1)],
                                  XBC[:, blk, s:T], MUL, ADD)
                    ins.then_inc(S("tap4_step") if s < 3 else S("dve_freed_pair"), 1)

            with v.Fori(0, 6) as it:
                for p in range(2):
                    ahead("xbc", p, it)
                    taps4(p, it)
            counts["dve_freed_pair"] += 12
            make_low(v, START["dt"] + 2)
            v.wait_ge(S("tile_used"), tiles_done("dt"))
            bank = LP[FIRST_PAIR["dt"] % 2]
            r = slice(0, 32)
            tell(ts(dtf[r, 0], bank[r, 0:T], param("dt_bias", 0, 32), ADD), "dve_freed_pair")
            split_tiles(v, make_low, START["qk"] + 2, START["z"] + 2)
            v.wait_ge(S("tile_used"), tiles_done("v"))
            for b in range(TB):
                for half in range(2):
                    ins = v.tensor_copy(V2[:, b, half * HY:half * HY + HY], ACC[2 * b + half])
            tell(ins, "acc_read")
            split_tiles(v, make_low, START["z"] + 2, START["z"] + COUNT["z"])
            v.wait_ge(S("dve_freed_pair"), counts["dve_freed_pair"])
            tell(stt(dtf[r, 1], dtf[r, 0], -1.0, dtf[r, 0], MUL, MIN), "dt_neg")
            v.wait_ge(S("dt_log"), 1)
            step(stt(dtf[r, 0], dtf[r, 0], 0.0, dtf[r, 1], MAX, ADD))
            step(ts(dtf[r, 3], dtf[r, 0], c_a[r, 0:1], MUL))
            step(v.memset(dtf[r, 5], 1.0))
            step(v.memset(dtf[r, 5, 0:T:P], 0.0))
            step(v.tensor_tensor_scan(dtf[r, 2], dtf[r, 5], dtf[r, 3], 0.0, MUL, ADD))
            tell(ts(dtf[r, 4, 0:P], dtf[r, 2, 0:P], -1.0, MUL, dtf[r, 2, P - 1:P], ADD), "dte_arg")
            for i in range(16 + 3):
                if i < 16:
                    o = wait_filled(v, ("scores", i))
                    if i >= 3:
                        v.wait_ge(S("log_ready"), i - 2)
                    step(ts(SP[:, i % 3], o[:, 0:3 * P], 0.0, MAX))
                    tell(stt(NEG[:, i % 3], SP[:, i % 3], -2.0, o[:, 0:3 * P], MUL, ADD), "neg_abs")
                    v.wait_ge(S("neg_log"), i + 1)
                    emptied(tt(SP[:, i % 3], SP[:, i % 3], NEG[:, i % 3], ADD), ("scores", i))
                if i >= 3 and (i - 3) % 2 == 1:
                    q = (i - 3) // 2
                    o = wait_filled(v, ("attend", q))
                    emptied(v.tensor_copy(OT[:, q], o[:, 0:T]), ("attend", q))
            for g0 in range(0, 4, 2):
                o = wait_filled(v, ("cb", g0))
                emptied(tt(CBT[:, g0:g0 + 2].rearrange("p a b c -> p (a b) c"), four(o), over(table("until"), 4), MUL),
                        ("cb", g0))
            wait_emptied(v, ("small_turns",))
            for b in range(TB):
                for c in range(4):
                    o = wait_filled(v, ("x_turn", b, c))
                    emptied(tt(XTM[:, b, c * HY:c * HY + HY].rearrange("p (a b) -> p a b", b=64),
                               o.rearrange("p (a b) -> p a b", b=64), along(SMALL[:, 2 + b, 8 * c:8 * c + 8], 64), MUL),
                            ("x_turn", b, c))
            wait_emptied(v, ("x_turn", 1, 3))
            tell(tt(XD.rearrange("p (a b) -> p a b", b=64), XTM[:, 0].rearrange("p (a b) -> p a b", b=64),
                    along(SMALL[:, 4], 64), MUL), "xd_ready")
            turn = 0
            for g in range(4):
                for b in range(TB):
                    for half in range(2):
                        turn += 1
                        o = wait_filled(v, ("decay_rows", g, b, half))
                        for i in range(4):
                            hd = 8 * g + 4 * half + i
                            ins = ts(DD[:, turn % 2, i], o[:, i * P:i * P + P], SMALL[:, b, hd:hd + 1], SUB, 0.0, MIN)
                        tell(ins, "decay_arg")
                        if b:
                            v.wait_ge(S("row_exp"), 2 * g + half + 1)
                            step(tt(CE[:, turn % 2], CE[:, turn % 2], over(XBC[:, 20 + g, P:T], 4), MUL))
                            signal_emptied(("decay_rows", g, b, half))
                        else:
                            v.wait_ge(S("decay_arg"), turn)
                            signal_emptied(("decay_rows", g, b, half))
                        v.wait_ge(S("decay_exp"), turn)
                        tell(tt(DM[:, turn % 2], DD[:, turn % 2], over(CBT[:, g, b], 4), MUL), "ssm_mix_ready")
                        o = wait_filled(v, ("ssm_y", g, b, half))
                        for qq in range(2):
                            q = 4 * g + 2 * half + qq
                            yy = XBC[:, q, b * P:b * P + P]
                            ins = stt(yy, yy, param("d_skip", q), o[:, qq * P:qq * P + P], MUL, ADD)
                        emptied(ins, ("ssm_y", g, b, half))
                wait_emptied(v, ("ssm_y", g, 1, 1))
                tell(tt(flat(XBC[:, 4 * g:4 * g + 4]), flat(XBC[:, 4 * g:4 * g + 4]), flat(Z[:, 4 * g:4 * g + 4]), MUL), "gated")
            cbt4 = CBT.rearrange("p a b c -> p a (b c)")
            for g0 in range(0, 4, 2):
                o = wait_filled(v, ("group_norm", g0))
                emptied(ts(flat(cbt4[:, g0:g0 + 2]), o, 1.0 / 512, MUL, EPS, ADD), ("group_norm", g0))
            v.wait_ge(S("gy_root"), 1)
            step(v.reciprocal(flat(cbt4), flat(cbt4)))
            for q in range(16):
                ins = stt(XBC[:, q], XBC[:, q], param("g_ssm", q), cbt4[:, q // 4], MUL, MUL)
            tell(ins, "ssm_done")
            pair_freed(v, "gates2", 7)
            gated("br_att", G2[:, 0:4], None, None)
            gated("br_ssm", G2[:, 4:8], (M2.rearrange("p (a b) c -> p a (b c)", a=4), G2[:, 0:4]), "merged")
            post_norm(5)

            v.wait_ge(S("in_mem"), 16)
            norm(6, HM, MX, "h_ready")
            v.wait_ge(S("tile_used"), tiles_done("mem_v"))
            for b in range(TB):
                for half in range(2):
                    ins = v.tensor_copy(VM[:, b, half * HY:half * HY + HY], ACC[2 * b + half])
            tell(ins, "acc_read")
            norm(7, h, x, "h_ready")
            for hd in range(4):
                o = wait_filled(v, ("xa_scores", hd))
                s2 = slice(2 * hd, 2 * hd + 2)
                step(v.tensor_reduce(stat[:, 1, s2], o.rearrange("p (a b) -> p a b", a=2), AX.X, MAX))
                tell(ts(stat[:, 0, s2], stat[:, 1, s2], -1.0 / 16, MUL), "xa_max")
            for hd in range(4):
                s2 = slice(2 * hd, 2 * hd + 2)
                wait_emptied(v, ("xa_scores", hd))
                step(v.tensor_reduce(stat[:, 1, s2], XP[:, hd], AX.X, ADD))
                step(v.reciprocal(stat[:, 2, s2], stat[:, 1, s2]))
                tell(tt(XP[:, hd], XP[:, hd], along(stat[:, 2, s2], T), MUL), "xa_probs")
            post_norm(8)
            norm(9, h, x, "h_ready", START["ffn3_up"], True)
            ffn_mul("ffn3_up", 2)
            post_norm(10)

        @block.gpsimd
        def _(g_):
            def high_of_act(name, index):
                base = PAIR_OWNER[FIRST_PAIR[name]][1]
                with g_.Fori(0, KF // 2) as it:
                    for p in range(2):
                        g_.wait_ge(S("dve_freed_pair"), 2 * it + (base + p + 1))
                        g_.tensor_copy(ACT_HI[:, 2 * it + p], act_raw[:, p]).then_inc(S("act_high"), 1)

            high_of_act("ffn1_up", 0)
            for d in range(2):
                for level in range(2, 6):
                    for u in range(4):
                        wait_emptied(g_, ("kappa_pairs", d, u, 1))
                        if level > 2 or u >= 2:
                            prev = ("product", d, level, u - 2) if u >= 2 else ("product", d, level - 1, u + 2)
                            g_.wait_ge(S("job_done"), jobs.index[prev] + 1)
                        else:
                            g_.wait_ge(S("job_done"), jobs.index[("kappa", d, 1)] + 1)
                        tell(g_.tensor_tensor(BT[:, u % 2], BX[:, u, :, 0, :], over(level_t[:, level - 1], 4), ALU.mult),
                             "off_diagonal")
            high_of_act("ffn2_up", 1)
            for hd in range(16):
                def weights(n):
                    wait_emptied(g_, ("stick", n))
                    tell(g_.tensor_tensor(WA[:, n % 3], WA[:, n % 3], table("causal"), ALU.mult), "stick_weights")

                wait_emptied(g_, ("scores", hd))
                if hd >= 3:
                    g_.wait_ge(S("job_done"), jobs.index[("stick", hd - 3)] + 1)
                tell(g_.tensor_tensor(LM[:, hd % 3], SP[:, hd % 3], table("neg_causal"), ALU.mult), "log_ready")
                if hd >= 2:
                    weights(hd - 2)
            weights(14)
            weights(15)
            high_of_act("ffn3_up", 2)


def blocks(m, rows=P):
    return m.reshape(m.shape[0] // P, P, m.shape[1] // P, P).transpose(0, 2, 1, 3)


def weight_stream(i):
    def pad(m, cols):
        return np.concatenate([m, np.zeros((m.shape[0], cols - m.shape[1]), m.dtype)], 1)

    def by_output(m):
        b = blocks(m)
        return b.transpose(1, 2, 0, 3).reshape(b.shape[1], P, D)

    def by_input(m):
        return m.reshape(m.shape[0] // P, P, D)

    def up(m):
        t = by_output(m)
        return np.stack([t[:KF], t[KF:]], 1).reshape(2 * KF, P, D)

    w1, w2 = i["w_in"], i["w_in_2"][0]
    hy, rw = 3 * HY, 3 * HY + 256 + 160
    rwkv = pad(w1[:, hy:hy + rw], 16 * P)
    at = np.cumsum([0, D, D, D, 2 * D, 3 * D, 32, D, D])
    q, k, v, z, xbc, dt, ga, gs = (w2[:, at[n]:at[n + 1]] for n in range(8))
    parts = {
        "ffn1_up": up(i["ffn1_w_gu"]), "ffn1_down": by_input(i["ffn1_w_down"]),
        "conv_in": np.concatenate([by_output(rwkv), by_output(w1[:, :hy])]), "gates": by_output(w1[:, hy + rw:]),
        "hy_out": by_input(i["hy_out"]), "rw_out": by_input(i["rw_out"]), "w_out": by_input(i["w_out"]),
        "ffn2_up": up(i["ffn2_w_gu"]), "ffn2_down": by_input(i["ffn2_w_down"]),
        "xbc": by_output(xbc), "dt": by_output(pad(dt, P)), "qk": np.concatenate([by_output(q), by_output(k)]),
        "v": by_input(v), "z": by_output(z), "gates2": np.concatenate([by_output(ga), by_output(gs)]),
        "br_att": by_input(i["w_br_att_2"][0]), "br_ssm": by_input(i["w_br_ssm_2"][0]),
        "mix_out": by_input(i["w_mix_out_2"][0]),
        "mem_k": by_output(i["w_xkv_2"][0][:, :D]), "mem_v": by_input(i["w_xkv_2"][0][:, D:]),
        "xq": by_output(i["w_xq_2"][0]), "xo": by_input(i["w_xo_2"][0]),
        "ffn3_up": up(i["w_gu_2"][0]), "ffn3_down": by_input(i["w_down_2"][0]),
    }
    for name, tiles, _ in SEGMENTS:
        assert parts[name].shape == (tiles, P, D), name
    return np.concatenate([parts[name] for name, _, _ in SEGMENTS])


def parameters(i):
    def cols(v):
        return np.reshape(v, (-1, P)).T

    def rows(v):
        v = np.reshape(v, (-1, v.shape[-1])).T
        return np.concatenate([v, np.zeros((P - v.shape[0], v.shape[1]), v.dtype)])

    mu = np.concatenate([i["rw_mu"], np.zeros((2, 16 * P - i["rw_mu"].shape[1]), np.float32)], 1)
    taps = i["hy_conv_w"]
    zero = np.zeros((P, 16), np.float32)
    p = {n: cols(i[n]) for n in ("ffn1_norm", "mix_norm", "ffn2_norm", "final_norm")}
    p |= {n: cols(i[n + "_2"]) for n in ("g_pre_mix", "g_post_mix", "g_pre_xa", "g_mem", "g_post_xa", "g_pre_ffn",
                                         "g_post_ffn", "conv_w", "conv_b")}
    p["tap_prev"] = np.concatenate([cols(mu[0]), cols(taps[0])], 1)
    p["tap_mid"] = np.concatenate([zero, cols(taps[1])], 1)
    p["tap_next"] = np.concatenate([cols(mu[1]), cols(taps[2])], 1)
    p["tap_bias"] = np.concatenate([zero, cols(i["hy_conv_b"])], 1)
    p |= {"hy_d": cols(i["hy_bias_d"]), "w0": cols(i["rw_w0"]), "a0": cols(i["rw_a0"]), "k_k": cols(i["rw_k_k"]),
          "k_a": cols(i["rw_k_a"]), "r_k": cols(i["rw_r_k"]), "ln_w": cols(i["rw_ln_w"]), "ln_b": cols(i["rw_ln_b"]),
          "g_ssm": cols(i["g_ssm_norm_2"]), "d_skip": cols(np.repeat(i["d_skip_2"][0], 64)),
          "sin_b": rows(np.stack([i["hy_ffn_b1"], i["hy_ffn_b2"]])), "sin_f": rows(i["hy_sin_freq"]),
          "dt_bias": rows(i["dt_bias_2"][0]), "a_log": rows(i["a_log_2"][0])}
    for name, (_, n) in PARAMS.items():
        assert p[name].shape == (P, n), (name, p[name].shape)
    return np.concatenate([p[name] for name in PARAMS], 1)


def small_matrices(i):
    g2 = i["rw_g2"]
    g2b = np.concatenate([g2[P:], np.zeros((2 * P - g2.shape[0], HY), g2.dtype)])
    lora = np.concatenate([i["rw_w2"].reshape(P, HY), i["rw_a2"].reshape(P, HY), g2[:P], g2b], 1)

    def pad(m):
        return np.concatenate([m, np.zeros((P - m.shape[0], m.shape[1]), m.dtype)])

    w3 = np.concatenate([i["hy_ffn_w3"], i["hy_ffn_b3"][None]])
    return lora, np.concatenate([pad(i["hy_ffn_w1"]), pad(i["hy_ffn_w2"]), pad(w3)], 1)


def kernel(**inputs):
    import concourse.bacc as _bacc
    from concourse.bass_utils import run_bass_kernel_spmd as _run

    i = {k: np.asarray(v) for k, v in inputs.items()}
    lora, filt = small_matrices(i)
    arrays = {
        "weights": weight_stream(i), "params": parameters(i), "tables": tables(),
        "x_t": i["x"][0].T.reshape(KD, P, T).transpose(1, 0, 2).reshape(P, KD * T),
        "mem_t": i["mem_2"][0].T.reshape(KD, P, T).transpose(1, 0, 2).reshape(P, KD * T),
        "lora": lora, "filt": filt, "decay": i["hy_decay"].reshape(4 * HY),
    }
    arrays = {k: np.ascontiguousarray(v) for k, v in arrays.items()}
    nc = _bacc.Bacc("TRN2", target_bir_lowering=False, num_devices=1)
    args = [nc.dram_tensor(k, a.shape, F32, kind="ExternalInput").ap() for k, a in arrays.items()]
    out = nc.dram_tensor("out_t", (P, KD * T), F32, kind="ExternalOutput").ap()
    build_program(nc, *args, out)
    got = _run(nc, [arrays], core_ids=[0]).results[0]["out_t"]
    return got.reshape(P, KD, T).transpose(2, 1, 0).reshape(1, T, D)
```

```python
import math
from contextlib import ExitStack

import numpy as np

import concourse.bass as bass
from concourse import mybir

F32 = mybir.dt.float32
F32R = mybir.dt.float32r
ALU = mybir.AluOpType
ACT = mybir.ActivationFunctionType
AX = mybir.AxisListType

P = 128
T = 256
TB = T // P
D = 1024
KD = D // P
FF = 2816
KF = FF // P
EPS = 1e-6
GN_EPS = 64e-5
LOG_DECAY = -math.exp(-0.5)
HY = 512
KH = HY // P
CH = 32
NCH = T // CH
ORDERS = 2
NFREQ = 2 * T // P
RING = 4
BANKS = 5

SEGMENTS = [
    ("ffn1_up", 2 * KF, "m"), ("ffn1_down", KF, "k"),
    ("conv_in", 16, "m"),
    ("gates_a", 6, "m"), ("hyena_a", 6, "m"), ("gates_b", 2, "m"), ("hyena_b", 6, "m"), ("gates_c", 8, "m"),
    ("rw_out", KH, "k"), ("hy_out", KH, "k"), ("w_out", KD, "k"),
    ("ffn2_up", 2 * KF, "m"), ("ffn2_down", KF, "k"),
    ("xbc", 24, "m"), ("dt", 1, "m"), ("qk", 16, "m"), ("v", KD, "k"), ("z", 16, "m"), ("gates2", 16, "m"),
    ("br_att", KD, "k"), ("br_ssm", 16, "k"), ("mem_k0", 4, "m"), ("mix_out", KD, "k"),
    ("mem_k1", 4, "m"), ("mem_v", KD, "k"), ("xq", KD, "m"), ("xo", KD, "k"), ("ffn3_up", 2 * KF, "m"), ("ffn3_down", KF, "k"),
]
SPLIT = {"ffn1_up", "ffn1_down", "conv_in", "rw_out", "hy_out", "w_out", "ffn2_up", "ffn2_down", "xbc", "dt", "qk", "v", "z", "br_ssm",
         "mem_k0", "mix_out", "mem_k1", "mem_v", "xq", "xo", "ffn3_up", "ffn3_down"}
LAST_READER = {"qk": "act", "z": "act", "gates2": "act", "mem_k0": "act",
               "mem_k1": "act", "xq": "act"}

FILLERS = {"gates_a", "hyena_a", "gates_b", "hyena_b", "gates_c"}
START, COUNT, FIRST_PAIR, PAIRS = {}, {}, {}, {}
PAIR_OWNER = []
_n = 0
_freed = {"dve": 0, "act": 0}
for _name, _tiles, _form in SEGMENTS:
    START[_name], COUNT[_name] = _n, _tiles
    _n += _tiles
    if _form == "m" and _name not in FILLERS:
        FIRST_PAIR[_name], PAIRS[_name] = len(PAIR_OWNER), (_tiles + 1) // 2
        for _ in range(PAIRS[_name]):
            _e = LAST_READER.get(_name, "dve")
            PAIR_OWNER.append((_e, _freed[_e]))
            _freed[_e] += 1
TILES = _n
RUNS, SPLIT_RANK = [], []
for _name, _tiles, _form in SEGMENTS:
    _split = _name in SPLIT
    for _ in range(_tiles):
        SPLIT_RANK.append(SPLIT_RANK[-1] + _was_split if SPLIT_RANK else 0)
        _was_split = int(_split)
    if RUNS and RUNS[-1][2] == _split:
        RUNS[-1] = (RUNS[-1][0], START[_name] + _tiles, _split)
    else:
        RUNS.append((START[_name], START[_name] + _tiles, _split))
RUN_STARTS = {_first for _first, _, _split in RUNS if _split}

PARAMS = {}
_n = 0
for _name, _cols in [
    ("ffn1_norm", KD), ("mix_norm", KD), ("ffn2_norm", KD), ("final_norm", KD), ("g_pre_mix", KD),
    ("g_post_mix", KD), ("g_pre_xa", KD), ("g_mem", KD), ("g_post_xa", KD), ("g_pre_ffn", KD), ("g_post_ffn", KD),
    ("tap_prev", 28), ("tap_mid", 28), ("tap_next", 28), ("tap_bias", 28),
    ("hy_d", 8), ("w0", 8), ("a0", 8), ("k_k", 4), ("k_a", 4), ("r_k", 4), ("ln_w", 4), ("ln_b", 4),
    ("conv_w", 96), ("conv_b", 24), ("g_ssm", 16), ("d_skip", 16),
    ("sin_b", 2), ("sin_f", 1), ("dt_bias", 1), ("a_log", 1),
]:
    PARAMS[_name] = (_n, _cols)
    _n += _cols
NPARAMS = _n

TABLES = {}
_n = 0
for _name, _cols in [
    ("ident", P), ("ones", P), ("head_ones", P), ("upper", 2 * P), ("level_n", P), ("level_t", 5 * P),
    ("causal", 3 * P), ("neg_causal", 3 * P), ("tri", P), ("until", P), ("keep32", 2 * HY),
    ("minus_t", TB), ("dft", TB * 2 * T), ("idft", NFREQ * T), ("feats", T),
]:
    TABLES[_name] = (_n, _cols)
    _n += _cols
NTABLES = _n
EMB = 33


def tables():
    t = {}
    i = np.arange(P)
    t["ident"] = np.eye(P)
    t["ones"] = np.ones((P, P))
    t["head_ones"] = (i[:, None] // 64 == i[None] // 64).astype(float)
    same = i[:, None] // CH == i[None] // CH
    strict = same & (i[:, None] < i[None])
    t["upper"] = np.concatenate([strict, same & (i[:, None] <= i[None])], 1)
    levels = []
    for l in range(1, 6):
        n = 1 << l
        levels.append((i[:, None] // n == i[None] // n) & (i[:, None] // (n // 2) < i[None] // (n // 2)))
    t["level_t"] = np.concatenate([-levels[0].astype(float)] + [x.astype(float) for x in levels[1:]], 1)
    t["level_n"] = -levels[0].T.astype(float)
    before = (i[:, None] < i[None]).astype(float)
    t["causal"] = np.concatenate([before, np.ones((P, P)), before], 1)
    t["neg_causal"] = -t["causal"]
    t["tri"] = (i[:, None] >= i[None]).astype(float)
    t["until"] = (i[:, None] <= i[None]).astype(float)
    t["keep32"] = np.tile((np.arange(2 * HY) % CH != 0).astype(float), (P, 1))
    n = np.arange(T)[:, None].astype(float)
    f = np.arange(T)[None].astype(float)
    angle = 2 * np.pi * ((n * f) % (2 * T)) / (2 * T)
    re, im = np.cos(angle), -np.sin(angle)
    im[:, 0] = (-1.0) ** np.arange(T)
    dft = np.concatenate([re, im], 1)
    t["dft"] = dft.reshape(TB, P, 2 * T).transpose(1, 0, 2).reshape(P, -1)
    scale = np.full((2 * T, 1), 2.0)
    scale[0] = scale[T] = 1.0
    idft = dft.T * scale / (2 * T)
    t["idft"] = idft.reshape(NFREQ, P, T).transpose(1, 0, 2).reshape(P, -1)
    pos = np.arange(T, dtype=np.float32)
    tt = pos / np.float32(T - 1)
    t["minus_t"] = -tt.reshape(TB, P).T
    ang = (np.float32(2.0 * math.pi / T) * pos)[:, None].astype(np.float64)
    bands = np.linspace(1e-4, 15, 16, dtype=np.float32)[None].astype(np.float64)
    feats = np.concatenate([tt[:, None], np.cos(bands * ang), -np.sin(bands * ang)], 1)
    fp = np.zeros((P, T))
    fp[:EMB] = feats.T
    t["feats"] = fp
    out = np.zeros((P, NTABLES), np.float32)
    for name, (at, cols) in TABLES.items():
        out[:, at:at + cols] = t[name]
    return out


class Jobs:

    def __init__(self):
        self.index, self.engine, self.order = {}, [], []
        self.emptied = {"dve": 0, "act": 0}

    def add(self, name, engine):
        self.index[name] = len(self.order)
        self.order.append((name, engine, self.emptied[engine]))
        self.emptied[engine] += 1


GATE_TILES = [START[_name] + _i for _name in ("gates_a", "gates_b", "gates_c") for _i in range(COUNT[_name])]
HYENA_TILES = [START[_name] + _i for _name in ("hyena_a", "hyena_b") for _i in range(COUNT[_name])]

TURN = [(g, b, half) for g in range(4) for b in range(TB) for half in range(2)]
TURNS = len(TURN)


def plan_jobs():
    jobs = Jobs()
    add = jobs.add
    for half in range(2):
        add(("gate_lora", half), "act")
    for half in range(2):
        add(("key_norm", half), "dve")

    def loras(d):
        for what in ("decay_lora", "rate_lora"):
            for half in range(2):
                add((what, d, half), "act")

    def turns(d, what):
        for b in range(TB):
            add((what, d, b), "act")

    loras(0)
    for d in range(2):
        turns(d, "v")
        turns(d, "alpha")
        for u in range(4):
            for e in range(2):
                add(("beta_pairs", d, u, e), "dve")
                add(("kappa_pairs", d, u, e), "dve")
            for e in range(2):
                add(("alpha_beta", d, u, e), "dve")
        turns(d, "beta")
        turns(d, "kappa")
        for level in range(2, 6):
            add(("product", d, level, 0), "act")
            add(("product", d, level, 1), "act")
            for u in range(4):
                if level < 5:
                    add(("inverse", d, level, u), "dve")
                add(("inverse_t", d, level, u), "dve")
                if u + 2 < 4:
                    add(("product", d, level, u + 2), "act")
        for b in range(TB):
            add(("alpha_v", d, b), "act")
            add(("w_t", d, b), "act")
        if d == 0:
            loras(1)
        for b in range(TB):
            for e in range(2):
                add(("chain", d, b, e), "dve")
        for pair in range(2):
            add(("y", d, pair), "dve")
    for half in range(2):
        add(("mean", half), "dve")
    for half in range(2):
        add(("var", half), "dve")
    for half in range(2):
        add(("bonus", half), "dve")
    add(("sin", 0), "dve")
    add(("sin", 1), "dve")
    for b in range(TB):
        for c in range(4):
            add(("filter", b, c), "dve")
    for o in range(ORDERS):
        add(("filter_norm", o), "dve")
        for m in range(NFREQ):
            add(("filter_dft", o, m), "dve")
        add(("nyquist", o), "dve")
    for o in range(ORDERS):
        for b in range(TB):
            add(("turn", o, b), "act")
        for m in (0, 2, 1, 3):
            add(("dft", o, m), "dve")
        for half in range(2):
            add(("idft", o, half), "dve")
    for n in range(8 + 2):
        for hd in (2 * n, 2 * n + 1):
            if n < 8:
                add(("scores", hd), "dve")
        for hd in (2 * n - 2, 2 * n - 1):
            if 1 <= n < 9:
                add(("stick", hd), "act")
        if n >= 2:
            add(("attend", n - 2), "dve")
    add(("small_turns",), "act")
    add(("b_turn",), "act")
    for g in range(0, 4, 2):
        add(("cb", g), "dve")
    for b in range(TB):
        for c in range(4):
            add(("x_turn", b, c), "dve")
    for g in range(4):
        add(("state", g), "act")
    add(("decay_rows", 0), "dve")
    for t in range(TURNS):
        if t:
            add(("ssm_y", t - 1), "dve")
        if t + 1 < TURNS:
            add(("decay_rows", t + 1), "dve")
    add(("ssm_y", TURNS - 1), "dve")
    for g in range(0, 4, 2):
        add(("group_norm", g), "dve")
    for h in range(4):
        add(("xa_scores", h), "act")
    for h in range(4):
        add(("xa_turn", h), "act")
        add(("xa_out", h), "act")
    return jobs


def build_program(nc, w, params_in, tables_in, x_in, mem_in, lora_in, filt_in, decay_in, out):
    jobs = plan_jobs()
    counts = {}
    with ExitStack() as ctx:
        sems = {}

        def S(name):
            if name not in sems:
                sems[name] = ctx.enter_context(nc.semaphore(name))
                counts[name] = 0
            return sems[name]

        for name in ("tile_used", "job_done", "dve_emptied", "act_emptied", "dve_freed_pair", "act_freed_pair",
                     "acc_read", "x_ready", "sq_ready", "ssq_done", "root_ready", "h_ready", "silu_ready",
                     "high_ready", "low_ready", "h_high", "h_low", "act_high", "act_low", "block_high",
                     "block_low",
                     "dve_step", "act_step", "pool_step"):
            S(name)
        landed = [ctx.enter_context(nc.semaphore(f"landed{s}")) for s in range(RING)]

        words = 53208
        base_words = NPARAMS + TABLES["dft"][0] + 2 * KD * T + RING * KD * P + 2 * T + 4 * HY + 2 * T + 28 + 2 + 4 + 3
        base_words += base_words % 2
        base = ctx.enter_context(nc.sbuf_tensor("base", [P, base_words], F32))
        with nc.sbuf_tensor("stages", [P, words - base_words], F32) as stages:
            pass
        split_words = 2 * (KF * T + KD * T + RING * KD * P)
        ctx.enter_context(nc.sbuf_tensor("below_split", [P, words - base_words - split_words], F32))
        act_parts = ctx.enter_context(nc.sbuf_tensor("act_parts", [P, 2 * KF * T], F32R))
        h_parts = ctx.enter_context(nc.sbuf_tensor("h_parts", [P, 2 * KD * T], F32R))
        ring_parts = ctx.enter_context(nc.sbuf_tensor("ring_parts", [P, 2 * RING * KD * P], F32R))
        ACT_HI, ACT_LO = (act_parts[:, i * KF * T:(i + 1) * KF * T].rearrange("p (a b) -> p a b", a=KF) for i in range(2))
        H_HI, H_LO = (h_parts[:, i * KD * T:(i + 1) * KD * T].rearrange("p (a b) -> p a b", a=KD) for i in range(2))
        W_HI, W_LO = (ring_parts[:, i * RING * KD * P:(i + 1) * RING * KD * P]
                      .rearrange("p (a b c) -> p a b c", a=RING, b=KD) for i in range(2))
        top = [0]

        def cut(cols, *shape):
            if top[0] < base_words:
                assert top[0] + cols <= base_words
                a = base[:, top[0]:top[0] + cols]
            else:
                a = stages[:, top[0] - base_words:top[0] - base_words + cols]
            top[0] += cols
            assert top[0] <= words, top[0]
            if len(shape) == 2:
                a = a.rearrange("p (a b) -> p a b", a=shape[0], b=shape[1])
            if len(shape) == 3:
                a = a.rearrange("p (a b c) -> p a b c", a=shape[0], b=shape[1], c=shape[2])
            if len(shape) == 4:
                a = a.rearrange("p (a b c d) -> p a b c d", a=shape[0], b=shape[1], c=shape[2], d=shape[3])
            return a

        par = cut(NPARAMS)
        tab_split = TABLES["dft"][0]
        tab = cut(tab_split)
        x = cut(KD * T, KD, T)
        h = cut(KD * T, KD, T)
        ring = cut(RING * KD * P, RING, KD, P)
        root = cut(T)
        rs = cut(T)
        lora = cut(4 * HY, 4, HY)
        gate_tmp = cut(2 * T, 2, T)
        c_mid = cut(28)
        c_fb = cut(2)
        c_ka = cut(4)
        c_a = cut(1)
        eps = cut(1)
        one_col = cut(1)
        assert base_words - top[0] in (0, 1)
        top[0] = free_from = base_words
        act_raw = cut(KF * T, KF, T)[:, 0:2]
        sq = cut(KD * T, KD, T)
        sq2 = sq.rearrange("p (a b) c -> p a (b c)", a=4)
        x2 = x.rearrange("p (a b) c -> p a (b c)", a=4)

        def param(name, i=0, rows=P):
            at, cols = PARAMS[name]
            assert i < cols
            return par[0:rows, at + i:at + i + 1]

        def table(name, rows=P):
            at, cols = TABLES[name]
            return tab[0:rows, at:at + cols]

        ident, ones, head_ones = table("ident"), table("ones"), table("head_ones")
        upper = table("upper").rearrange("p (a b) -> p a b", a=2)
        level_t = table("level_t").rearrange("p (a b) -> p a b", a=5)

        gates_dram = nc.dram_tensor("gates_dram", (P, 8, 2 * T), F32, kind="Internal").ap()
        psum = ctx.enter_context(nc.psum_tensor("psum", [P, 8, 512], F32))
        LP = [psum[:, i, :] for i in range(2)]
        MB = [psum[:, 2 + i, :] for i in range(BANKS)]
        ACC = [psum[:, 2 + i, :] for i in range(4)]
        GB = psum[:, 7, :]
        GATE_BANK = [GB, LP[0], LP[1], GB, LP[0], LP[1], GB, LP[0]]
        SS = psum[:, 7, 0:T]

        top[0] = free_from
        U = cut(28 * T, 28, T)
        G = cut(KH * T, KH, T)
        KK = cut(KH * T, KH, T)
        BON = cut(KH * T, KH, T)
        Y = cut(KH * T, KH, T)
        rwkv_from = top[0]
        L = cut(KH * T, KH, T)
        A = cut(KH * T, KH, T)
        AR = cut(2 * KH * T, KH, TB, 2, P)
        BE = cut(KH * T, KH, T)
        KA = cut(KH * T, KH, T)
        hat_from = top[0]
        BH = cut(KH * T, KH, T)
        KHAT = cut(KH * T, KH, T)
        hat_to = top[0]
        TM = {n: cut(TB * HY, TB, HY) for n in ("v", "alpha", "beta", "kappa")}
        BX = cut(4 * 4 * 2 * P, 4, 4, 2, P)
        KX = cut(4 * 4 * 2 * P, 4, 4, 2, P)
        WT = cut(KH * T, KH, T)
        AV = cut(TB * HY, TB, HY)
        EEND = cut(KH * NCH)
        tr_from = top[0]
        RV = cut(KH * T, KH, T)
        C = BE
        EP, EX, EN = C, KA, BH
        top[0] = tr_from
        TN = cut(4 * HY, 4, 4, P)
        TT = cut(4 * HY, 4, 4, P)
        rwkv_top = top[0]
        top[0] = hat_from
        BT = cut(2 * HY, 2, 4, P)
        PR = cut(2 * HY, 2, 4, P)
        assert top[0] <= hat_to
        top[0] = tr_from
        HS = cut((NCH + 1) * KH * 64, NCH + 1, KH * 64)
        SA = cut(TB * HY, TB, 2, HY // 2)
        assert top[0] <= rwkv_top
        top[0] = rwkv_from
        FK = cut(2 * NFREQ * HY, ORDERS, NFREQ, HY)
        FKP = cut(2 * HY, ORDERS, HY)
        sin_in = cut(T)
        sin_k = cut(T)
        sin_out = cut(2 * T, 2, T)
        assert top[0] == hat_from
        late_tab = cut(TB * 2 * T + NFREQ * T + T)
        dft = late_tab[:, 0:TB * 2 * T].rearrange("p (a b) -> p a b", a=TB)
        idft = late_tab[:, TB * 2 * T:TB * 2 * T + NFREQ * T].rearrange("p (a b) -> p a b", a=NFREQ)
        feats = late_tab[:, TB * 2 * T + NFREQ * T:]
        filt_w = cut(2 * 64 + 4 * HY)
        spectra_from = top[0]
        fsum = cut(2 * 2 * HY, ORDERS, TB, HY)
        fdiff = cut(2 * 2 * HY, ORDERS, TB, HY)
        fnorm = cut(2 * HY, ORDERS, HY)
        env_from = top[0]
        env = cut(4 * 2 * HY, TB, 4, HY)
        decay_row = cut(4 * HY, 4, HY)
        top[0] = env_from
        ZF = cut(4 * HY, 4, HY)
        Z1, Z2 = BON, KK
        top[0] = spectra_from
        ZT = cut(TB * HY, TB, HY)
        YF = cut(NFREQ * HY, NFREQ, HY)
        assert top[0] <= words - 2 * (KD * T + RING * KD * P)
        top[0] = env_from + 2 * 4 * HY
        ZSQ = cut(16 * T, 2, 4, HY)
        GATE2 = U[:, 0:16].rearrange("p (a b) c -> p a (b c)", b=2)
        top[0] = env_from
        top[0] = rwkv_from
        M1 = cut(KD * T, KD, T)

        top[0] = free_from
        XBC = cut(24 * T, 24, T)
        Z = cut(16 * T, 16, T)
        V2 = cut(TB * D, TB, D)
        OT = cut(KD * T, KD, T)
        QK = cut(16 * T, 16, T)
        Q, K2 = QK[:, 0:KD], QK[:, KD:]
        G2 = QK.rearrange("p (a b) c -> p a (b c)", b=2)
        dtf = cut(6 * T, 6, T)
        mix2_from = top[0]
        NEG = cut(4 * 3 * P, 4, 3 * P)
        SP = cut(4 * 3 * P, 4, 3 * P)
        LM = cut(4 * 3 * P, 4, 3 * P)
        WA = cut(4 * 3 * P, 4, 3 * P)
        top[0] = mix2_from
        SMALL = cut(5 * 32, 5, 32)
        CBT = cut(4 * TB * P, 4, TB, P)
        BTM = cut(4 * P, 4, P)
        XTM = cut(TB * 2 * D, TB, 2 * D)
        XD = cut(2 * D)
        S0 = cut(4 * HY, 4, HY)
        DD = cut(2 * HY, 2, 4, P)
        DM = cut(2 * HY, 2, 4, P)
        CE = cut(2 * HY, 2, 4, P)
        assert top[0] <= words, top[0]
        SQ4 = XTM.rearrange("p a (b c) -> p (a b) c", c=T)
        M2 = XBC[:, 0:KD]
        top[0] = free_from
        XQ = cut(KD * T, KD, T)
        VM = cut(TB * D, TB, D)
        XT = cut(2 * 2 * T, 2, TB, T)
        stat = cut(3 * 8, 3, 8)
        top[0] = free_from + KF * T + KD * T
        MX = cut(KD * T, KD, T)
        MX2 = MX.rearrange("p (a b) c -> p a (b c)", b=2)
        HM = cut(KD * T, KD, T)
        KM = cut(KD * T, KD, T)
        top[0] = words - split_words
        XO = cut(KD * T, KD, T)
        XP = cut(4 * 2 * T, 4, TB, T)
        HM_HI, HM_LO = ACT_LO[:, 0:KD], ACT_LO[:, KD:2 * KD]

        def tell(ins, name, n=1):
            ins.then_inc(S(name), n)
            counts[name] += n
            return counts[name]

        def link(eng, ins, name):
            eng.wait_ge(S(name), tell(ins, name))

        def wait_emptied(eng, name):
            _, engine, before = jobs.order[jobs.index[name]]
            eng.wait_ge(S(engine + "_emptied"), before + 1)

        def wait_filled(eng, name):
            i = jobs.index[name]
            eng.wait_ge(S("job_done"), i + 1)
            return MB[i % BANKS]

        def emptied(ins, name):
            _, engine, before = jobs.order[jobs.index[name]]
            assert tell(ins, engine + "_emptied") == before + 1, name

        def tiles_done(name, n=None):
            return START[name] + (COUNT[name] if n is None else n)

        def pair_freed(eng, name, j):
            engine, before = PAIR_OWNER[FIRST_PAIR[name] + j]
            eng.wait_ge(S(engine + "_freed_pair"), before + 1)

        def flat(a):
            return a.rearrange("p a b -> p (a b)")

        def four(a):
            return a.rearrange("p (a b) -> p a b", a=4)

        def over(a, n):
            return a.unsqueeze(1).broadcast_to([a.shape[0], n, a.shape[1]])

        def along(a, n):
            return a.unsqueeze(2).broadcast_to([a.shape[0], a.shape[1], n])

        NORMS = ["ffn1_norm", "mix_norm", "ffn2_norm", "final_norm", "g_pre_mix", "g_mem", "g_post_mix",
                 "g_pre_xa", "g_post_xa", "g_pre_ffn", "g_post_ffn"]
        X_VERSION = {"mix_norm": 1, "ffn2_norm": 2, "final_norm": 3, "g_pre_mix": 4, "g_pre_xa": 5, "g_pre_ffn": 6}
        H_VERSION = {"ffn1_norm": 1, "mix_norm": 2, "ffn2_norm": 3, "g_pre_mix": 4, "g_mem": 5, "g_pre_xa": 6,
                     "g_pre_ffn": 7}

        SPLIT_VERSION = {1: 0, 2: 1, 3: 2, 4: 3, 6: 4, 7: 5}

        def make_high(act_eng, n, it=None):
            value = 16 * (n // RING + 1)
            act_eng.wait_ge(landed[n % RING], value if it is None else 16 * it + value)
            if n - RING >= max(r for r in RUN_STARTS if r <= n):
                act_eng.wait_ge(S("tile_used"), n - RING + 1 if it is None else RING * it + (n - RING + 1))
            act_eng.activation(flat(W_HI[:, n % RING]), flat(ring[:, n % RING]), ACT.Copy).then_inc(S("high_ready"), 1)

        def make_low(vec, n, it=None):
            value = SPLIT_RANK[n] + 1
            vec.wait_ge(S("high_ready"), value if it is None else RING * it + value)
            vec.tensor_tensor(flat(W_LO[:, n % RING]), flat(ring[:, n % RING]), flat(W_HI[:, n % RING]).bitcast(F32),
                              ALU.subtract).then_inc(S("low_ready"), 1)

        def split_tiles(eng, make, first, end):
            loops = (end - first) // RING
            if loops > 1:
                with eng.Fori(0, loops) as it:
                    for i in range(RING):
                        make(eng, first + i, it)
            else:
                loops = 0
            for n in range(first + RING * loops, end):
                make(eng, n)

        block = ctx.enter_context(nc.Block())

        @block.sync
        def _(sp):
            w_tile = [w[n] for n in range(RING)]
            for s in range(RING):
                sp.dma_start(ring[:, s].rearrange("p a b -> p (a b)"), w_tile[s]).then_inc(landed[s], 16)

            def refill(m, split, it=None):
                slot = m % RING
                if split:
                    value = SPLIT_RANK[m] + 1
                    sp.wait_ge(S("low_ready"), value if it is None else RING * it + value)
                else:
                    sp.wait_ge(S("tile_used"), m + 1 if it is None else RING * it + (m + 1))
                n = m + RING
                sp.dma_start(flat(ring[:, slot]), w[n] if it is None else w[RING * it + n]).then_inc(landed[slot], 16)

            for first, end, split in RUNS:
                end = min(end, TILES - RING)
                loops = (end - first) // RING
                if loops > 1:
                    with sp.Fori(0, loops) as it:
                        for i in range(RING):
                            refill(first + i, split, it)
                else:
                    loops = 0
                for m in range(first + RING * loops, end):
                    refill(m, split)

        @block.tensor
        def _(pe):
            begun = [0]
            accs = [0]
            blocks_split = [0]

            def mm(o, l, r, start=True, stop=True, loose=False):
                return pe.matmul(o, l, r, start=start, stop=stop, skip_group_check=loose)

            def begin(name):
                i = jobs.index[name]
                assert i == begun[0], (name, i, begun)
                begun[0] += 1
                if i >= BANKS:
                    wait_emptied(pe, jobs.order[i - BANKS][0])
                return MB[i % BANKS]

            def banks_idle():
                for name, engine, _ in reversed(jobs.order[:begun[0]][-BANKS:]):
                    wait_emptied(pe, name)
                if accs[0]:
                    pe.wait_ge(S("acc_read"), accs[0])

            def done(ins):
                tell(ins, "job_done")

            def wait_tile(n, it=None):
                value = 16 * (n // RING + 1)
                pe.wait_ge(landed[n % RING], value if it is None else 16 * it + value)
                return ring[:, n % RING]

            def norm_sum(i):
                for c in range(4):
                    pe.wait_ge(S("sq_ready"), 4 * i + c + 1)
                    for k in (2 * c, 2 * c + 1):
                        m = mm(SS, ones, sq[:, k], start=k == 0, stop=k == KD - 1)
                tell(m, "ssq_done")

            def mm3(o, l_hi, l_lo, r_hi, r_lo, start, stop, loose=False):
                mm(o, l_hi, r_hi, start=start, stop=False, loose=loose)
                mm(o, l_hi, r_lo, start=False, stop=False, loose=loose)
                return mm(o, l_lo, r_hi, start=False, stop=stop, loose=loose)

            def wait_parts(n, it=None):
                value = SPLIT_RANK[n] + 1
                pe.wait_ge(S("low_ready"), value if it is None else RING * it + value)
                return W_HI[:, n % RING], W_LO[:, n % RING]

            def pair(name, j, rhs, it=None, parts_of=None, parts=(H_HI, H_LO)):
                g = FIRST_PAIR[name] + j
                if g >= 2:
                    engine, before = PAIR_OWNER[g - 2]
                    pe.wait_ge(S(engine + "_freed_pair"), before + 1 if it is None else before + 1 + 2 * it)
                for half in range(2):
                    if 2 * j + half >= COUNT[name]:
                        break
                    n = START[name] + 2 * j + half
                    dst = LP[g % 2][:, half * T:half * T + T]
                    if name in SPLIT:
                        hi, lo = wait_parts(n, it)
                        for k in range(KD):
                            if parts_of is not None and half == 0:
                                pe.wait_ge(S("h_low"), KD * parts_of + k + 1)
                            m = mm3(dst, hi[:, k], lo[:, k], parts[0][:, k], parts[1][:, k], k == 0, k == KD - 1)
                    else:
                        tile = wait_tile(n, it)
                        for k in range(KD):
                            m = mm(dst, tile[:, k], rhs[:, k], start=k == 0, stop=k == KD - 1)
                    m.then_inc(S("tile_used"), 1)

            def ups(name, rhs, version):
                if name not in SPLIT:
                    pe.wait_ge(S("h_ready"), KD * version)
                pairs = PAIRS[name]
                for j in range(min(2, pairs)):
                    pair(name, j, rhs, None, SPLIT_VERSION[version] if name in SPLIT and j == 0 else None)
                loops = (pairs - 2) // 2
                if COUNT[name] % 2:
                    loops = 0
                if loops > 1:
                    with pe.Fori(0, loops) as it:
                        pair(name, 2, rhs, it)
                        pair(name, 3, rhs, it)
                else:
                    loops = 0
                for j in range(2 + 2 * loops, pairs):
                    pair(name, j, rhs)

            def acc_tile(n, rhs, first, last, it=None):
                tile = wait_tile(n, it)
                for m_ in range(KD):
                    m = mm(ACC[m_ // 2][:, (m_ % 2) * T:(m_ % 2) * T + T], tile[:, m_], rhs,
                           start=first and m_ % 2 == 0, stop=last, loose=True)
                m.then_inc(S("tile_used"), 1)

            def downs(name, rhs):
                banks_idle()
                if name in SPLIT:
                    for k in range(COUNT[name]):
                        hi, lo = wait_parts(START[name] + k)
                        slot = blocks_split[0] % KD
                        blocks_split[0] += 1
                        pe.wait_ge(S("block_low"), blocks_split[0])
                        for m_ in range(KD):
                            m = mm3(ACC[m_ // 2][:, (m_ % 2) * T:(m_ % 2) * T + T], hi[:, m_], lo[:, m_],
                                    H_HI[:, slot], H_LO[:, slot], k == 0 and m_ % 2 == 0,
                                    k == COUNT[name] - 1, loose=True)
                        m.then_inc(S("tile_used"), 1)
                    accs[0] += 1
                    return
                for k in range(COUNT[name]):
                    acc_tile(START[name] + k, rhs[:, k], k == 0, k == COUNT[name] - 1)
                accs[0] += 1

            def ffn_down(name, index):
                banks_idle()
                n0 = START[name]

                def one(k, it=None):
                    hi, lo = wait_parts(n0 + k, it)
                    value = KF * index + k + 1
                    pe.wait_ge(S("act_low"), value if it is None else RING * it + value)
                    at = k if it is None else RING * it + k
                    for m_ in range(KD):
                        m = mm3(ACC[m_ // 2][:, (m_ % 2) * T:(m_ % 2) * T + T], hi[:, m_], lo[:, m_],
                                ACT_HI[:, at], ACT_LO[:, at], it is None and k == 0 and m_ % 2 == 0,
                                it is None and k == KF - 1, loose=True)
                    m.then_inc(S("tile_used"), 1)

                one(0)
                one(1)
                with pe.Fori(0, 4) as it:
                    for i in range(4):
                        one(2 + i, it)
                for k in range(KF - 4, KF):
                    one(k)
                accs[0] += 1

            def by_token(name, src, parts=(H_HI, H_LO), after_tile=None):
                banks_idle()
                for k in range(COUNT[name]):
                    if name in SPLIT:
                        hi, lo = (flat(part) for part in wait_parts(START[name] + k))
                    else:
                        tile = flat(wait_tile(START[name] + k))
                    for b in range(TB):
                        at = slice(b * P, b * P + P)
                        for half in range(2):
                            cols = slice(half * HY, half * HY + HY)
                            if name in SPLIT:
                                m = mm3(ACC[2 * b + half], parts[0][:, k, at], parts[1][:, k, at], hi[:, cols], lo[:, cols],
                                        k == 0, k == COUNT[name] - 1, loose=True)
                            else:
                                m = mm(ACC[2 * b + half], src[:, k, at], tile[:, cols],
                                       start=k == 0, stop=k == COUNT[name] - 1, loose=True)
                    m.then_inc(S("tile_used"), 1)
                    if after_tile is not None and k == after_tile[0]:
                        norm_sum(after_tile[1])
                accs[0] += 1

            pe.wait_ge(S("in_par"), 16 * 2)
            norm_sum(0)
            ups("ffn1_up", h, 1)
            ffn_down("ffn1_down", 0)
            norm_sum(1)
            ups("conv_in", h, 2)

            fill_steps = {"gates": 0, "hyena": 0}

            def fill(what, limit):
                i = fill_steps[what]
                if i >= limit:
                    return False
                fill_steps[what] += 1
                n = (GATE_TILES if what == "gates" else HYENA_TILES)[i // 2]
                bank = GATE_BANK[i // 4] if what == "gates" else GB
                if what == "gates" and i == 28:
                    pe.wait_ge(S("gate_read"), 5)
                if i % 4 == 0 and bank is GB:
                    if what == "gates":
                        gates, hyena = {0: 0, 3: 1, 6: 4}[i // 4], fill_steps["hyena"] // 4
                    else:
                        gates, hyena = 1 if i < 12 else 4, i // 4
                    if gates:
                        pe.wait_ge(S("gate_read"), gates)
                    if hyena:
                        pe.wait_ge(S("hyena_conv"), hyena)
                if i % 2 == 0:
                    wait_tile(n)
                tile = ring[:, n % RING]
                half = i // 2 % 2
                for k in range(4 * (i % 2), 4 * (i % 2) + 4):
                    m = mm(bank[:, half * T:half * T + T], tile[:, k], h[:, k], start=k == 0, stop=k == KD - 1, loose=True)
                if i % 2:
                    m.then_inc(S("tile_used"), 1)
                return True

            banks_idle()
            pe.wait_ge(S("in_small"), 16)
            pe.wait_ge(S("lora_in"), 2)
            for half in range(2):
                o = begin(("gate_lora", half))
                for qq in range(2):
                    q = 2 * half + qq
                    mm(o[:, qq * T:qq * T + T], lora[:, 2, q * P:q * P + P], U[:, 14], stop=False)
                    m = mm(o[:, qq * T:qq * T + T], lora[0:32, 3, q * P:q * P + P], U[0:32, 15], start=False)
                done(m)
            for half in range(2):
                pe.wait_ge(S("kk_sq"), 1)
                o = begin(("key_norm", half))
                done(mm(o, head_ones, flat(Y[:, 2 * half:2 * half + 2])))

            def loras(d):
                rows = slice(64 * d, 64 * d + 64)
                for name, wi, ui in (("decay_lora", 0, 12), ("rate_lora", 1, 13)):
                    for half in range(2):
                        o = begin((name, d, half))
                        for qq in range(2):
                            q = 2 * half + qq
                            m = mm(o[:, qq * T:qq * T + T], lora[rows, wi, q * P:q * P + P], U[rows, ui])
                        done(m)

            def turns(d, what, src):
                for b in range(TB):
                    o = begin((what, d, b))
                    for q in range(KH):
                        m = pe.transpose(o[:, q * P:q * P + P], src(q, b), ident)
                    done(m)

            def blocks_of(s):
                return lambda q, b: s[:, q, b * P:b * P + P]

            loras(0)
            for d in range(2):
                while fill("gates", 16 if d else 12):
                    pass
                if d:
                    pe.wait_ge(S("rv_ready"), 1)
                turns(d, "v", blocks_of(RV if d else U[:, 8:12]))
                pe.wait_ge(S("dir_ready"), d + 1)
                turns(d, "alpha", lambda q, b: AR[:, q, b, 0])
                for u in range(4):
                    b = u // 2
                    for e in range(2):
                        r = slice(64 * e, 64 * e + 64)
                        for name, src in (("beta_pairs", BE), ("kappa_pairs", KA)):
                            o = begin((name, d, u, e))
                            for qq in range(2):
                                q = 2 * (u % 2) + qq
                                m = mm(o[:, qq * T:qq * T + T], src[r, q, b * P:b * P + P],
                                       AR[r, q, b].rearrange("p a b -> p (a b)"))
                            done(m)
                    for e in range(2):
                        r = slice(64 * e, 64 * e + 64)
                        o = begin(("alpha_beta", d, u, e))
                        for qq in range(2):
                            q = 2 * (u % 2) + qq
                            m = mm(o[:, qq * P:qq * P + P], AR[r, q, b, 0], BE[r, q, b * P:b * P + P])
                        done(m)

                pe.wait_ge(S("hats_ready"), d + 1)
                turns(d, "beta", blocks_of(BH))
                turns(d, "kappa", blocks_of(KHAT))

                def product(level, u):
                    o = begin(("product", d, level, u))
                    if level > 2:
                        wait_emptied(pe, ("inverse", d, level - 1, u))
                    else:
                        pe.wait_ge(S("first_level"), 4 * d + u + 1)
                    pe.wait_ge(S("off_diagonal"), 16 * d + 4 * (level - 2) + u + 1)
                    for hh in range(4):
                        m = mm(o[:, hh * P:hh * P + P], BT[:, u % 2, hh], TN[:, u, hh])
                    done(m)

                for level in range(2, 6):
                    product(level, 0)
                    product(level, 1)
                    for u in range(4):
                        if level > 2:
                            wait_emptied(pe, ("inverse_t", d, level - 1, u))
                        wait_emptied(pe, ("product", d, level, u))
                        if level < 5:
                            o = begin(("inverse", d, level, u))
                            for hh in range(4):
                                m = mm(o[:, hh * P:hh * P + P], TT[:, u, hh], PR[:, u % 2, hh])
                            done(m)
                        o = begin(("inverse_t", d, level, u))
                        for hh in range(4):
                            m = mm(o[:, hh * P:hh * P + P], PR[:, u % 2, hh], TT[:, u, hh])
                        done(m)
                        if u + 2 < 4:
                            product(level, u + 2)
                for b in range(TB):
                    wait_emptied(pe, ("v", d, b))
                    wait_emptied(pe, ("alpha", d, b))
                    wait_emptied(pe, ("kappa_pairs", d, 3, 1))
                    wait_emptied(pe, ("inverse_t", d, 5, 3))
                    o = begin(("alpha_v", d, b))
                    for hd in range(8):
                        u, hh = 2 * b + hd // 4, hd % 4
                        m = mm(o[:, hd * 64:hd * 64 + 64], KX[:, u, hh, 0], TM["v"][:, b, hd * 64:hd * 64 + 64])
                    done(m)
                    o = begin(("w_t", d, b))
                    for hd in range(8):
                        u, hh = 2 * b + hd // 4, hd % 4
                        m = mm(o[64 * (hd % 2):64 * (hd % 2) + 64, (hd // 2) * P:(hd // 2) * P + P],
                               TM["alpha"][:, b, hd * 64:hd * 64 + 64], TT[:, u, hh])
                    done(m)
                if d == 0:
                    loras(1)
                wait_emptied(pe, ("beta", d, 1))
                wait_emptied(pe, ("kappa", d, 1))
                for c in range(NCH):
                    b, r = c // 4, slice(CH * (c % 4), CH * (c % 4) + CH)
                    if c % 4 == 0:
                        fill("hyena", 12 * d + 4 * (1 + c // 3))
                        wait_emptied(pe, ("alpha_v", d, b))
                        wait_emptied(pe, ("w_t", d, b))
                        o2 = [begin(("chain", d, b, e)) for e in range(2)]
                        for e in range(2):
                            for q in range(KH):
                                hd = 2 * q + e
                                u, hh = 2 * b + hd // 4, hd % 4
                                m = mm(o2[e][:, q * 64:q * 64 + 64], TT[:, u, hh], AV[:, b, hd * 64:hd * 64 + 64],
                                       start=q == 0, stop=c == 0, loose=True)
                    if c:
                        fill("hyena", 12 * d + 4 * (1 + c // 3))
                        pe.wait_ge(S("state_ready"), 7 * d + c)
                        for e in range(2):
                            er = slice(64 * e, 64 * e + 64)
                            for q in range(KH):
                                m = mm(o2[e][r, q * 64:q * 64 + 64], WT[er, q, c * CH:c * CH + CH],
                                       HS[er, c, q * 64:q * 64 + 64], start=False, stop=True, loose=True)
                            if c % 4 == 3:
                                done(m)
                    if c % 4 < 3:
                        tell(m, "sa_psum")
                    if c == NCH - 1:
                        break
                    for hd in range(8):
                        q, e = hd // 2, slice(64 * (hd % 2), 64 * (hd % 2) + 64)
                        mm(LP[c % 2][e, q * 64:q * 64 + 64], TM["kappa"][r, b, hd * 64:hd * 64 + 64],
                           TM["v"][r, b, hd * 64:hd * 64 + 64], start=hd < 2, stop=False, loose=True)
                    fill("hyena", 12 * d + 4 * (1 + c // 3))
                    pe.wait_ge(S("sa_ready"), 8 * d + c + 1)
                    for hd in range(8):
                        q, e = hd // 2, slice(64 * (hd % 2), 64 * (hd % 2) + 64)
                        m = mm(LP[c % 2][e, q * 64:q * 64 + 64], TM["beta"][r, b, hd * 64:hd * 64 + 64],
                               SA[r, b, hd % 2, q * 64:q * 64 + 64], start=False, stop=True, loose=True)
                    tell(m, "state_psum")
                while fill("hyena", 12 * d + 12):
                    pass
                pe.wait_ge(S("sa_ready"), 8 * d + NCH)
                for pr in range(2):
                    o = begin(("y", d, pr))
                    for qq in range(2):
                        q = 2 * pr + qq
                        for e in range(2):
                            er = slice(64 * e, 64 * e + 64)
                            hd = 2 * q + e
                            for b in range(TB):
                                u, hh = 2 * b + hd // 4, hd % 4
                                cols = slice(qq * T + b * P, qq * T + b * P + P)
                                mm(o[er, cols], SA[:, b, e, q * 64:q * 64 + 64], BX[:, u, hh, 1],
                                   start=qq == 0 and b == 0, stop=False, loose=True)
                                m = mm(o[er, cols], TM["v"][:, b, hd * 64:hd * 64 + 64], KX[:, u, hh, 1],
                                       start=False, stop=True, loose=True)
                                for cc in range(4):
                                    if 4 * b + cc == 0:
                                        continue
                                    at = qq * T + b * P + cc * CH
                                    m = mm(o[er, at:at + CH], HS[er, 4 * b + cc, q * 64:q * 64 + 64],
                                           AR[er, q, b, 1, cc * CH:cc * CH + CH], start=False, stop=True, loose=True)
                    done(m)
            fill("gates", 18)
            fill("gates", 18)
            wait_emptied(pe, ("y", 1, 1))
            for half in range(2):
                o = begin(("mean", half))
                done(mm(o, head_ones, flat(Y[:, 2 * half:2 * half + 2])))
            fill("gates", 20)
            fill("gates", 20)
            for half in range(2):
                pe.wait_ge(S("y_sq"), half + 1)
                o = begin(("var", half))
                done(mm(o, head_ones, flat(KA[:, 2 * half:2 * half + 2])))
            for half in range(2):
                o = begin(("bonus", half))
                done(mm(o, head_ones, flat(BON[:, 2 * half:2 * half + 2])))

            pe.wait_ge(S("in_hyena"), 16 * 3)
            o = begin(("sin", 0))
            done(mm(o[0:64, 0:T], filt_w[0:EMB, 0:64], feats[0:EMB, :]))
            while fill("gates", 28):
                pass
            pe.wait_ge(S("sin_ready"), 1)
            o = begin(("sin", 1))
            done(mm(o[0:64, 0:T], filt_w[0:64, 64:128], sin_out[0:64, 0]))
            while fill("gates", 32):
                pass
            pe.wait_ge(S("sin_ready"), 2)
            for b in range(TB):
                for c in range(4):
                    o = begin(("filter", b, c))
                    done(mm(o, sin_out[0:65, 1, b * P:b * P + P], filt_w[0:65, 128 + c * HY:128 + c * HY + HY]))
            for o_ in range(ORDERS):
                pe.wait_ge(S("filt_sq"), 4 * (o_ + 1))
                o = begin(("filter_norm", o_))
                for i in range(4):
                    m = mm(o, ones, ZSQ[:, o_, i], start=i == 0, stop=i == 3)
                done(m)
                pe.wait_ge(S("filt_sum"), 4 * (o_ + 1))
                for m_ in range(NFREQ):
                    o = begin(("filter_dft", o_, m_))
                    src = fsum if m_ < 2 else fdiff
                    for b in range(TB):
                        m = mm(o, dft[:, b, m_ * P:m_ * P + P], src[:, o_, b], start=b == 0, stop=b == 1)
                    done(m)
                o = begin(("nyquist", o_))
                for b in range(TB):
                    m = mm(o[0:1], dft[:, b, T:T + 1], fsum[:, o_, b], start=b == 0, stop=b == 1)
                done(m)
            for o_ in range(ORDERS):
                src = U[:, 24:28] if o_ == 0 else Z1
                if o_:
                    wait_emptied(pe, ("idft", 0, 1))
                else:
                    wait_emptied(pe, ("nyquist", 1))
                for b in range(TB):
                    o = begin(("turn", o_, b))
                    for q in range(KH):
                        m = pe.transpose(o[:, q * P:q * P + P], src[:, q, b * P:b * P + P], ident)
                    done(m)
                wait_emptied(pe, ("turn", o_, 1))
                for m_ in (0, 2, 1, 3):
                    o = begin(("dft", o_, m_))
                    for b in range(TB):
                        m = mm(o, dft[:, b, m_ * P:m_ * P + P], ZT[:, b], start=b == 0, stop=b == 1)
                    done(m)
                pe.wait_ge(S("spectrum_ready"), 2 * (o_ + 1))
                for half in range(2):
                    o = begin(("idft", o_, half))
                    for qq in range(2):
                        q = 2 * half + qq
                        for m_ in range(NFREQ):
                            m = mm(o[:, qq * T:qq * T + T], YF[:, m_, q * P:q * P + P], idft[:, m_],
                                   start=m_ == 0, stop=m_ == NFREQ - 1)
                    done(m)
            assert fill_steps == {"gates": 32, "hyena": 24}
            downs("rw_out", Y)
            downs("hy_out", Z2)
            pe.wait_ge(S("merged"), 1)
            downs("w_out", M1)
            norm_sum(2)
            ups("ffn2_up", h, 3)
            ffn_down("ffn2_down", 1)
            norm_sum(3)
            norm_sum(4)

            ups("xbc", h, 4)
            ups("dt", h, 4)
            ups("qk", h, 4)
            by_token("v", h)
            ups("z", h, 4)
            banks_idle()
            pair_freed(pe, "qk", PAIRS["qk"] - 1)

            def scores_into(o, i, start, stop):
                q, r = i // 2, slice(64 * (i % 2), 64 * (i % 2) + 64)
                mm(o[:, 0:T], K2[r, q, 0:P], Q[r, q, :], start=start, stop=stop, loose=True)
                return mm(o[:, T:T + P], K2[r, q, P:T], Q[r, q, P:T], start=False, stop=stop, loose=True)

            for n in range(8 + 2):
                for hd in (2 * n, 2 * n + 1):
                    if n < 8:
                        o = begin(("scores", hd))
                        done(scores_into(o, hd, True, True))
                for hd in (2 * n - 2, 2 * n - 1):
                    if 1 <= n < 9:
                        o = begin(("stick", hd))
                        scores_into(o, hd, True, False)
                        pe.wait_ge(S("log_ready"), hd + 1)
                        lm = LM[:, hd % 4]
                        mm(o[:, 0:T], table("tri"), lm[:, 0:T], start=False, stop=False, loose=True)
                        mm(o[:, P:T], ones, lm[:, T:T + P], start=False, stop=True, loose=True)
                        done(mm(o[:, T:T + P], table("tri"), lm[:, T:T + P], start=False, stop=True, loose=True))
                if n >= 2:
                    q = n - 2
                    o = begin(("attend", q))
                    for e in range(2):
                        hd = 2 * q + e
                        pe.wait_ge(S("stick_weights"), hd + 1)
                        wa = WA[:, hd % 4]
                        r = slice(64 * e, 64 * e + 64)
                        mm(o[r, 0:T], V2[:, 0, hd * 64:hd * 64 + 64], wa[:, 0:T], start=True, stop=False, loose=True)
                        m = mm(o[r, P:T], V2[:, 1, hd * 64:hd * 64 + 64], wa[:, T:T + P], start=False, stop=True, loose=True)
                    done(m)
            pe.wait_ge(S("dt_ready"), 1)
            o = begin(("small_turns",))
            for j, src in enumerate((dtf[0:32, 2, 0:P], dtf[0:32, 2, P:T], dtf[0:32, 0, 0:P], dtf[0:32, 0, P:T],
                                     dtf[0:32, 4, 0:P])):
                m = pe.transpose(o[:, 32 * j:32 * j + 32], src, ident[0:32, 0:32])
            done(m)
            pe.wait_ge(S("xbc_ready"), 3)
            o = begin(("b_turn",))
            for g in range(4):
                m = pe.transpose(o[:, g * P:g * P + P], XBC[:, 16 + g, 0:P], ident)
            done(m)
            for g0 in range(0, 4, 2):
                o = begin(("cb", g0))
                for gg in range(2):
                    for b in range(TB):
                        at = (gg * TB + b) * P
                        m = mm(o[:, at:at + P], XBC[:, 16 + g0 + gg, b * P:b * P + P], XBC[:, 20 + g0 + gg, b * P:b * P + P])
                done(m)
            for b in range(TB):
                for c in range(4):
                    o = begin(("x_turn", b, c))
                    for q in range(4):
                        m = pe.transpose(o[:, q * P:q * P + P], XBC[:, 4 * c + q, b * P:b * P + P], ident)
                    done(m)
            wait_emptied(pe, ("b_turn",))
            for g in range(4):
                pe.wait_ge(S("xd_ready"), 1)
                o = begin(("state", g))
                done(mm(o, BTM[:, g], XD[:, g * HY:g * HY + HY]))

            def decay_rows(t):
                g, b, half = TURN[t]
                o = begin(("decay_rows", t))
                for i in range(4):
                    hd = 8 * g + 4 * half + i
                    m = mm(o[:, i * P:i * P + P], ident[0:32, hd:hd + 1].broadcast_to([32, P]),
                           dtf[0:32, 2, b * P:b * P + P])
                done(m)

            def ssm_y(t):
                g, b, half = TURN[t]
                pe.wait_ge(S("ssm_mix_ready"), t + 1)
                o = begin(("ssm_y", t))
                if b:
                    wait_emptied(pe, ("state", g))
                    pe.wait_ge(S("row_ready"), 2 * g + half + 1)
                for i in range(4):
                    hd = 8 * g + 4 * half + i
                    dst = o[64 * (i % 2):64 * (i % 2) + 64, (i // 2) * P:(i // 2) * P + P]
                    m = mm(dst, XTM[:, b, hd * 64:hd * 64 + 64], DM[:, t % 2, i],
                           start=i < 2, stop=b == 0, loose=True)
                    if b:
                        m = mm(dst, S0[:, g, (4 * half + i) * 64:(4 * half + i) * 64 + 64], CE[:, t % 2, i],
                               start=False, stop=True, loose=True)
                done(m)

            decay_rows(0)
            for t in range(TURNS):
                if t:
                    ssm_y(t - 1)
                if t + 1 < TURNS:
                    decay_rows(t + 1)
                if t % 2:
                    pair("gates2", t // 2, h)
            ssm_y(TURNS - 1)
            for g0 in range(0, 4, 2):
                o = begin(("group_norm", g0))
                for gg in range(2):
                    pe.wait_ge(S("gy_sq"), g0 + gg + 1)
                    for q in range(4):
                        m = mm(o[:, gg * T:gg * T + T], ones, SQ4[:, 4 * (g0 + gg) + q], start=q == 0, stop=q == 3)
                done(m)
            norm_sum(5)
            wait_emptied(pe, ("attend", 7))
            downs("br_att", OT)
            downs("br_ssm", XBC)
            pe.wait_ge(S("mem_low"), KD)
            mem = (HM_HI, HM_LO)
            pair("mem_k0", 0, None, parts=mem)
            pair("mem_k0", 1, None, parts=mem)
            downs("mix_out", M2)
            pair("mem_k1", 0, None, parts=mem)
            norm_sum(6)

            pair("mem_k1", 1, None, parts=mem)
            by_token("mem_v", HM, mem, (2, 7))
            ups("xq", h, 6)
            banks_idle()
            pair_freed(pe, "mem_k1", 1)
            pair_freed(pe, "xq", 3)
            for hd in range(4):
                o = begin(("xa_scores", hd))
                for b in range(TB):
                    for c in range(2):
                        m = mm(o[:, b * T:b * T + T], XQ[:, 2 * hd + c, b * P:b * P + P], KM[:, 2 * hd + c],
                               start=c == 0, stop=c == 1)
                done(m)
            for hd in range(4):
                pe.wait_ge(S("xa_probs"), hd + 1)
                o = begin(("xa_turn", hd))
                for mb in range(2):
                    for b in range(TB):
                        m = pe.transpose(o[:, mb * T + b * P:mb * T + b * P + P], XP[:, hd, b, mb * P:mb * P + P], ident)
                done(m)
                wait_emptied(pe, ("xa_turn", hd))
                o = begin(("xa_out", hd))
                for dd in range(2):
                    for mb in range(2):
                        m = mm(o[:, dd * T:dd * T + T], VM[:, mb, hd * T + dd * P:hd * T + dd * P + P], XT[:, hd % 2, mb],
                               start=mb == 0, stop=mb == 1)
                done(m)
            wait_emptied(pe, ("xa_out", 3))
            downs("xo", XO)
            norm_sum(8)
            norm_sum(9)
            ups("ffn3_up", h, 7)
            ffn_down("ffn3_down", 2)
            norm_sum(10)

        @block.scalar
        def _(a):
            def f(o, i, func, **kw):
                return a.activation(o, i, func, **kw)

            def root_of(i):
                if i:
                    a.wait_ge(S("root_read"), i)
                a.wait_ge(S("ssq_done"), i + 1)
                tell(f(root, SS, ACT.Sqrt, scale=1.0 / D, bias=eps[:, 0:1]), "root_ready")

            def squares(i, first_tile=None, then_root=True):
                name = NORMS[i]
                after = {"g_post_mix": "mix_out", "g_post_xa": "xo", "g_post_ffn": "ffn3_down"}
                if i:
                    a.wait_ge(S("ssq_done"), i)
                if name in after:
                    a.wait_ge(S("tile_used"), tiles_done(after[name]))
                if name == "g_mem":
                    a.wait_ge(S("in_mem"), 16)
                src = [ACC[c] for c in range(4)] if name in after else [(MX2 if name == "g_mem" else x2)[:, c] for c in range(4)]
                for c in range(4):
                    if name == "ffn1_norm":
                        a.wait_ge(S(f"in_x{c}"), 16)
                    if name in X_VERSION:
                        a.wait_ge(S("x_ready"), 4 * (X_VERSION[name] - 1) + c + 1)
                    tell(f(sq2[:, c], src[c], ACT.Square), "sq_ready")
                if first_tile is not None:
                    make_high(a, first_tile)
                    make_high(a, first_tile + 1)
                if then_root:
                    root_of(i)

            def split_h(version):
                for k in range(KD):
                    a.wait_ge(S("h_ready"), KD * (version - 1) + k + 1)
                    tell(f(H_HI[:, k], h[:, k], ACT.Copy), "h_high")

            def ahead(name, j, it=None):
                for n in (START[name] + 2 * j + 2, START[name] + 2 * j + 3):
                    make_high(a, n, it)

            def split_block(src, k, slot_tile=None):
                if slot_tile is not None:
                    a.wait_ge(S("tile_used"), slot_tile + 1)
                tell(f(H_HI[:, counts["block_high"] % KD], src[:, k], ACT.Copy), "block_high")

            def silus(name, version):
                n0, fp = START[name], FIRST_PAIR[name]
                before = PAIR_OWNER[fp][1]

                def one(j, it=None):
                    ahead(name, j, it)
                    tw = n0 + 2 * j + 2
                    a.wait_ge(S("tile_used"), tw if it is None else 2 * 2 * it + tw)
                    if j >= 2:
                        fr = before + j - 1
                        a.wait_ge(S("dve_freed_pair"), fr if it is None else 2 * it + fr)
                    f(gate_tmp[:, j % 2], LP[(fp + j) % 2][:, 0:T], ACT.Silu).then_inc(S("silu_ready"), 1)

                one(0)
                one(1)
                with a.Fori(0, (KF - 2) // 2) as it:
                    one(2, it)
                    one(3, it)
                down = n0 + 2 * KF
                split_tiles(a, make_high, down + 2, down + KF + (0 if name == "ffn3_up" else 2))

            def pair_loop(name, body):
                loops, n0 = PAIRS[name] // 2, START[name]
                last = name in ("conv_in", "z")
                with a.Fori(0, loops - last) as it:
                    for p in range(2):
                        if name in SPLIT:
                            ahead(name, p, it)
                        a.wait_ge(S("tile_used"), n0 + 2 * p + 2 + 4 * it)
                        body(p, it)
                if last:
                    for p in range(2):
                        if p == 0:
                            ahead(name, 2 * (loops - 1))
                        a.wait_ge(S("tile_used"), n0 + 4 * (loops - 1) + 2 * p + 2)
                        body(p, loops - 1)

            for c in range(4):
                a.dma_start(x2[:, c], x_in[:, c * 2 * T:(c + 1) * 2 * T]).then_inc(S(f"in_x{c}"), 16)
            a.dma_start(tab[:, 0:3 * P], tables_in[:, 0:3 * P]).then_inc(S("in_par"), 16)
            a.dma_start(par, params_in).then_inc(S("in_par"), 16)
            a.dma_start(tab[:, 3 * P:], tables_in[:, 3 * P:tab_split]).then_inc(S("in_tab"), 16)
            a.dma_start(flat(lora), lora_in).then_inc(S("in_small"), 16)
            a.wait_ge(S("consts"), 2)
            squares(0, START["ffn1_up"])
            split_h(1)
            a.wait_ge(S("in_par"), 32)
            tell(f(c_a[0:32], param("a_log", 0, 32), ACT.Exp), "c_a_exp")
            silus("ffn1_up", 0)
            squares(1)
            split_h(2)
            a.wait_ge(S("coefs"), 2)

            def taps_mid(p, it):
                bank = LP[(FIRST_PAIR["conv_in"] + p) % 2]
                at = PARAMS["tap_bias"][0]
                for half in range(2):
                    blk = 4 * it + (2 * p + half)
                    ins = f(U[:, blk], bank[:, half * T:half * T + T], ACT.Identity, scale=c_mid[:, bass.ds(blk, 1)],
                            bias=par[:, bass.ds(blk + at, 1)])
                ins.then_inc(S("mid_ready"), 1)

            pair_loop("conv_in", taps_mid)

            pair_freed(a, "conv_in", 7)
            tell(f(U[:, 12], U[:, 12], ACT.Tanh), "lora_in")
            tell(f(U[:, 14:16], U[:, 14:16], ACT.Sigmoid), "lora_in")
            for half in range(2):
                o = wait_filled(a, ("gate_lora", half))
                emptied(f(flat(G[:, 2 * half:2 * half + 2]), o, ACT.Copy), ("gate_lora", half))
            a.wait_ge(S("kk_raw"), 1)
            tell(f(Y, KK, ACT.Square), "kk_sq")
            wait_emptied(a, ("key_norm", 1))
            tell(f(BON, BON, ACT.Sqrt), "kk_root")

            def loras(d):
                if d:
                    a.wait_ge(S("dir_ready"), d)
                    a.wait_ge(S("bon_ready"), d)
                for name, dst, bias in (("decay_lora", L, "w0"), ("rate_lora", A, "a0")):
                    for half in range(2):
                        o = wait_filled(a, (name, d, half))
                        for qq in range(2):
                            q = 2 * half + qq
                            to = dst[:, q, ::-1] if d else dst[:, q, :]
                            ins = f(to, o[:, qq * T:qq * T + T], ACT.Sigmoid, bias=param(bias, 4 * d + q))
                        emptied(ins, (name, d, half))

            def exp_negative(d):
                a.wait_ge(S("cum_ready"), 2 * d + 1)
                tell(f(EN, C, ACT.Exp, scale=-LOG_DECAY), "exps")

            def exp_positive(d):
                a.wait_ge(S("cum_ready"), 2 * d + 2)
                tell(f(EX, EX, ACT.Exp, scale=LOG_DECAY), "exps")
                a.wait_ge(S("exps"), 3 * d + 1)
                tell(f(EP, C, ACT.Exp, scale=LOG_DECAY), "exps")

            def store_gates(p):
                a.wait_ge(S("tile_used"), GATE_TILES[2 * p + 1] + 1)
                if p:
                    a.wait_ge(S("gate_out"), 16 * p)
                link(a, f(flat(gate_tmp), GATE_BANK[p], ACT.Sigmoid), "gate_read")
                a.dma_start(gates_dram[:, p], flat(gate_tmp)).then_inc(S("gate_out"), 16)

            def hyena_mid(r):
                a.wait_ge(S("tile_used"), HYENA_TILES[2 * r + 1] + 1)
                for half in range(2):
                    blk = 16 + 2 * r + half
                    ins = f(U[:, blk], GB[:, half * T:half * T + T], ACT.Identity, scale=c_mid[:, blk:blk + 1],
                            bias=param("tap_bias", blk))
                tell(ins, "hyena_mid")

            def turns(d, what):
                for b in range(TB):
                    o = wait_filled(a, (what, d, b))
                    emptied(f(TM[what][:, b], o, ACT.Copy), (what, d, b))

            loras(0)
            exp_negative(0)
            exp_positive(0)
            store_gates(0)
            for d in range(2):
                if d:
                    wait_filled(a, ("y", 0, 1))
                    tell(f(RV, U[:, 8:12, ::-1], ACT.Copy), "rv_ready")
                turns(d, "v")
                turns(d, "alpha")
                store_gates(3 if d else 1)
                turns(d, "beta")
                if d == 0:
                    store_gates(2)
                turns(d, "kappa")
                for level in range(2, 6):
                    for u in range(4):
                        o = wait_filled(a, ("product", d, level, u))
                        emptied(f(PR[:, u % 2], four(o), ACT.Copy), ("product", d, level, u))
                for b in range(TB):
                    o = wait_filled(a, ("alpha_v", d, b))
                    emptied(f(AV[:, b], o, ACT.Copy), ("alpha_v", d, b))
                    o = wait_filled(a, ("w_t", d, b))
                    emptied(f(WT[:, :, b * P:b * P + P], four(o), ACT.Copy), ("w_t", d, b))
                if d == 0:
                    loras(1)
                    exp_negative(1)
                    hyena_mid(0)
                    exp_positive(1)
                for r in range(3 * d + (d == 0), 3 * d + 3):
                    hyena_mid(r)
            wait_filled(a, ("y", 1, 1))
            a.dma_start(late_tab, tables_in[:, tab_split:]).then_inc(S("in_hyena"), 16)
            a.dma_start(filt_w, filt_in).then_inc(S("in_hyena"), 16)
            a.dma_start(flat(decay_row), decay_in.partition_broadcast(P)).then_inc(S("in_hyena"), 16)
            for half in range(2):
                wait_emptied(a, ("mean", half))
                tell(f(KA[:, 2 * half:2 * half + 2], Y[:, 2 * half:2 * half + 2], ACT.Square), "y_sq")
            wait_emptied(a, ("var", 1))
            tell(f(BE, BE, ACT.Sqrt), "y_root")
            store_gates(4)
            store_gates(5)

            a.wait_ge(S("in_hyena"), 48)
            link(a, f(decay_row, decay_row, ACT.Abs), "act_step")
            for b in range(TB):
                tell(f(env[:, b], decay_row, ACT.Exp, scale=table("minus_t")[:, b:b + 1]), "env_ready")
            for i in range(2):
                a.wait_ge(S("sin_args"), i + 1)
                tell(f(sin_out[0:64, i], sin_in[0:64], ACT.Sin), "sin_ready")
                store_gates(6 + i)
            for o_ in range(ORDERS):
                a.wait_ge(S("filt_made"), 1)
                for i in range(4):
                    tell(f(ZSQ[:, o_, i], env[:, i % 2, 2 * (i // 2) + o_], ACT.Square), "filt_sq")
            for o_ in range(ORDERS):
                o = wait_filled(a, ("filter_norm", o_))
                tell(f(fnorm[:, o_], o, ACT.Sqrt, bias=eps[:, 0:1]), "filt_root")
            a.wait_ge(S("rwkv_done"), 1)
            a.wait_ge(S("gate_out"), 16 * 8)
            a.dma_start(GATE2, gates_dram).then_inc(S("gate_in"), 16)
            for o_ in range(ORDERS):
                for b in range(TB):
                    o = wait_filled(a, ("turn", o_, b))
                    emptied(f(ZT[:, b], o, ACT.Copy), ("turn", o_, b))
            n0 = START["rw_out"]
            a.wait_ge(S("filt_sum"), 8)
            split_tiles(a, make_high, n0, n0 + 4)
            a.wait_ge(S("spectrum_ready"), 4)
            for k in range(KH):
                split_block(Y, k)
            wait_emptied(a, ("idft", 1, 1))
            for k in range(KH):
                split_block(Z2, k)
            split_tiles(a, make_high, n0 + 4, n0 + 10)
            a.wait_ge(S("merged"), 1)
            for k in range(KD):
                split_block(M1, k)
                make_high(a, START["w_out"] + k + 2)
            squares(2)
            split_h(3)
            silus("ffn2_up", 1)
            squares(3)
            squares(4)
            split_h(4)


            def conv_last(p, it):
                bank = LP[(FIRST_PAIR["xbc"] + p) % 2]
                at, bt = PARAMS["conv_w"][0] + 72, PARAMS["conv_b"][0]
                for half in range(2):
                    blk = 4 * it + (2 * p + half)
                    ins = f(XBC[:, blk], bank[:, half * T:half * T + T], ACT.Identity,
                            scale=par[:, bass.ds(blk + at, 1)], bias=par[:, bass.ds(blk + bt, 1)])
                ins.then_inc(S("mid2_ready"), 1)

            pair_loop("xbc", conv_last)
            make_high(a, START["dt"] + 2)
            for at, scale in ((0, 0.125), (4, 1.0)):
                with a.Fori(0, 2) as it:
                    for p in range(2):
                        ahead("qk", at + p, it)
                        a.wait_ge(S("tile_used"), START["qk"] + 2 * (at + p) + 2 + 4 * it)
                        f(G2[:, 2 * it + (at + p)], LP[(FIRST_PAIR["qk"] + p) % 2], ACT.Copy, scale=scale)\
                            .then_inc(S("act_freed_pair"), 1)

            pair_freed(a, "xbc", PAIRS["xbc"] - 1)
            for c in range(3):
                split_tiles(a, make_high, START["v"] + 2 + 2 * c, START["v"] + 4 + 2 * c)
                tell(f(XBC[:, 8 * c:8 * c + 8], XBC[:, 8 * c:8 * c + 8], ACT.Silu), "xbc_ready")
            split_tiles(a, make_high, START["v"] + 8, START["z"] + 2)

            def z_silu(p, it):
                bank = LP[(FIRST_PAIR["z"] + p) % 2]
                f(flat(Z).rearrange("p (a b) -> p a b", b=2 * T)[:, 2 * it + p], bank, ACT.Silu)\
                    .then_inc(S("act_freed_pair"), 1)

            pair_loop("z", z_silu)
            for n in range(9):
                pair_of = (2 * n, 2 * n + 1)
                if n < 8:
                    for hd in pair_of:
                        a.wait_ge(S("neg_abs"), hd + 1)
                        tell(f(NEG[:, hd % 4], NEG[:, hd % 4], ACT.Exp), "neg_exp")
                    if n == 0:
                        a.wait_ge(S("dt_neg"), 1)
                        tell(f(dtf[0:32, 1], dtf[0:32, 1], ACT.Exp), "dt_exp")
                    for hd in pair_of:
                        a.wait_ge(S("neg_exp"), hd + 1)
                        tell(f(NEG[:, hd % 4], NEG[:, hd % 4], ACT.Ln, bias=one_col[:, 0:1]), "neg_log")
                    if n == 0:
                        a.wait_ge(S("dt_exp"), 1)
                        tell(f(dtf[0:32, 1], dtf[0:32, 1], ACT.Ln, bias=one_col[0:32, 0:1]), "dt_log")
                for hd in (2 * n - 2, 2 * n - 1):
                    if n >= 1:
                        o = wait_filled(a, ("stick", hd))
                        if hd >= 4:
                            a.wait_ge(S("job_done"), jobs.index[("attend", (hd - 4) // 2)] + 1)
                        emptied(f(WA[:, hd % 4], o[:, 0:3 * P], ACT.Exp), ("stick", hd))
            a.wait_ge(S("dte_arg"), 1)
            tell(f(dtf[0:32, 4, 0:P], dtf[0:32, 4, 0:P], ACT.Exp), "dt_ready")
            o = wait_filled(a, ("small_turns",))
            emptied(f(SMALL.rearrange("p a b -> p (a b)"), o[:, 0:160], ACT.Copy), ("small_turns",))
            o = wait_filled(a, ("b_turn",))
            emptied(f(BTM, four(o), ACT.Copy), ("b_turn",))
            for g in range(4):
                o = wait_filled(a, ("state", g))
                emptied(f(S0[:, g], o, ACT.Copy), ("state", g))

            def exps(t):
                g, b, half = TURN[t]
                o = wait_filled(a, ("decay_rows", t))
                a.wait_ge(S("decay_arg"), t + 1)
                tell(f(DD[:, t % 2], DD[:, t % 2], ACT.Exp), "decay_exp")
                if b:
                    if t >= 2:
                        wait_filled(a, ("ssm_y", t - 2))
                    tell(f(CE[:, t % 2], four(o), ACT.Exp), "row_exp")

            exps(0)
            for t in range(TURNS):
                if t + 1 < TURNS:
                    exps(t + 1)
                if t % 2:
                    j = t // 2
                    a.wait_ge(S("tile_used"), START["gates2"] + 2 * j + 2)
                    f(G2[:, j], LP[(FIRST_PAIR["gates2"] + j) % 2], ACT.Sigmoid).then_inc(S("act_freed_pair"), 1)
            for g in range(4):
                a.wait_ge(S("gated"), g + 1)
                tell(f(SQ4[:, 4 * g:4 * g + 4], XBC[:, 4 * g:4 * g + 4], ACT.Square), "gy_sq")
            a.dma_start(flat(MX), mem_in).then_inc(S("in_mem"), 16)
            wait_emptied(a, ("group_norm", 2))
            tell(f(CBT.rearrange("p a b c -> p (a b c)"), CBT.rearrange("p a b c -> p (a b c)"), ACT.Sqrt), "gy_root")
            squares(5, START["br_ssm"])
            a.wait_ge(S("ssm_done"), 1)
            n0 = START["br_ssm"]
            for k in range(16):
                split_block(XBC, k, n0 + k - KD if k >= KD else None)
                make_high(a, n0 + k + 2)
                if k >= 8:
                    a.wait_ge(S("h_ready"), KD * 4 + k - 7)
                    tell(f(HM_HI[:, k - 8], HM[:, k - 8], ACT.Copy), "mem_high")
            KM2 = KM.rearrange("p (a b) c -> p a (b c)", b=2)

            def mem_keys(name, j, to):
                a.wait_ge(S("tile_used"), START[name] + 2 * j + 2)
                f(KM2[:, to], LP[(FIRST_PAIR[name] + j) % 2], ACT.Copy).then_inc(S("act_freed_pair"), 1)

            for j in range(2):
                ahead("mem_k0", j)
                mem_keys("mem_k0", j, j)
            a.wait_ge(S("merged"), 2)
            for k in range(KD):
                split_block(M2, k)
                make_high(a, START["mix_out"] + k + 2)
            ahead("mem_k1", 0)
            squares(6, None, False)
            mem_keys("mem_k1", 0, 2)
            ahead("mem_k1", 1)
            root_of(6)
            mem_keys("mem_k1", 1, 3)
            n0 = START["mem_v"]
            make_high(a, n0 + 2)
            make_high(a, n0 + 3)
            squares(7, None, False)
            make_high(a, n0 + 4)
            root_of(7)
            make_high(a, n0 + 5)
            make_high(a, n0 + 6)
            split_h(6)
            for n in range(n0 + 7, n0 + 10):
                make_high(a, n)

            def xa_queries(p, it):
                bank = LP[(FIRST_PAIR["xq"] + p) % 2]
                f(XQ.rearrange("p (a b) c -> p a (b c)", b=2)[:, 2 * it + p], bank, ACT.Copy)\
                    .then_inc(S("act_freed_pair"), 1)

            pair_loop("xq", xa_queries)
            for hd in range(4):
                a.wait_ge(S("xa_max"), hd + 1)
                o = wait_filled(a, ("xa_scores", hd))
                for b in range(TB):
                    ins = f(XP[:, hd, b], o[:, b * T:b * T + T], ACT.Exp, scale=1.0 / 16,
                            bias=stat[:, 0, 2 * hd + b:2 * hd + b + 1])
                emptied(ins, ("xa_scores", hd))
            for hd in range(4):
                o = wait_filled(a, ("xa_turn", hd))
                emptied(f(flat(XT[:, hd % 2]), o, ACT.Copy), ("xa_turn", hd))
                o = wait_filled(a, ("xa_out", hd))
                emptied(f(flat(XO[:, 2 * hd:2 * hd + 2]), o, ACT.Copy), ("xa_out", hd))
            wait_emptied(a, ("xa_out", 3))
            for k in range(KD):
                split_block(XO, k)
                make_high(a, START["xo"] + k + 2)
            squares(8)
            squares(9)
            split_h(7)
            silus("ffn3_up", 2)
            squares(10)
            for c in range(4):
                a.wait_ge(S("x_ready"), 24 + c + 1)
                a.dma_start(out[:, c * 2 * T:(c + 1) * 2 * T], x2[:, c]).then_inc(S("stored"), 16)
            a.wait_ge(S("stored"), 64)

        @block.vector
        def _(v):
            def tt(o, i, j, op):
                return v.tensor_tensor(o, i, j, op)

            def ts(o, i, s1, op0, s2=None, op1=None):
                return v.tensor_scalar(o, i, s1, s2, op0) if op1 is None else v.tensor_scalar(o, i, s1, s2, op0, op1)

            def stt(o, i, s, j, op0, op1):
                return v.scalar_tensor_tensor(out=o, in0=i, scalar=s, in1=j, op0=op0, op1=op1)

            MUL, ADD, SUB, MAX, MIN = ALU.mult, ALU.add, ALU.subtract, ALU.max, ALU.min

            def step(ins):
                link(v, ins, "dve_step")

            def signal(name):
                v.sem_inc(S(name), 1)
                counts[name] += 1

            def signal_emptied(name):
                assert counts["dve_emptied"] == jobs.order[jobs.index[name]][2]
                signal("dve_emptied")

            def inverse_root(i):
                v.wait_ge(S("root_ready"), i + 1)
                link(v, v.reciprocal(rs, root), "root_read")

            def low_of_h(k):
                v.wait_ge(S("h_high"), counts["h_low"] + 1)
                tell(tt(H_LO[:, k], h[:, k], H_HI[:, k].bitcast(F32), SUB), "h_low")

            def low_of_block(src, k):
                v.wait_ge(S("block_high"), counts["block_low"] + 1)
                slot = counts["block_low"] % KD
                tell(tt(H_LO[:, slot], src[:, k], H_HI[:, slot].bitcast(F32), SUB), "block_low")

            def norm(i, dst, src, sem, first_tile=None, split=False):
                if first_tile is not None:
                    make_low(v, first_tile)
                    make_low(v, first_tile + 1)
                inverse_root(i)
                for k in range(KD):
                    ins = stt(dst[:, k], src[:, k], param(NORMS[i], k), rs, MUL, MUL)
                    if sem == "h_ready" or k % 2:
                        tell(ins, sem)
                    if split and k >= 2:
                        low_of_h(k - 2)
                if split:
                    low_of_h(KD - 2)
                    low_of_h(KD - 1)

            def residual(name, scale):
                v.wait_ge(S("tile_used"), tiles_done(name))
                for c in range(4):
                    tell(stt(x2[:, c], ACC[c], scale, x2[:, c], MUL, ADD), "x_ready")
                v.wait_ge(S("x_ready"), counts["x_ready"])
                signal("acc_read")

            def post_norm(i):
                inverse_root(i)
                scaled = []
                for k in range(KD):
                    ins = stt(h[:, k], ACC[k // 2][:, (k % 2) * T:(k % 2) * T + T], param(NORMS[i], k), rs, MUL, MUL)
                    scaled.append(tell(ins, "dve_step" if k < KD - 1 else "acc_read"))
                for c in range(4):
                    v.wait_ge(S("dve_step" if c < 3 else "acc_read"), scaled[2 * c + 1])
                    tell(tt(x2[:, c], x2[:, c], flat(h[:, 2 * c:2 * c + 2]), ADD), "x_ready")

            def ffn_mul(name, index):
                n0, fp = START[name], FIRST_PAIR[name]

                def low_of_act(j, it=None):
                    value = KF * index + j + 1
                    v.wait_ge(S("act_high"), value if it is None else value + 2 * it)
                    at = j if it is None else 2 * it + j
                    tt(ACT_LO[:, at], act_raw[:, j % 2], ACT_HI[:, at].bitcast(F32), SUB).then_inc(S("act_low"), 1)

                def one(j, it=None):
                    for n in (n0 + 2 * j + 2, n0 + 2 * j + 3):
                        make_low(v, n, it)
                    value = KF * index + j + 1
                    v.wait_ge(S("silu_ready"), value if it is None else value + 2 * it)
                    if j >= 2:
                        v.wait_ge(S("act_low"), value - 2 if it is None else value - 2 + 2 * it)
                    tt(act_raw[:, j % 2], gate_tmp[:, j % 2], LP[(fp + j) % 2][:, T:2 * T], MUL)\
                        .then_inc(S("dve_freed_pair"), 1)
                    if it is not None or j:
                        low_of_act(j - 1, it)

                one(0)
                one(1)
                with v.Fori(0, (KF - 2) // 2) as it:
                    one(2, it)
                    one(3, it)
                low_of_act(KF - 1)
                down = n0 + 2 * KF
                split_tiles(v, make_low, down + 2, down + KF + (0 if name == "ffn3_up" else 2))
                counts["dve_freed_pair"] += KF

            def ahead(name, j, it=None):
                for n in (START[name] + 2 * j + 2, START[name] + 2 * j + 3):
                    make_low(v, n, it)

            tell(v.memset(eps, EPS), "consts")
            tell(v.memset(one_col, 1.0), "consts")

            v.wait_ge(S("in_par"), 32)
            at_p, at_m, at_n = (PARAMS[n][0] for n in ("tap_prev", "tap_mid", "tap_next"))
            step(ts(c_mid[:, 0:16], par[:, at_p:at_p + 16], -1.0, MUL, 1.0, ADD))
            step(tt(c_mid[:, 0:16], c_mid[:, 0:16], par[:, at_n:at_n + 16], SUB))
            tell(v.tensor_copy(c_mid[:, 16:28], par[:, at_m + 16:at_m + 28]), "coefs")
            step(ts(c_ka, par[:, PARAMS["k_a"][0]:PARAMS["k_a"][0] + 4], -1.0, MUL, 1.0, ADD))
            step(ts(c_fb[0:64], par[0:64, PARAMS["sin_b"][0]:PARAMS["sin_b"][0] + 2], param("sin_f", 0, 64), MUL))
            v.wait_ge(S("coefs"), 1)
            signal("coefs")
            for c in range(4):
                v.wait_ge(S(f"in_x{c}"), 16)
            norm(0, h, x, "h_ready", START["ffn1_up"], True)
            v.wait_ge(S("c_a_exp"), 1)
            step(ts(c_a[0:32], c_a[0:32], -1.0, MUL))
            ffn_mul("ffn1_up", 0)
            residual("ffn1_down", 0.5)
            norm(1, h, x, "h_ready", None, True)

            def taps(p, it):
                bank = LP[(FIRST_PAIR["conv_in"] + p) % 2]
                v.wait_ge(S("mid_ready"), 2 * it + (p + 1))
                for half in range(2):
                    blk = 4 * it + (2 * p + half)
                    src = bank[:, half * T:half * T + T]
                    stt(U[:, blk, 1:T], src[:, 0:T - 1], par[:, bass.ds(blk + at_p, 1)], U[:, blk, 1:T], MUL, ADD)\
                        .then_inc(S("tap_step"), 1)
                v.wait_ge(S("tap_step"), 4 * it + (2 * p + 2))
                for half in range(2):
                    blk = 4 * it + (2 * p + half)
                    src = bank[:, half * T:half * T + T]
                    ins = stt(U[:, blk, 0:T - 1], src[:, 1:T], par[:, bass.ds(blk + at_n, 1)], U[:, blk, 0:T - 1], MUL, ADD)
                ins.then_inc(S("dve_freed_pair"), 1)

            with v.Fori(0, 3) as it:
                for p in range(2):
                    ahead("conv_in", p, it)
                    taps(p, it)
            ahead("conv_in", 6)
            taps(0, 3)
            taps(1, 3)
            counts["dve_freed_pair"] += 8
            v.wait_ge(S("dve_freed_pair"), counts["dve_freed_pair"])

            for q in range(KH):
                ins = ts(KK[:, q], U[:, 4 + q], param("k_k", q), MUL)
            tell(ins, "kk_raw")
            for half in range(2):
                o = wait_filled(v, ("key_norm", half))
                emptied(ts(flat(BON[:, 2 * half:2 * half + 2]), o, 1e-24, MAX), ("key_norm", half))
            v.wait_ge(S("kk_root"), 1)
            step(v.reciprocal(flat(BON), flat(BON)))
            step(tt(flat(KK), flat(KK), flat(BON), MUL))
            v.wait_ge(S("in_tab"), 16)

            def prepare(d, i):
                def R(s):
                    return s[:, :, ::-1] if d else s

                if i == 0:
                    wait_emptied(v, ("rate_lora", d, 1))
                    tell(v.tensor_tensor_scan(flat(C), table("keep32"), flat(L), 0.0, MUL, ADD), "cum_ready")
                    v.wait_ge(S("cum_ready"), 2 * d + 1)
                elif i == 1:
                    tell(tt(flat(EX), flat(C), flat(L), SUB), "cum_ready")
                    v.wait_ge(S("cum_ready"), 2 * d + 2)
                elif i == 2:
                    for q in range(KH):
                        ins = ts(L[:, q], A[:, q], param("k_a", q), MUL, c_ka[:, q:q + 1], ADD)
                    step(ins)
                elif i == 3:
                    step(tt(L, L, R(U[:, 4:8]), MUL))
                else:
                    step(tt(A, A, R(KK), MUL))

            def hyena_taps(r):
                v.wait_ge(S("hyena_mid"), r + 1)
                for half in range(2):
                    blk, src = 16 + 2 * r + half, GB[:, half * T:half * T + T]
                    ins = stt(U[:, blk, 1:T], src[:, 0:T - 1], param("tap_prev", blk), U[:, blk, 1:T], MUL, ADD)
                step(ins)
                for half in range(2):
                    blk, src = 16 + 2 * r + half, GB[:, half * T:half * T + T]
                    ins = stt(U[:, blk, 0:T - 1], src[:, 1:T], param("tap_next", blk), U[:, blk, 0:T - 1], MUL, ADD)
                tell(ins, "hyena_conv")
                v.wait_ge(S("hyena_conv"), r + 1)

            for i in range(5):
                prepare(0, i)
            for d in range(2):
                v.wait_ge(S("exps"), 3 * d + 3)
                for q in range(KH):
                    b2 = "p (b t) -> p b t"
                    kk_q, r_q = (KK[:, q, ::-1], U[:, q, ::-1]) if d else (KK[:, q, :], U[:, q, :])
                    tt(AR[:, q, :, 0, :], kk_q.rearrange(b2, b=TB), EX[:, q].rearrange(b2, b=TB), MUL)
                    tt(AR[:, q, :, 1, :], r_q.rearrange(b2, b=TB), EP[:, q].rearrange(b2, b=TB), MUL)
                step(v.tensor_copy(EEND.rearrange("p (a b) -> p a b", a=KH), EP[:, :, CH - 1:T:CH]))
                tt(flat(KA), flat(L), flat(EN), MUL)
                tell(tt(flat(BE), flat(A), flat(EN), MUL), "dir_ready")
                v.wait_ge(S("dir_ready"), d + 1)
                for u in range(4):
                    for e in range(2):
                        for name, dst in (("beta_pairs", BX), ("kappa_pairs", KX)):
                            o = wait_filled(v, (name, d, u, e))
                            emptied(tt(dst[:, u, e::2].rearrange("p e a b -> p e (a b)"),
                                       o.rearrange("p (e a) -> p e a", e=2), over(table("upper"), 2), MUL),
                                    (name, d, u, e))
                    wait_emptied(v, ("kappa_pairs", d, u, 1))
                    tt(TT[:, u], BX[:, u, :, 0, :], over(level_t[:, 0], 4), MUL)
                    for e in range(2):
                        o = wait_filled(v, ("alpha_beta", d, u, e))
                        emptied(tt(TN[:, u, e::2], o[:, 0:T].rearrange("p (a b) -> p a b", a=2),
                                   over(table("level_n"), 2), MUL), ("alpha_beta", d, u, e))
                    wait_emptied(v, ("alpha_beta", d, u, 1))
                    tt(TT[:, u], TT[:, u], over(ident, 4), ADD)
                    tell(tt(TN[:, u], TN[:, u], over(ident, 4), ADD), "first_level")
                if d:
                    v.wait_ge(S("bon_ready"), 2)
                    for q in range(KH):
                        ins = stt(BON[:, q], U[:, q], param("r_k", q), BON[:, q], MUL, MUL)
                    step(ins)
                for level in range(2, 6):
                    for u in range(4):
                        if level < 5:
                            o = wait_filled(v, ("inverse", d, level, u))
                            emptied(tt(flat(TN[:, u]), flat(TN[:, u]), o, SUB), ("inverse", d, level, u))
                        o = wait_filled(v, ("inverse_t", d, level, u))
                        if level < 5:
                            emptied(tt(flat(TT[:, u]), flat(TT[:, u]), o, SUB), ("inverse_t", d, level, u))
                        else:
                            emptied(tt(flat(TT[:, u]), o, flat(TT[:, u]), SUB), ("inverse_t", d, level, u))
                ends = EEND.rearrange("p (a b) -> p a b", a=KH)
                for c in range(NCH):
                    b, r = c // 4, slice(CH * (c % 4), CH * (c % 4) + CH)
                    if c % 4 == 3:
                        wait_filled(v, ("chain", d, b, 1))
                    else:
                        v.wait_ge(S("sa_psum"), 6 * d + 3 * b + c % 4 + 1)
                    for e in range(2):
                        bank = MB[jobs.index[("chain", d, b, e)] % BANKS]
                        ins = v.tensor_copy(SA[r, b, e], bank[r, 0:T])
                    tell(ins, "sa_ready")
                    if c % 4 == 3:
                        v.wait_ge(S("sa_ready"), counts["sa_ready"])
                        for e in range(2):
                            signal_emptied(("chain", d, b, e))
                    if d == 0 and c < 5:
                        prepare(1, c)
                    if c in (2, 5):
                        hyena_taps(3 * d + c // 3)
                    if c == NCH - 1:
                        break
                    to = HS[:, c + 1].rearrange("p (a b) -> p a b", a=KH)
                    st = LP[c % 2][:, 0:KH * 64].rearrange("p (a b) -> p a b", a=KH)
                    if c:
                        fr = HS[:, c].rearrange("p (a b) -> p a b", a=KH)
                        step(tt(to, fr, ends[:, :, c:c + 1].broadcast_to([P, KH, 64]), MUL))
                        v.wait_ge(S("state_psum"), 7 * d + c + 1)
                        tell(tt(to, to, st, ADD), "state_ready")
                    else:
                        v.wait_ge(S("state_psum"), 7 * d + c + 1)
                        tell(v.tensor_copy(to, st), "state_ready")
                    v.wait_ge(S("state_ready"), counts["state_ready"])
                hyena_taps(3 * d + 2)
                for pr in range(2):
                    o = wait_filled(v, ("y", d, pr)).rearrange("p (a b) -> p a b", a=2)
                    to = Y[:, 2 * pr:2 * pr + 2]
                    if d:
                        emptied(tt(to, to, o[:, :, ::-1], ADD), ("y", d, pr))
                    else:
                        emptied(v.tensor_copy(to, o), ("y", d, pr))
            for half in range(2):
                o = wait_filled(v, ("mean", half))
                yy = flat(Y[:, 2 * half:2 * half + 2])
                emptied(stt(yy, o, -1.0 / 64, yy, MUL, ADD), ("mean", half))
            for half in range(2):
                o = wait_filled(v, ("var", half))
                emptied(ts(flat(BE[:, 2 * half:2 * half + 2]), o, 1.0 / 64, MUL, GN_EPS, ADD), ("var", half))
            v.wait_ge(S("y_root"), 1)
            step(v.reciprocal(flat(BE), flat(BE)))
            step(tt(flat(Y), flat(Y), flat(BE), MUL))
            for q in range(KH):
                ins = ts(Y[:, q], Y[:, q], param("ln_w", q), MUL, param("ln_b", q), ADD)
            step(ins)
            for half in range(2):
                o = wait_filled(v, ("bonus", half))
                s2 = slice(2 * half, 2 * half + 2)
                emptied(tt(flat(L[:, s2]), o, flat(U[:, 8 + 2 * half:10 + 2 * half]), MUL), ("bonus", half))
            wait_emptied(v, ("bonus", 1))
            step(tt(flat(Y), flat(Y), flat(L), ADD))
            tell(tt(flat(Y), flat(Y), flat(G), MUL), "rwkv_done")
            v.wait_ge(S("rwkv_done"), 1)

            two_pi_hi = 6.28125
            two_pi_lo = 2 * math.pi - two_pi_hi
            for i in range(2):
                o = wait_filled(v, ("sin", i))
                if i:
                    v.wait_ge(S("sin_ready"), 1)
                emptied(ts(sin_in[0:64], o[0:64, 0:T], param("sin_f", 0, 64), MUL, c_fb[0:64, i:i + 1], ADD), ("sin", i))
                wait_emptied(v, ("sin", i))
                step(ts(sin_k[0:64], sin_in[0:64], 1 / (2 * math.pi), MUL, 12582912.0, ADD))
                step(ts(sin_k[0:64], sin_k[0:64], -12582912.0, ADD))
                step(stt(sin_in[0:64], sin_k[0:64], -two_pi_hi, sin_in[0:64], MUL, ADD))
                step(stt(sin_in[0:64], sin_k[0:64], -two_pi_lo, sin_in[0:64], MUL, ADD))
                if i == 0:
                    step(v.memset(sin_out[64:65, 1], 1.0))
                tell(ts(sin_in[0:64], sin_in[0:64], 3.1415925, MIN, -3.1415925, MAX), "sin_args")
            for b in range(TB):
                v.wait_ge(S("env_ready"), b + 1)
                for c in range(4):
                    o = wait_filled(v, ("filter", b, c))
                    emptied(tt(env[:, b, c], o, env[:, b, c], MUL), ("filter", b, c))
            wait_emptied(v, ("filter", 1, 3))
            for o_ in range(ORDERS):
                step(v.memset(env[0:1, 0, 2 + o_], 0.0))
            signal("filt_made")
            for o_ in range(ORDERS):
                for b in range(TB):
                    tell(tt(fsum[:, o_, b], env[:, b, o_], env[:, b, 2 + o_], ADD), "filt_sum")
                    tell(tt(fdiff[:, o_, b], env[:, b, o_], env[:, b, 2 + o_], SUB), "filt_sum")
            for o_ in range(ORDERS):
                v.wait_ge(S("filt_root"), o_ + 1)
                step(v.reciprocal(fnorm[:, o_], fnorm[:, o_]))
                signal_emptied(("filter_norm", o_))
                for m_ in range(NFREQ):
                    o = wait_filled(v, ("filter_dft", o_, m_))
                    emptied(tt(FK[:, o_, m_], o, fnorm[:, o_], MUL), ("filter_dft", o_, m_))
                wait_emptied(v, ("filter_dft", o_, 3))
                step(v.tensor_copy(FKP[:, o_], FK[:, o_, 0]))
                step(v.memset(FK[0:1, o_, 2], 0.0))
                o = wait_filled(v, ("nyquist", o_))
                emptied(tt(FKP[0:1, o_], o[0:1], fnorm[0:1, o_], MUL), ("nyquist", o_))
            wait_emptied(v, ("nyquist", 1))
            for o_ in range(ORDERS):
                for pr in range(2):
                    re, im = FK[:, o_, pr], FK[:, o_, 2 + pr]
                    re_im = FKP[:, o_] if pr == 0 else re
                    o = wait_filled(v, ("dft", o_, pr))
                    tt(ZF[:, 0], o, re, MUL)
                    emptied(tt(ZF[:, 1], o, im, MUL), ("dft", o_, pr))
                    o = wait_filled(v, ("dft", o_, 2 + pr))
                    tt(ZF[:, 2], o, im, MUL)
                    emptied(tt(ZF[:, 3], o, re_im, MUL), ("dft", o_, 2 + pr))
                    wait_emptied(v, ("dft", o_, 2 + pr))
                    tt(YF[:, pr], ZF[:, 0], ZF[:, 2], SUB)
                    tell(tt(YF[:, 2 + pr], ZF[:, 1], ZF[:, 3], ADD), "spectrum_ready")
                    v.wait_ge(S("spectrum_ready"), counts["spectrum_ready"])
                if o_:
                    make_low(v, START["rw_out"])
                    make_low(v, START["rw_out"] + 1)
                    for k in range(KH):
                        low_of_block(Y, k)
                zin, dst, xg = (U[:, 24:28], Z1, U[:, 16:20]) if o_ == 0 else (Z1, Z2, U[:, 20:24])
                for half in range(2):
                    o = wait_filled(v, ("idft", o_, half))
                    for qq in range(2):
                        q = 2 * half + qq
                        step(stt(dst[:, q], zin[:, q], param("hy_d", 4 * o_ + q), o[:, qq * T:qq * T + T], MUL, ADD))
                    s2 = slice(2 * half, 2 * half + 2)
                    emptied(tt(flat(dst[:, s2]), flat(dst[:, s2]), flat(xg[:, s2]), MUL), ("idft", o_, half))
                    wait_emptied(v, ("idft", o_, half))
            m12 = M1.rearrange("p (a b) c -> p a (b c)", a=4)

            def gated(name, gate, prev, sem, free=True):
                v.wait_ge(S("tile_used"), tiles_done(name))
                for c in range(4):
                    ins = tt(gate[:, c], ACC[c], gate[:, c], MUL)
                tell(ins, "acc_read")
                v.wait_ge(S("acc_read"), counts["acc_read"])
                if prev is not None:
                    dst, other = prev
                    for c in range(4):
                        ins = tt(dst[:, c], gate[:, c], other[:, c], ADD)
                    tell(ins, sem)

            n0 = START["rw_out"]
            split_tiles(v, make_low, n0 + 2, n0 + 4)
            for k in range(KH):
                low_of_block(Z2, k)
            make_low(v, n0 + 4)
            v.wait_ge(S("gate_in"), 16)
            gated("rw_out", GATE2[:, 4:8], None, None)
            split_tiles(v, make_low, n0 + 5, n0 + 10)
            gated("hy_out", GATE2[:, 0:4], (m12, GATE2[:, 4:8]), "merged")
            for k in range(KD):
                low_of_block(M1, k)
                make_low(v, START["w_out"] + k + 2)
            residual("w_out", 1.0)
            norm(2, h, x, "h_ready", None, True)
            ffn_mul("ffn2_up", 1)
            residual("ffn2_down", 0.5)
            norm(3, x, x, "x_ready")
            norm(4, h, x, "h_ready", None, True)

            at_w = PARAMS["conv_w"][0]

            def taps4(p, it):
                bank = LP[(FIRST_PAIR["xbc"] + p) % 2]
                v.wait_ge(S("mid2_ready"), 2 * it + (p + 1))
                for s in (1, 2, 3):
                    if s > 1:
                        v.wait_ge(S("tap4_step"), 4 * it + (2 * p + s - 1))
                    for half in range(2):
                        blk = 4 * it + (2 * p + half)
                        src = bank[:, half * T:half * T + T]
                        ins = stt(XBC[:, blk, s:T], src[:, 0:T - s], par[:, bass.ds(blk + (at_w + 24 * (3 - s)), 1)],
                                  XBC[:, blk, s:T], MUL, ADD)
                    ins.then_inc(S("tap4_step") if s < 3 else S("dve_freed_pair"), 1)

            with v.Fori(0, 6) as it:
                for p in range(2):
                    ahead("xbc", p, it)
                    taps4(p, it)
            counts["dve_freed_pair"] += 12
            make_low(v, START["dt"] + 2)
            v.wait_ge(S("tile_used"), tiles_done("dt"))
            bank = LP[FIRST_PAIR["dt"] % 2]
            r = slice(0, 32)
            tell(ts(dtf[r, 0], bank[r, 0:T], param("dt_bias", 0, 32), ADD), "dve_freed_pair")
            split_tiles(v, make_low, START["qk"] + 2, START["z"] + 2)
            v.wait_ge(S("tile_used"), tiles_done("v"))
            for b in range(TB):
                for half in range(2):
                    ins = v.tensor_copy(V2[:, b, half * HY:half * HY + HY], ACC[2 * b + half])
            tell(ins, "acc_read")
            split_tiles(v, make_low, START["z"] + 2, START["z"] + COUNT["z"])
            v.wait_ge(S("dve_freed_pair"), counts["dve_freed_pair"])
            tell(stt(dtf[r, 1], dtf[r, 0], -1.0, dtf[r, 0], MUL, MIN), "dt_neg")
            for n in range(8 + 2):
                if n == 1:
                    v.wait_ge(S("dt_log"), 1)
                    step(stt(dtf[r, 0], dtf[r, 0], 0.0, dtf[r, 1], MAX, ADD))
                    step(ts(dtf[r, 3], dtf[r, 0], c_a[r, 0:1], MUL))
                    step(v.memset(dtf[r, 5], 1.0))
                    step(v.memset(dtf[r, 5, 0:T:P], 0.0))
                    step(v.tensor_tensor_scan(dtf[r, 2], dtf[r, 5], dtf[r, 3], 0.0, MUL, ADD))
                    tell(ts(dtf[r, 4, 0:P], dtf[r, 2, 0:P], -1.0, MUL, dtf[r, 2, P - 1:P], ADD), "dte_arg")
                if n < 8:
                    for hd in (2 * n, 2 * n + 1):
                        o = wait_filled(v, ("scores", hd))
                        if hd >= 4:
                            v.wait_ge(S("log_ready"), hd - 3)
                        step(ts(SP[:, hd % 4], o[:, 0:3 * P], 0.0, MAX))
                        tell(stt(NEG[:, hd % 4], SP[:, hd % 4], -2.0, o[:, 0:3 * P], MUL, ADD), "neg_abs")
                    for hd in (2 * n, 2 * n + 1):
                        v.wait_ge(S("neg_log"), hd + 1)
                        emptied(tt(SP[:, hd % 4], SP[:, hd % 4], NEG[:, hd % 4], ADD), ("scores", hd))
                if n >= 2:
                    o = wait_filled(v, ("attend", n - 2))
                    emptied(v.tensor_copy(OT[:, n - 2], o[:, 0:T]), ("attend", n - 2))
            for g0 in range(0, 4, 2):
                o = wait_filled(v, ("cb", g0))
                emptied(tt(CBT[:, g0:g0 + 2].rearrange("p a b c -> p (a b) c"), four(o), over(table("until"), 4), MUL),
                        ("cb", g0))
            wait_emptied(v, ("small_turns",))
            for b in range(TB):
                for c in range(4):
                    o = wait_filled(v, ("x_turn", b, c))
                    emptied(tt(XTM[:, b, c * HY:c * HY + HY].rearrange("p (a b) -> p a b", b=64),
                               o.rearrange("p (a b) -> p a b", b=64), along(SMALL[:, 2 + b, 8 * c:8 * c + 8], 64), MUL),
                            ("x_turn", b, c))
            wait_emptied(v, ("x_turn", 1, 3))
            tell(tt(XD.rearrange("p (a b) -> p a b", b=64), XTM[:, 0].rearrange("p (a b) -> p a b", b=64),
                    along(SMALL[:, 4], 64), MUL), "xd_ready")

            def decay_args(t):
                g, b, half = TURN[t]
                o = wait_filled(v, ("decay_rows", t))
                if t >= 2:
                    v.wait_ge(S("ssm_mix_ready"), t - 1)
                for i in range(4):
                    hd = 8 * g + 4 * half + i
                    ins = ts(DD[:, t % 2, i], o[:, i * P:i * P + P], SMALL[:, b, hd:hd + 1], SUB, 0.0, MIN)
                tell(ins, "decay_arg")

            def rows_done(t):
                g, b, half = TURN[t]
                if b:
                    v.wait_ge(S("row_exp"), 2 * g + half + 1)
                    tell(tt(CE[:, t % 2], CE[:, t % 2], over(XBC[:, 20 + g, P:T], 4), MUL), "row_ready")
                v.wait_ge(S("decay_arg"), t + 1)
                signal_emptied(("decay_rows", t))

            def add_y(t):
                g, b, half = TURN[t]
                o = wait_filled(v, ("ssm_y", t))
                for qq in range(2):
                    q = 4 * g + 2 * half + qq
                    yy = XBC[:, q, b * P:b * P + P]
                    ins = stt(yy, yy, param("d_skip", q), o[:, qq * P:qq * P + P], MUL, ADD)
                emptied(ins, ("ssm_y", t))
                if b and half:
                    wait_emptied(v, ("ssm_y", t))
                    tell(tt(flat(XBC[:, 4 * g:4 * g + 4]), flat(XBC[:, 4 * g:4 * g + 4]), flat(Z[:, 4 * g:4 * g + 4]), MUL),
                         "gated")

            decay_args(0)
            rows_done(0)
            for t in range(TURNS):
                g, b, half = TURN[t]
                if t + 1 < TURNS:
                    decay_args(t + 1)
                v.wait_ge(S("decay_exp"), t + 1)
                tell(tt(DM[:, t % 2], DD[:, t % 2], over(CBT[:, g, b], 4), MUL), "ssm_mix_ready")
                if t:
                    add_y(t - 1)
                if t + 1 < TURNS:
                    rows_done(t + 1)
            add_y(TURNS - 1)
            cbt4 = CBT.rearrange("p a b c -> p a (b c)")
            for g0 in range(0, 4, 2):
                o = wait_filled(v, ("group_norm", g0))
                emptied(ts(flat(cbt4[:, g0:g0 + 2]), o, 1.0 / 512, MUL, EPS, ADD), ("group_norm", g0))
            v.wait_ge(S("gy_root"), 1)
            step(v.reciprocal(flat(cbt4), flat(cbt4)))
            for q in range(16):
                ins = stt(XBC[:, q], XBC[:, q], param("g_ssm", q), cbt4[:, q // 4], MUL, MUL)
            tell(ins, "ssm_done")
            n0 = START["br_ssm"]
            make_low(v, n0)
            make_low(v, n0 + 1)
            pair_freed(v, "gates2", 7)
            gated("br_att", G2[:, 0:4], None, None)
            n0 = START["br_ssm"]
            for k in range(16):
                low_of_block(XBC, k)
                make_low(v, n0 + k + 2)
                if k == 1:
                    inverse_root(5)
                if 2 <= k < 2 + KD:
                    tell(stt(HM[:, k - 2], MX[:, k - 2], param("g_mem", k - 2), rs, MUL, MUL), "h_ready")
                if k >= 8:
                    v.wait_ge(S("mem_high"), k - 7)
                    tell(tt(HM_LO[:, k - 8], HM[:, k - 8], HM_HI[:, k - 8].bitcast(F32), SUB), "mem_low")
            ahead("mem_k0", 0)
            gated("br_ssm", G2[:, 4:8], (M2.rearrange("p (a b) c -> p a (b c)", a=4), G2[:, 0:4]), "merged")
            ahead("mem_k0", 1)
            for k in range(KD):
                low_of_block(M2, k)
                make_low(v, START["mix_out"] + k + 2)
            ahead("mem_k1", 0)
            ahead("mem_k1", 1)
            post_norm(6)

            n0 = START["mem_v"]
            split_tiles(v, make_low, n0 + 2, n0 + 6)
            norm(7, h, x, "h_ready", None, True)
            split_tiles(v, make_low, n0 + 6, n0 + 10)
            v.wait_ge(S("tile_used"), tiles_done("mem_v"))
            for b in range(TB):
                for half in range(2):
                    ins = v.tensor_copy(VM[:, b, half * HY:half * HY + HY], ACC[2 * b + half])
            tell(ins, "acc_read")
            split_tiles(v, make_low, START["xq"] + 2, START["xo"] + 2)
            for hd in range(4):
                o = wait_filled(v, ("xa_scores", hd))
                s2 = slice(2 * hd, 2 * hd + 2)
                step(v.tensor_reduce(stat[:, 1, s2], o.rearrange("p (a b) -> p a b", a=2), AX.X, MAX))
                tell(ts(stat[:, 0, s2], stat[:, 1, s2], -1.0 / 16, MUL), "xa_max")
            for hd in range(4):
                s2 = slice(2 * hd, 2 * hd + 2)
                wait_emptied(v, ("xa_scores", hd))
                step(v.tensor_reduce(stat[:, 1, s2], XP[:, hd], AX.X, ADD))
                step(v.reciprocal(stat[:, 2, s2], stat[:, 1, s2]))
                tell(tt(XP[:, hd], XP[:, hd], along(stat[:, 2, s2], T), MUL), "xa_probs")
            for k in range(KD):
                low_of_block(XO, k)
                make_low(v, START["xo"] + k + 2)
            post_norm(8)
            norm(9, h, x, "h_ready", None, True)
            ffn_mul("ffn3_up", 2)
            post_norm(10)

        @block.gpsimd
        def _(g_):
            def high_of_act(name, index):
                base = PAIR_OWNER[FIRST_PAIR[name]][1]
                with g_.Fori(0, KF // 2) as it:
                    for p in range(2):
                        g_.wait_ge(S("dve_freed_pair"), 2 * it + (base + p + 1))
                        g_.tensor_copy(ACT_HI[:, 2 * it + p], act_raw[:, p]).then_inc(S("act_high"), 1)

            high_of_act("ffn1_up", 0)
            for d in range(2):
                g_.wait_ge(S("dir_ready"), d + 1)
                ends = EEND.unsqueeze(2).broadcast_to([P, KH * NCH, CH])
                for dst, src in ((BH, BE), (KHAT, KA)):
                    ins = g_.tensor_tensor(flat(dst).rearrange("p (a b) -> p a b", b=CH),
                                           flat(src).rearrange("p (a b) -> p a b", b=CH), ends, ALU.mult)
                tell(ins, "hats_ready")
                if d:
                    ins = g_.tensor_tensor(BON, BON, L[:, :, ::-1], ALU.add)
                else:
                    ins = g_.tensor_copy(flat(BON), flat(L))
                tell(ins, "bon_ready")
                for level in range(2, 6):
                    for u in range(4):
                        wait_emptied(g_, ("kappa_pairs", d, u, 1))
                        if level > 2 or u >= 2:
                            prev = ("product", d, level, u - 2) if u >= 2 else ("product", d, level - 1, u + 2)
                            g_.wait_ge(S("job_done"), jobs.index[prev] + 1)
                        else:
                            g_.wait_ge(S("job_done"), jobs.index[("kappa", d, 1)] + 1)
                        tell(g_.tensor_tensor(BT[:, u % 2], BX[:, u, :, 0, :], over(level_t[:, level - 1], 4), ALU.mult),
                             "off_diagonal")
            high_of_act("ffn2_up", 1)
            def log_rest(hd):
                wait_emptied(g_, ("scores", hd))
                if hd >= 4:
                    g_.wait_ge(S("job_done"), jobs.index[("stick", hd - 4)] + 1)
                tell(g_.tensor_tensor(LM[:, hd % 4], SP[:, hd % 4], table("neg_causal"), ALU.mult), "log_ready")

            def weights(hd):
                wait_emptied(g_, ("stick", hd))
                tell(g_.tensor_tensor(WA[:, hd % 4], WA[:, hd % 4], table("causal"), ALU.mult), "stick_weights")

            for n in range(9):
                if n < 8:
                    log_rest(2 * n)
                    log_rest(2 * n + 1)
                if n:
                    weights(2 * n - 2)
                    weights(2 * n - 1)
            high_of_act("ffn3_up", 2)


def blocks(m, rows=P):
    return m.reshape(m.shape[0] // P, P, m.shape[1] // P, P).transpose(0, 2, 1, 3)


def weight_stream(i):
    def pad(m, cols):
        return np.concatenate([m, np.zeros((m.shape[0], cols - m.shape[1]), m.dtype)], 1)

    def by_output(m):
        b = blocks(m)
        return b.transpose(1, 2, 0, 3).reshape(b.shape[1], P, D)

    def by_input(m):
        return m.reshape(m.shape[0] // P, P, D)

    def up(m):
        t = by_output(m)
        return np.stack([t[:KF], t[KF:]], 1).reshape(2 * KF, P, D)

    w1, w2 = i["w_in"], i["w_in_2"][0]
    hy, rw = 3 * HY, 3 * HY + 256 + 160
    rwkv = pad(w1[:, hy:hy + rw], 16 * P)
    at = np.cumsum([0, D, D, D, 2 * D, 3 * D, 32, D, D])
    q, k, v, z, xbc, dt, ga, gs = (w2[:, at[n]:at[n + 1]] for n in range(8))
    hyena, gates = by_output(w1[:, :hy]), by_output(w1[:, hy + rw:])
    parts = {
        "ffn1_up": up(i["ffn1_w_gu"]), "ffn1_down": by_input(i["ffn1_w_down"]),
        "conv_in": by_output(rwkv), "hyena_a": hyena[:6], "hyena_b": hyena[6:],
        "gates_a": gates[:6], "gates_b": gates[6:8], "gates_c": gates[8:],
        "hy_out": by_input(i["hy_out"]), "rw_out": by_input(i["rw_out"]), "w_out": by_input(i["w_out"]),
        "ffn2_up": up(i["ffn2_w_gu"]), "ffn2_down": by_input(i["ffn2_w_down"]),
        "xbc": by_output(xbc), "dt": by_output(pad(dt, P)), "qk": np.concatenate([by_output(q), by_output(k)]),
        "v": by_input(v), "z": by_output(z), "gates2": np.concatenate([by_output(ga), by_output(gs)]),
        "br_att": by_input(i["w_br_att_2"][0]), "br_ssm": by_input(i["w_br_ssm_2"][0]),
        "mix_out": by_input(i["w_mix_out_2"][0]),
        "mem_k0": by_output(i["w_xkv_2"][0][:, :D // 2]), "mem_k1": by_output(i["w_xkv_2"][0][:, D // 2:D]), "mem_v": by_input(i["w_xkv_2"][0][:, D:]),
        "xq": by_output(i["w_xq_2"][0]), "xo": by_input(i["w_xo_2"][0]),
        "ffn3_up": up(i["w_gu_2"][0]), "ffn3_down": by_input(i["w_down_2"][0]),
    }
    for name, tiles, _ in SEGMENTS:
        assert parts[name].shape == (tiles, P, D), name
    return np.concatenate([parts[name] for name, _, _ in SEGMENTS])


def parameters(i):
    def cols(v):
        return np.reshape(v, (-1, P)).T

    def rows(v):
        v = np.reshape(v, (-1, v.shape[-1])).T
        return np.concatenate([v, np.zeros((P - v.shape[0], v.shape[1]), v.dtype)])

    mu = np.concatenate([i["rw_mu"], np.zeros((2, 16 * P - i["rw_mu"].shape[1]), np.float32)], 1)
    taps = i["hy_conv_w"]
    zero = np.zeros((P, 16), np.float32)
    p = {n: cols(i[n]) for n in ("ffn1_norm", "mix_norm", "ffn2_norm", "final_norm")}
    p |= {n: cols(i[n + "_2"]) for n in ("g_pre_mix", "g_post_mix", "g_pre_xa", "g_mem", "g_post_xa", "g_pre_ffn",
                                         "g_post_ffn", "conv_w", "conv_b")}
    p["tap_prev"] = np.concatenate([cols(mu[0]), cols(taps[0])], 1)
    p["tap_mid"] = np.concatenate([zero, cols(taps[1])], 1)
    p["tap_next"] = np.concatenate([cols(mu[1]), cols(taps[2])], 1)
    p["tap_bias"] = np.concatenate([zero, cols(i["hy_conv_b"])], 1)
    p |= {"hy_d": cols(i["hy_bias_d"]), "w0": cols(i["rw_w0"]), "a0": cols(i["rw_a0"]), "k_k": cols(i["rw_k_k"]),
          "k_a": cols(i["rw_k_a"]), "r_k": cols(i["rw_r_k"]), "ln_w": cols(i["rw_ln_w"]), "ln_b": cols(i["rw_ln_b"]),
          "g_ssm": cols(i["g_ssm_norm_2"]), "d_skip": cols(np.repeat(i["d_skip_2"][0], 64)),
          "sin_b": rows(np.stack([i["hy_ffn_b1"], i["hy_ffn_b2"]])), "sin_f": rows(i["hy_sin_freq"]),
          "dt_bias": rows(i["dt_bias_2"][0]), "a_log": rows(i["a_log_2"][0])}
    for name, (_, n) in PARAMS.items():
        assert p[name].shape == (P, n), (name, p[name].shape)
    return np.concatenate([p[name] for name in PARAMS], 1)


def small_matrices(i):
    g2 = i["rw_g2"]
    g2b = np.concatenate([g2[P:], np.zeros((2 * P - g2.shape[0], HY), g2.dtype)])
    lora = np.concatenate([i["rw_w2"].reshape(P, HY), i["rw_a2"].reshape(P, HY), g2[:P], g2b], 1)

    def pad(m):
        return np.concatenate([m, np.zeros((P - m.shape[0], m.shape[1]), m.dtype)])

    w3 = np.concatenate([i["hy_ffn_w3"], i["hy_ffn_b3"][None]])
    return lora, np.concatenate([pad(i["hy_ffn_w1"]), pad(i["hy_ffn_w2"]), pad(w3)], 1)


def kernel(**inputs):
    import concourse.bacc as _bacc
    from concourse.bass_utils import run_bass_kernel_spmd as _run

    i = {k: np.asarray(v) for k, v in inputs.items()}
    lora, filt = small_matrices(i)
    arrays = {
        "weights": weight_stream(i), "params": parameters(i), "tables": tables(),
        "x_t": i["x"][0].T.reshape(KD, P, T).transpose(1, 0, 2).reshape(P, KD * T),
        "mem_t": i["mem_2"][0].T.reshape(KD, P, T).transpose(1, 0, 2).reshape(P, KD * T),
        "lora": lora, "filt": filt, "decay": i["hy_decay"].reshape(4 * HY),
    }
    arrays = {k: np.ascontiguousarray(v) for k, v in arrays.items()}
    nc = _bacc.Bacc("TRN2", target_bir_lowering=False, num_devices=1)
    args = [nc.dram_tensor(k, a.shape, F32, kind="ExternalInput").ap() for k, a in arrays.items()]
    out = nc.dram_tensor("out_t", (P, KD * T), F32, kind="ExternalOutput").ap()
    build_program(nc, *args, out)
    got = _run(nc, [arrays], core_ids=[0]).results[0]["out_t"]
    return got.reshape(P, KD, T).transpose(2, 1, 0).reshape(1, T, D)
```
